# Optimizing a Trainium2 kernel written in Bass

```python
import math
import jax, jax.numpy as jnp
from jax import lax
import numpy as np

D_MODEL = 2048
BATCH = 1
SEQ = 256
DEPTH = 1

HEAD_DIM = 64
N_HEADS_TOTAL = D_MODEL // HEAD_DIM
N_HEADS_A = N_HEADS_TOTAL // 4
N_KV_A = N_HEADS_A // 4
N_HEADS_B = N_HEADS_TOTAL // 4
N_HEADS_C = N_HEADS_TOTAL // 2
BLOCK = 128
WINDOW_A = 128
DILATED_PAIRS = ((128, 1), (512, 4), (2048, 16))
N_BUCKETS = 32
T5_MAX_DIST = 2048
D_FF = 256 * (-(-(8 * D_MODEL // 3) // 256))
CONV_WIDTH = 3
EPS = 1e-6
NEG_INF = -1e30

A_Q = N_HEADS_A * HEAD_DIM
A_KV = N_KV_A * HEAD_DIM
B_W = N_HEADS_B * HEAD_DIM
C_W = N_HEADS_C * HEAD_DIM
IN_WIDTH = A_Q + 2 * A_KV + 3 * B_W + 3 * C_W
MIX_WIDTH = A_Q + B_W + C_W


def rmsnorm(x, g):
    xf = x.astype(jnp.float32)
    y = xf * lax.rsqrt(jnp.mean(xf * xf, axis=-1, keepdims=True) + EPS)
    return (y * g.astype(jnp.float32)).astype(x.dtype)

def t5_bucket(dist):
    max_exact = N_BUCKETS // 2
    d = jnp.maximum(dist, 0)
    large = max_exact + (jnp.log(jnp.maximum(d, 1).astype(jnp.float32) / max_exact)
                         / math.log(T5_MAX_DIST / max_exact) * (N_BUCKETS - max_exact)).astype(jnp.int32)
    large = jnp.minimum(large, N_BUCKETS - 1)
    return jnp.where(d < max_exact, d, large)

def block_rel_bias(table, dil):
    rel = jnp.arange(BLOCK)[:, None] + BLOCK - jnp.arange(2 * BLOCK)[None, :]
    buckets = t5_bucket(rel * dil)
    return jnp.transpose(table[buckets], (2, 0, 1)).astype(jnp.float32)

def banded_attention(q, k, v, bias, max_dist, sinks=None):
    n, length, hq, hd = q.shape
    hk = k.shape[2]
    grp = hq // hk
    lp = -(-length // BLOCK) * BLOCK
    if lp != length:
        padw = ((0, 0), (0, lp - length), (0, 0), (0, 0))
        q, k, v = jnp.pad(q, padw), jnp.pad(k, padw), jnp.pad(v, padw)
    nb = lp // BLOCK
    qb = q.reshape(n, nb, BLOCK, hk, grp, hd).astype(jnp.float32)
    kb = k.reshape(n, nb, BLOCK, hk, hd).astype(jnp.float32)
    vb = v.reshape(n, nb, BLOCK, hk, hd).astype(jnp.float32)
    prev = ((0, 0), (1, 0), (0, 0), (0, 0), (0, 0))
    kk = jnp.concatenate([jnp.pad(kb[:, :-1], prev), kb], axis=2)
    vv = jnp.concatenate([jnp.pad(vb[:, :-1], prev), vb], axis=2)
    logits = (jnp.einsum('nbqhgd,nbkhd->nbhgqk', qb, kk) * (hd ** -0.5)
              + bias.reshape(hk, grp, BLOCK, 2 * BLOCK))
    rel = jnp.arange(BLOCK)[:, None] + BLOCK - jnp.arange(2 * BLOCK)[None, :]
    key_abs = (jnp.arange(nb)[:, None] - 1) * BLOCK + jnp.arange(2 * BLOCK)[None, :]
    mask = ((rel >= 0) & (rel <= max_dist))[None] & (key_abs >= 0)[:, None, :]
    logits = jnp.where(mask[None, :, None, None], logits, NEG_INF)
    m = jnp.max(logits, axis=-1, keepdims=True)
    if sinks is not None:
        s = sinks.astype(jnp.float32).reshape(hk, grp, 1, 1)
        m = jnp.maximum(m, s)
    p = jnp.exp(logits - m)
    denom = jnp.sum(p, axis=-1, keepdims=True)
    if sinks is not None:
        denom = denom + jnp.exp(s - m)
    out = jnp.einsum('nbhgqk,nbkhd->nbhgqd', p / denom, vv)
    out = jnp.transpose(out, (0, 1, 4, 2, 3, 5)).reshape(n, lp, hq, hd)[:, :length]
    lse = jnp.transpose((m + jnp.log(denom))[..., 0], (0, 1, 4, 2, 3)).reshape(n, lp, hq)[:, :length]
    return out, lse

def stick_breaking_attention(q, k, v):
    b_, s_, h, hd = q.shape
    nb = s_ // BLOCK
    qb = jnp.transpose(q.reshape(b_, nb, BLOCK, h, hd), (1, 0, 2, 3, 4))
    kf = k.astype(jnp.float32)
    vf = v.astype(jnp.float32)
    s_pos = jnp.arange(s_)

    def one_block(args):
        qblk, blk = args
        z = jnp.einsum('bqhd,bkhd->bhqk', qblk.astype(jnp.float32), kf) * (hd ** -0.5)
        t_pos = blk * BLOCK + jnp.arange(BLOCK)
        causal = s_pos[None, :] < t_pos[:, None]
        log_rem = jnp.where(causal, jax.nn.log_sigmoid(-z), 0.0)
        suffix = lax.cumsum(log_rem, axis=3, reverse=True) - log_rem
        a = jnp.where(causal, jnp.exp(jax.nn.log_sigmoid(z) + suffix), 0.0)
        return jnp.einsum('bhqk,bkhd->bqhd', a, vf)

    out = lax.map(one_block, (qb, jnp.arange(nb)))
    return jnp.transpose(out, (1, 0, 2, 3, 4)).reshape(b_, s_, h, hd)

def dilated_attention(q, k, v, table_c):
    b_, s_, h, hd = q.shape
    outs, lses = [], []
    for window, dil in DILATED_PAIRS:
        def to_sub(t):
            return jnp.transpose(t.reshape(b_, s_ // dil, dil, h, hd), (0, 2, 1, 3, 4)).reshape(b_ * dil, s_ // dil, h, hd)
        o, lse = banded_attention(to_sub(q), to_sub(k), to_sub(v), block_rel_bias(table_c, dil), window // dil)
        outs.append(jnp.transpose(o.reshape(b_, dil, s_ // dil, h, hd), (0, 2, 1, 3, 4)).reshape(b_, s_, h, hd))
        lses.append(jnp.transpose(lse.reshape(b_, dil, s_ // dil, h), (0, 2, 1, 3)).reshape(b_, s_, h))
    w = jax.nn.softmax(jnp.stack(lses, axis=0), axis=0)
    return jnp.sum(w[..., None] * jnp.stack(outs, axis=0), axis=0)

def causal_dwconv(u, w, b):
    up = jnp.pad(u, ((0, 0), (CONV_WIDTH - 1, 0), (0, 0)))
    s_ = u.shape[1]
    acc = b
    for i in range(CONV_WIDTH):
        acc = acc + w[i] * up[:, i:i + s_]
    return acc

def first_inputs(seed: int = 0) -> dict:
    key = jax.random.key(seed)
    ks = jax.random.split(key, 20)
    f32 = jnp.float32

    def nrm(k, shape, scale):
        return jax.random.normal(k, shape, f32) * scale

    return {
        "x": nrm(ks[0], (BATCH, SEQ, D_MODEL), 1.0),
        "attn_norm": 1.0 + nrm(ks[1], (DEPTH, D_MODEL), 0.02),
        "w_in": nrm(ks[2], (DEPTH, D_MODEL, IN_WIDTH), D_MODEL ** -0.5),
        "a_q_gain": 1.0 + nrm(ks[3], (DEPTH, HEAD_DIM), 0.02),
        "a_k_gain": 1.0 + nrm(ks[4], (DEPTH, HEAD_DIM), 0.02),
        "a_sinks": nrm(ks[5], (DEPTH, N_HEADS_A), 0.5),
        "c_q_gain": 1.0 + nrm(ks[6], (DEPTH, HEAD_DIM), 0.02),
        "c_k_gain": 1.0 + nrm(ks[7], (DEPTH, HEAD_DIM), 0.02),
        "rel_bias_table": nrm(ks[8], (N_BUCKETS, N_HEADS_A + N_HEADS_C), 0.5),
        "mix_out_gain": 1.0 + nrm(ks[9], (DEPTH, MIX_WIDTH), 0.02),
        "w_out": nrm(ks[10], (DEPTH, MIX_WIDTH, D_MODEL), MIX_WIDTH ** -0.5),
        "ffn_norm": 1.0 + nrm(ks[11], (DEPTH, D_MODEL), 0.02),
        "w_up": nrm(ks[12], (DEPTH, D_MODEL, 2 * D_FF), D_MODEL ** -0.5),
        "conv_w": nrm(ks[13], (DEPTH, CONV_WIDTH, 2 * D_FF), CONV_WIDTH ** -0.5),
        "conv_b": nrm(ks[14], (DEPTH, 2 * D_FF), 0.02),
        "w_down": nrm(ks[15], (DEPTH, D_FF, D_MODEL), D_FF ** -0.5),
    }

def first_block(x, attn_norm, w_in, a_q_gain, a_k_gain, a_sinks, c_q_gain, c_k_gain, rel_bias_table,
              mix_out_gain, w_out, ffn_norm, w_up, conv_w, conv_b, w_down):
    b_, s_, _ = x.shape
    sizes = [A_Q, A_KV, A_KV, B_W, B_W, B_W, C_W, C_W, C_W]
    offsets = [int(o) for o in np.cumsum(sizes)[:-1]]
    table_a = rel_bias_table[:, :N_HEADS_A]
    table_c = rel_bias_table[:, N_HEADS_A:]
    bias_a = block_rel_bias(table_a, 1)
    for l in range(DEPTH):
        h = rmsnorm(x, attn_norm[l])
        proj = jnp.einsum('bsd,de->bse', h, w_in[l])
        aq, ak, av, bq, bk, bv, cq, ck, cv = jnp.split(proj, offsets, axis=-1)
        heads = lambda t, n: t.reshape(b_, s_, n, HEAD_DIM)
        out_a, _ = banded_attention(rmsnorm(heads(aq, N_HEADS_A), a_q_gain[l]),
                                    rmsnorm(heads(ak, N_KV_A), a_k_gain[l]),
                                    heads(av, N_KV_A), bias_a, WINDOW_A - 1, sinks=a_sinks[l])
        out_b = stick_breaking_attention(heads(bq, N_HEADS_B), heads(bk, N_HEADS_B), heads(bv, N_HEADS_B))
        out_c = dilated_attention(rmsnorm(heads(cq, N_HEADS_C), c_q_gain[l]),
                                  rmsnorm(heads(ck, N_HEADS_C), c_k_gain[l]),
                                  heads(cv, N_HEADS_C), table_c)
        g = mix_out_gain[l]
        ya = rmsnorm(out_a.reshape(b_, s_, A_Q), g[:A_Q])
        yb = rmsnorm(out_b.reshape(b_, s_, B_W), g[A_Q:A_Q + B_W])
        yc = rmsnorm(out_c.reshape(b_, s_, C_W), g[A_Q + B_W:])
        mix = jnp.concatenate([ya, yb, yc], axis=-1).astype(x.dtype)
        x = x + jnp.einsum('bse,ed->bsd', mix, w_out[l])
        h = rmsnorm(x, ffn_norm[l])
        u = causal_dwconv(jnp.einsum('bsd,df->bsf', h, w_up[l]), conv_w[l], conv_b[l])
        gate, up = jnp.split(u, [D_FF], axis=-1)
        x = x + jnp.einsum('bsf,fd->bsd', jax.nn.silu(gate) * up, w_down[l])
    return x


D_BR = D_MODEL // 2
N_BRANCHES = 4
GMLP_CHUNK = 128
GMLP_GROUPS = 8
GMLP_GROUP_DIM = D_BR // GMLP_GROUPS
LRU_BLOCKS = 8
LRU_BLOCK_DIM = D_BR // LRU_BLOCKS
CONV_WIDTH_2 = 4
LRU_C = 8.0
NSA_HEAD_DIM = 64
NSA_HEADS = D_BR // NSA_HEAD_DIM
NSA_KV_HEADS = NSA_HEADS // 4
NSA_GROUP = NSA_HEADS // NSA_KV_HEADS
NSA_KV_W = NSA_KV_HEADS * NSA_HEAD_DIM
CMP_BLOCK = 32
CMP_STRIDE = 16
CMP_HIDDEN = 256
SLC_BLOCK = 64
SLC_TOPK = 8
WINDOW = 256
Q_BLOCK = 128
MEM_LEN = 256
MEM_HEADS = 4
MEM_HEAD_DIM = D_BR // MEM_HEADS
REL_BUCKETS = 32
REL_MAX_DIST = 1024
DN_ALPHA = (2 * DEPTH) ** 0.25
DN_BETA = (8 * DEPTH) ** -0.25
LN_EPS = 1e-5
IN_WIDTH_2 = 9 * D_BR + 6 * NSA_KV_W + 3 * NSA_HEADS + N_BRANCHES * D_MODEL


def in_split_points():
    sizes = (D_BR, D_BR, D_BR, D_BR, D_BR, D_BR,
             NSA_KV_W, NSA_KV_W, NSA_KV_W, NSA_KV_W, NSA_KV_W, NSA_KV_W,
             3 * NSA_HEADS, D_BR, D_BR, D_BR, N_BRANCHES * D_MODEL)
    return tuple(int(v) for v in np.cumsum(sizes)[:-1])

def layer_norm(x, g, b):
    xf = x.astype(jnp.float32)
    mu = jnp.mean(xf, -1, keepdims=True)
    var = jnp.mean(jnp.square(xf - mu), -1, keepdims=True)
    return ((xf - mu) * lax.rsqrt(var + LN_EPS) * g + b).astype(x.dtype)

def masked_softmax(s, mask):
    s = jnp.where(mask, s.astype(jnp.float32), -1e30)
    m = jnp.max(s, axis=-1, keepdims=True)
    p = jnp.where(mask, jnp.exp(s - m), 0.0)
    return p / jnp.maximum(jnp.sum(p, -1, keepdims=True), 1e-30)

def rel_bucket(dist):
    n = jnp.maximum(dist, 0)
    exact = REL_BUCKETS // 2
    nf = jnp.maximum(n, 1).astype(jnp.float32)
    large = exact + (jnp.log(nf / exact) / math.log(REL_MAX_DIST / exact)
                     * (REL_BUCKETS - exact)).astype(jnp.int32)
    return jnp.where(n < exact, n, jnp.minimum(large, REL_BUCKETS - 1))

def gmlp_spatial_gating(u, v, ln_g, ln_b, w_s, b_s):
    bsz, seq, _ = u.shape
    u = jax.nn.gelu(u)
    v = layer_norm(jax.nn.gelu(v), ln_g, ln_b)
    vc = v.reshape(bsz, seq // GMLP_CHUNK, GMLP_CHUNK, GMLP_GROUPS, GMLP_GROUP_DIM)
    causal = jnp.tril(jnp.ones((GMLP_CHUNK, GMLP_CHUNK), dtype=bool))
    w = jnp.where(causal, w_s, 0).astype(v.dtype)
    mixed = jnp.einsum('gts,bcsgd->bctgd', w, vc) + jnp.swapaxes(b_s, 0, 1)[:, :, None]
    return u * mixed.reshape(bsz, seq, D_BR)

def causal_depthwise_conv(x, w, b):
    out = lax.conv_general_dilated(
        x, w[:, None, :].astype(x.dtype), window_strides=(1,),
        padding=[(CONV_WIDTH_2 - 1, 0)], dimension_numbers=('NWC', 'WIO', 'NWC'),
        feature_group_count=x.shape[-1])
    return out + b

def block_diag_linear(x, w, b):
    bsz, seq, _ = x.shape
    xb = x.reshape(bsz, seq, LRU_BLOCKS, LRU_BLOCK_DIM)
    return jnp.einsum('bsnd,nde->bsne', xb, w).reshape(bsz, seq, D_BR) + b

def rg_lru(x, wa, ba, wx, bx, lam):
    f32 = jnp.float32
    r = jax.nn.sigmoid(block_diag_linear(x, wa, ba).astype(f32))
    i = jax.nn.sigmoid(block_diag_linear(x, wx, bx).astype(f32))
    log_a = -LRU_C * r * jax.nn.softplus(-lam.astype(f32))
    a = jnp.exp(log_a)
    gated = jnp.sqrt(-jnp.expm1(2.0 * log_a)) * i * x.astype(f32)

    def combine(lhs, rhs):
        a1, b1 = lhs
        a2, b2 = rhs
        return a1 * a2, a2 * b1 + b2

    _, h = lax.associative_scan(combine, (a, gated), axis=1)
    return h.astype(x.dtype)

def nsa_attention(q, k_c, v_c, k_s, v_s, k_w, v_w, gate_logits, gate_b, rel_table,
                  pe_k, pe_v, w1_k, w1_v, w2_k, w2_v):
    f32 = jnp.float32
    bsz, seq, _ = q.shape
    dk = NSA_HEAD_DIM
    pos = jnp.arange(seq)
    tab = rel_table.reshape(REL_BUCKETS, NSA_KV_HEADS, NSA_GROUP)

    def heads_kv(t):
        return t.reshape(bsz, seq, NSA_KV_HEADS, dk).transpose(0, 2, 1, 3)

    qh = q.reshape(bsz, seq, NSA_KV_HEADS, NSA_GROUP, dk).transpose(0, 2, 3, 1, 4) * (dk ** -0.5)
    k_c, v_c, k_s, v_s, k_w, v_w = (heads_kv(t) for t in (k_c, v_c, k_s, v_s, k_w, v_w))

    def compress(t, pe, w1, w2):
        t16 = t.reshape(bsz, NSA_KV_HEADS, seq // CMP_STRIDE, CMP_STRIDE, dk)
        blocks = jnp.concatenate([t16[:, :, :-1], t16[:, :, 1:]], axis=3) + pe
        flat = blocks.reshape(blocks.shape[:3] + (CMP_BLOCK * dk,))
        return jax.nn.silu(flat @ w1) @ w2

    kc = compress(k_c, pe_k, w1_k, w2_k)
    vc = compress(v_c, pe_v, w1_v, w2_v)
    n_cmp = kc.shape[2]
    c_start = jnp.arange(n_cmp) * CMP_STRIDE
    dist_c = pos[:, None] - (c_start + CMP_BLOCK - 1)[None, :]
    bias_c = jnp.moveaxis(tab[rel_bucket(dist_c)], (-2, -1), (0, 1))
    s_c = jnp.einsum('bhgsd,bhnd->bhgsn', qh, kc).astype(f32) + bias_c
    p_c = masked_softmax(s_c, dist_c >= 0)
    o_c = jnp.einsum('bhgsn,bhnd->bhgsd', p_c.astype(vc.dtype), vc)

    n_slc = seq // SLC_BLOCK
    s_start = jnp.arange(n_slc) * SLC_BLOCK
    overlap = jnp.clip(
        jnp.minimum(c_start[:, None] + CMP_BLOCK, s_start[None, :] + SLC_BLOCK)
        - jnp.maximum(c_start[:, None], s_start[None, :]), 0, None).astype(f32) / CMP_BLOCK
    imp = jnp.einsum('bhgsn,nj->bhsj', p_c, overlap)
    q_blk = pos // SLC_BLOCK
    j = jnp.arange(n_slc)
    forced = (j[None, :] == 0) | (j[None, :] == q_blk[:, None]) | (j[None, :] == q_blk[:, None] - 1)
    future = j[None, :] > q_blk[:, None]
    imp = jnp.where(future, -jnp.inf, jnp.where(forced, jnp.inf, imp))
    top_k = min(SLC_TOPK, n_slc)
    _, sel = lax.top_k(imp, top_k)

    k_sb = k_s.reshape(bsz, NSA_KV_HEADS, n_slc, SLC_BLOCK, dk)
    v_sb = v_s.reshape(bsz, NSA_KV_HEADS, n_slc, SLC_BLOCK, dk)
    k_wp = jnp.pad(k_w, ((0, 0), (0, 0), (WINDOW, 0), (0, 0)))
    v_wp = jnp.pad(v_w, ((0, 0), (0, 0), (WINDOW, 0), (0, 0)))
    n_qb = seq // Q_BLOCK
    b_ix = jnp.arange(bsz)[:, None, None, None]
    h_ix = jnp.arange(NSA_KV_HEADS)[None, :, None, None]
    tab_kv = jnp.transpose(tab, (1, 0, 2))
    offs = jnp.arange(SLC_BLOCK)
    win_offs = jnp.arange(WINDOW + Q_BLOCK)

    def block_step(args):
        qb, q_b, sel_b = args
        tq = qb * Q_BLOCK + jnp.arange(Q_BLOCK)
        ks = k_sb[b_ix, h_ix, sel_b]
        vs = v_sb[b_ix, h_ix, sel_b]
        kpos = sel_b[..., None] * SLC_BLOCK + offs
        dist = tq[:, None, None] - kpos
        bias = tab_kv[h_ix[..., None], rel_bucket(dist)]
        bias = jnp.moveaxis(bias, -1, 2).reshape(bsz, NSA_KV_HEADS, NSA_GROUP, Q_BLOCK, top_k * SLC_BLOCK)
        s = jnp.einsum('bhgqd,bhqnkd->bhgqnk', q_b, ks).astype(f32).reshape(
            bsz, NSA_KV_HEADS, NSA_GROUP, Q_BLOCK, top_k * SLC_BLOCK) + bias
        mask = (dist >= 0).reshape(bsz, NSA_KV_HEADS, 1, Q_BLOCK, top_k * SLC_BLOCK)
        p = masked_softmax(s, mask).reshape(bsz, NSA_KV_HEADS, NSA_GROUP, Q_BLOCK, top_k, SLC_BLOCK)
        o_s = jnp.einsum('bhgqnk,bhqnkd->bhgqd', p.astype(vs.dtype), vs)

        kw = lax.dynamic_slice_in_dim(k_wp, qb * Q_BLOCK, WINDOW + Q_BLOCK, axis=2)
        vw = lax.dynamic_slice_in_dim(v_wp, qb * Q_BLOCK, WINDOW + Q_BLOCK, axis=2)
        kpos_w = qb * Q_BLOCK - WINDOW + win_offs
        dist_w = tq[:, None] - kpos_w[None, :]
        mask_w = (dist_w >= 0) & (dist_w < WINDOW) & (kpos_w[None, :] >= 0)
        bias_w = jnp.moveaxis(tab[rel_bucket(dist_w)], (-2, -1), (0, 1))
        s_w = jnp.einsum('bhgqd,bhkd->bhgqk', q_b, kw).astype(f32) + bias_w
        p_w = masked_softmax(s_w, mask_w)
        o_w = jnp.einsum('bhgqk,bhkd->bhgqd', p_w.astype(vw.dtype), vw)
        return o_s, o_w

    q_blocks = jnp.moveaxis(qh.reshape(bsz, NSA_KV_HEADS, NSA_GROUP, n_qb, Q_BLOCK, dk), 3, 0)
    sel_blocks = jnp.moveaxis(sel.reshape(bsz, NSA_KV_HEADS, n_qb, Q_BLOCK, top_k), 2, 0)
    o_s, o_w = lax.map(block_step, (jnp.arange(n_qb), q_blocks, sel_blocks))
    o_s = jnp.moveaxis(o_s, 0, 3).reshape(bsz, NSA_KV_HEADS, NSA_GROUP, seq, dk)
    o_w = jnp.moveaxis(o_w, 0, 3).reshape(bsz, NSA_KV_HEADS, NSA_GROUP, seq, dk)

    g = jax.nn.sigmoid(gate_logits.astype(f32) + gate_b)
    g = g.reshape(bsz, seq, 3, NSA_KV_HEADS, NSA_GROUP).transpose(2, 0, 3, 4, 1)[..., None]
    o = g[0] * o_c + g[1] * o_s + g[2] * o_w
    return o.transpose(0, 3, 1, 2, 4).reshape(bsz, seq, D_BR).astype(q.dtype)

def memory_attention(q, mem, w_kv):
    bsz, seq, _ = q.shape
    k, v = jnp.split(mem @ w_kv, 2, axis=-1)
    k = k.reshape(bsz, -1, MEM_HEADS, MEM_HEAD_DIM)
    v = v.reshape(bsz, -1, MEM_HEADS, MEM_HEAD_DIM)
    qh = q.reshape(bsz, seq, MEM_HEADS, MEM_HEAD_DIM) * (MEM_HEAD_DIM ** -0.5)
    p = jax.nn.softmax(jnp.einsum('bshd,bmhd->bhsm', qh, k).astype(jnp.float32), axis=-1)
    return jnp.einsum('bhsm,bmhd->bshd', p.astype(v.dtype), v).reshape(bsz, seq, D_BR)

def second_inputs(seed: int = 0) -> dict:
    key = jax.random.key(seed)
    ks = jax.random.split(key, 32)
    f32 = jnp.float32
    dk = NSA_HEAD_DIM

    def nrm(k, shape, scale):
        return jax.random.normal(k, shape, f32) * scale

    a_pow = jax.random.uniform(ks[14], (DEPTH, D_BR), f32, 0.9, 0.999)
    a_base = a_pow ** (1.0 / LRU_C)
    lru_lambda = jnp.log(a_base) - jnp.log1p(-a_base)
    return {
        "x": nrm(ks[0], (BATCH, SEQ, D_MODEL), 1.0),
        "mem": nrm(ks[1], (BATCH, MEM_LEN, D_MODEL), 1.0),
        "rel_bias": nrm(ks[2], (REL_BUCKETS, NSA_HEADS), 0.5),
        "w_in": nrm(ks[3], (DEPTH, D_MODEL, IN_WIDTH_2), D_MODEL ** -0.5),
        "sgu_ln_g": 1.0 + nrm(ks[4], (DEPTH, D_BR), 0.01),
        "sgu_ln_b": nrm(ks[5], (DEPTH, D_BR), 0.01),
        "sgu_w": nrm(ks[6], (DEPTH, GMLP_GROUPS, GMLP_CHUNK, GMLP_CHUNK), GMLP_CHUNK ** -0.5),
        "sgu_b": 1.0 + nrm(ks[7], (DEPTH, GMLP_GROUPS, GMLP_CHUNK), 0.01),
        "conv_w": nrm(ks[8], (DEPTH, CONV_WIDTH_2, D_BR), CONV_WIDTH_2 ** -0.5),
        "conv_b": nrm(ks[9], (DEPTH, D_BR), 0.01),
        "lru_wa": nrm(ks[10], (DEPTH, LRU_BLOCKS, LRU_BLOCK_DIM, LRU_BLOCK_DIM), LRU_BLOCK_DIM ** -0.5),
        "lru_ba": nrm(ks[11], (DEPTH, D_BR), 0.01),
        "lru_wx": nrm(ks[12], (DEPTH, LRU_BLOCKS, LRU_BLOCK_DIM, LRU_BLOCK_DIM), LRU_BLOCK_DIM ** -0.5),
        "lru_bx": nrm(ks[13], (DEPTH, D_BR), 0.01),
        "lru_lambda": lru_lambda,
        "cmp_pe_k": nrm(ks[15], (DEPTH, CMP_BLOCK, dk), 0.1),
        "cmp_pe_v": nrm(ks[16], (DEPTH, CMP_BLOCK, dk), 0.1),
        "cmp_w1_k": nrm(ks[17], (DEPTH, CMP_BLOCK * dk, CMP_HIDDEN), (CMP_BLOCK * dk) ** -0.5),
        "cmp_w1_v": nrm(ks[18], (DEPTH, CMP_BLOCK * dk, CMP_HIDDEN), (CMP_BLOCK * dk) ** -0.5),
        "cmp_w2_k": nrm(ks[19], (DEPTH, CMP_HIDDEN, dk), CMP_HIDDEN ** -0.5),
        "cmp_w2_v": nrm(ks[20], (DEPTH, CMP_HIDDEN, dk), CMP_HIDDEN ** -0.5),
        "nsa_gate_b": nrm(ks[21], (DEPTH, 3 * NSA_HEADS), 0.01),
        "w_mem_kv": nrm(ks[22], (DEPTH, D_MODEL, 2 * D_BR), D_MODEL ** -0.5),
        "w_branch": nrm(ks[23], (DEPTH, N_BRANCHES, D_BR, D_MODEL), DN_BETA * D_BR ** -0.5),
        "w_out": nrm(ks[24], (DEPTH, D_MODEL, D_MODEL), DN_BETA * D_MODEL ** -0.5),
        "ln_g": 1.0 + nrm(ks[25], (DEPTH, D_MODEL), 0.01),
        "ln_b": nrm(ks[26], (DEPTH, D_MODEL), 0.01),
    }

def second_block(x, mem, rel_bias, w_in, sgu_ln_g, sgu_ln_b, sgu_w, sgu_b, conv_w, conv_b,
              lru_wa, lru_ba, lru_wx, lru_bx, lru_lambda, cmp_pe_k, cmp_pe_v, cmp_w1_k, cmp_w1_v,
              cmp_w2_k, cmp_w2_v, nsa_gate_b, w_mem_kv, w_branch, w_out, ln_g, ln_b):
    bsz, seq, _ = x.shape
    split_points = in_split_points()
    for l in range(DEPTH):
        h = x @ w_in[l]
        (u_a, v_a, g_a, x_b, g_b, q_c, kc_c, vc_c, ks_c, vs_c, kw_c, vw_c, gl_c, g_c,
         q_m, g_m, g_merge) = jnp.split(h, split_points, axis=-1)

        o_a = gmlp_spatial_gating(u_a, v_a, sgu_ln_g[l], sgu_ln_b[l], sgu_w[l], sgu_b[l]) * jax.nn.silu(g_a)
        x_conv = causal_depthwise_conv(x_b, conv_w[l], conv_b[l])
        o_b = rg_lru(x_conv, lru_wa[l], lru_ba[l], lru_wx[l], lru_bx[l], lru_lambda[l]) * jax.nn.silu(g_b)
        o_c = nsa_attention(q_c, kc_c, vc_c, ks_c, vs_c, kw_c, vw_c, gl_c, nsa_gate_b[l], rel_bias,
                            cmp_pe_k[l], cmp_pe_v[l], cmp_w1_k[l], cmp_w1_v[l],
                            cmp_w2_k[l], cmp_w2_v[l]) * jax.nn.silu(g_c)
        o_m = memory_attention(q_m, mem, w_mem_kv[l]) * jax.nn.silu(g_m)

        gates = jax.nn.sigmoid(g_merge.reshape(bsz, seq, N_BRANCHES, D_MODEL))
        merged = gates[:, :, 0] * (o_a @ w_branch[l, 0])
        merged = merged + gates[:, :, 1] * (o_b @ w_branch[l, 1])
        merged = merged + gates[:, :, 2] * (o_c @ w_branch[l, 2])
        merged = merged + gates[:, :, 3] * (o_m @ w_branch[l, 3])
        y = merged @ w_out[l]
        x = layer_norm(DN_ALPHA * x + y, ln_g[l], ln_b[l])
    return x


_first_inputs = second_inputs


def second_inputs(seed=0):
    import zlib

    import numpy as np

    out = dict(_first_inputs(seed))
    spreads = {}
    factors = {'mem': 5.908,
     'rel_bias': 7.199,
     'sgu_ln_g': 64.0,
     'sgu_ln_b': 64.0,
     'sgu_b': 64.0,
     'conv_b': 64.0,
     'lru_wa': 33.232,
     'lru_ba': 64.0,
     'lru_bx': 64.0,
     'lru_lambda': 31.016,
     'cmp_pe_k': 8.0,
     'cmp_pe_v': 8.0,
     'cmp_w1_k': 8.0,
     'cmp_w1_v': 3.824,
     'cmp_w2_k': 8.0,
     'cmp_w2_v': 3.161,
     'nsa_gate_b': 64.0,
     'w_mem_kv': 5.741,
     'ln_g': 29.705,
     'ln_b': 31.551,
     'conv_w': 8.0,
     'lru_wx': 8.0}
    for name, (base, spread) in spreads.items():
        noise = np.random.default_rng([zlib.crc32(name.encode()), seed]).standard_normal(out[name].shape)
        drawn = base * np.exp(spread * noise) if base else spread * noise
        out[name] = __import__('jax').numpy.asarray(drawn.astype(out[name].dtype))
    for name, factor in factors.items():
        out[name] = (out[name] * factor).astype(out[name].dtype)
    return out


_narrow_inputs = second_inputs


def second_inputs(seed=0):

    out = dict(_narrow_inputs(seed))
    wider = {'rel_bias': 4.36,
     'sgu_ln_g': 12.0,
     'sgu_ln_b': 12.0,
     'sgu_b': 9.93,
     'nsa_gate_b': 3.15,
     'ln_g': 6.15,
     'ln_b': 6.14}
    for name, times in wider.items():
        mean = out[name].mean()
        out[name] = (mean + times * (out[name] - mean)).astype(out[name].dtype)
    return out


def setup_inputs(seed=0):
    out = dict(first_inputs(seed))
    for name, value in second_inputs(seed + 1).items():
        if name != "x":
            out[name + "_2"] = value
    return out


def reference(
    x, attn_norm, w_in, a_q_gain, a_k_gain, a_sinks, c_q_gain, c_k_gain, rel_bias_table,
    mix_out_gain, w_out, ffn_norm, w_up, conv_w, conv_b, w_down, mem_2, rel_bias_2, w_in_2,
    sgu_ln_g_2, sgu_ln_b_2, sgu_w_2, sgu_b_2, conv_w_2, conv_b_2, lru_wa_2, lru_ba_2, lru_wx_2,
    lru_bx_2, lru_lambda_2, cmp_pe_k_2, cmp_pe_v_2, cmp_w1_k_2, cmp_w1_v_2, cmp_w2_k_2,
    cmp_w2_v_2, nsa_gate_b_2, w_mem_kv_2, w_branch_2, w_out_2, ln_g_2, ln_b_2,
):
    x = first_block(
        x, attn_norm, w_in, a_q_gain, a_k_gain, a_sinks, c_q_gain, c_k_gain, rel_bias_table,
        mix_out_gain, w_out, ffn_norm, w_up, conv_w, conv_b, w_down,
    )
    return second_block(
        x, mem_2, rel_bias_2, w_in_2, sgu_ln_g_2, sgu_ln_b_2, sgu_w_2, sgu_b_2, conv_w_2,
        conv_b_2, lru_wa_2, lru_ba_2, lru_wx_2, lru_bx_2, lru_lambda_2, cmp_pe_k_2, cmp_pe_v_2,
        cmp_w1_k_2, cmp_w1_v_2, cmp_w2_k_2, cmp_w2_v_2, nsa_gate_b_2, w_mem_kv_2, w_branch_2,
        w_out_2, ln_g_2, ln_b_2,
    )


_drawn_inputs = setup_inputs


def setup_inputs(seed=0):
    import zlib

    import numpy as np

    out = dict(_drawn_inputs(seed))
    spreads = {}
    factors = {'a_sinks': 3.246}
    for name, (base, spread) in spreads.items():
        noise = np.random.default_rng([zlib.crc32(name.encode()), seed]).standard_normal(out[name].shape)
        drawn = base * np.exp(spread * noise) if base else spread * noise
        out[name] = __import__('jax').numpy.asarray(drawn.astype(out[name].dtype))
    for name, factor in factors.items():
        out[name] = (out[name] * factor).astype(out[name].dtype)
    return out
```

```python
import math
from contextlib import ExitStack

import numpy as np
import concourse.bass as bass
from concourse import mybir

F32 = mybir.dt.float32
F32R = mybir.dt.float32r
ACT = mybir.ActivationFunctionType
ALU = mybir.AluOpType
AX = mybir.AxisListType.X

P = 128
SEQ = 256
DM = 2048
NT = DM // P
HD = 64
NF = 44
UK, UN = 2, 512
RING = 4
LEAD = 3
NEG = -1.0e30
TABW = 512
EPS, LN_EPS = 1e-6, 1e-5

STREAM = {}
_at = 0
for _name, _chunks, _per in (("mem", 4, 8), ("proj", 11, 8), ("wout", 4, 8), ("up", 22, 8),
                             ("down", 22, 4), ("p_a", 6, 8), ("m_a", 4, 12), ("p_b", 4, 8),
                             ("m_b", 4, 12), ("p_m", 4, 8), ("m_m", 4, 12), ("p_c", 7, 8),
                             ("m_c", 4, 12), ("out2", 4, 8)):
    STREAM[_name] = _at
    _at += _chunks * _per
UNITS = _at

VEC = {}
_at = 0
for _name, _n in (("attn_norm", 16), ("ffn_norm", 16), ("mix_gain", 16), ("aq", 1), ("ak", 1), ("cq", 1),
                  ("ck", 1), ("conv_w", 3 * 88), ("conv_b", 88), ("conv2_w", 32), ("conv2_b", 8),
                  ("lru_ba", 8), ("lru_bx", 8), ("lru_lam", 8), ("ln_g", 16), ("ln_b", 16),
                  ("cmp_pe_k", 16), ("cmp_pe_v", 16)):
    VEC[_name] = (_at, _n)
    _at += _n
NVEC = _at


class Signal:

    def __init__(self, sem, base):
        self.sem, self.base = sem, base

    def __call__(self, n):
        return self.sem, n + self.base




def two_blocks(nc, W, xT, memT, vecs, squares, masks, cmask, onehots, tabs, sinks, ln_rows, sgu_wT, sgu_b,
               lru_w, gl_w, gl_b, cmp_w1, cmp_w2k, cmp_w2v, out):
    ctx = ExitStack()
    with ctx:
        def sb(name, shape, dt=F32):
            return ctx.enter_context(nc.sbuf_tensor(name, shape, dt))

        def sem(name):
            return ctx.enter_context(nc.semaphore(name))

        raw = sb("raw", [P, RING, UK * UN])
        w_hi = sb("w_hi", [P, RING, UK * UN], F32R)
        w_lo = sb("w_lo", [P, RING, UK * UN], F32R)
        x = sb("x", [P, NT, SEQ])
        h_hi = sb("h_hi", [P, NT, SEQ], F32R)
        h_lo = sb("h_lo", [P, NT, SEQ], F32R)
        o_hi = sb("o_hi", [P, 8, SEQ], F32R)
        o_lo = sb("o_lo", [P, 8, SEQ], F32R)
        kmT = sb("kmT", [P, 8, SEQ])
        vm = sb("vm", [P, 2, 1024])
        vec = sb("vec", [P, NVEC])
        sq_c = sb("sq_c", [P, 5, P])
        ones, blocks, ident, tri, causal = (sq_c[:, n, :] for n in range(5))
        small = sb("small", [P, 160])
        AW = 18950
        arena = sb("arena", [P, AW])
        bank = [ctx.enter_context(nc.psum_tensor(f"bank{n}", [P, 512], F32)) for n in range(8)]

        def at(off, *shape, parts=(0, P)):
            n = int(np.prod(shape))
            assert off + n <= AW, (off, shape)
            v = arena[parts[0]:parts[1], off:off + n]
            if len(shape) == 2:
                v = v.rearrange("p (a b) -> p a b", a=shape[0])
            elif len(shape) == 3:
                v = v.rearrange("p (a b c) -> p a b c", a=shape[0], b=shape[1])
            return v

        def vcol(name, n=0):
            o, cnt = VEC[name]
            assert n < cnt
            return vec[:, o + n:o + n + 1]

        row_dram = nc.dram_tensor("row_dram", (40, TABW), F32, kind="Internal").ap()
        bias_dram = nc.dram_tensor("bias_dram", (40, P, TABW), F32, kind="Internal").ap()

        raw_ready = [sem(f"raw_ready{n}") for n in range(RING)]
        hi_ready, lo_ready, unit_done = sem("hi_ready"), sem("lo_ready"), sem("unit_done")
        stage_done = sem("stage_done")

        def split_hi(act, u, j):
            s = (j + LEAD) % RING
            v = u + LEAD
            act.wait_ge(raw_ready[s], (v - s) * (16 // RING) + 16)
            if not (isinstance(v, int) and v < RING):
                act.wait_ge(unit_done, v - RING + 1)
            nc.scalar.activation(w_hi[:, s, :], raw[:, s, :], ACT.Copy).then_inc(hi_ready, 1)

        def split_lo(dve, u, j):
            s = (j + LEAD) % RING
            v = u + LEAD
            dve.wait_ge(hi_ready, v + 1)
            if not (isinstance(v, int) and v < RING):
                dve.wait_ge(unit_done, v - RING + 1)
            nc.vector.tensor_tensor(w_lo[:, s, :], raw[:, s, :], w_hi[:, s, :].bitcast(F32),
                                    ALU.subtract).then_inc(lo_ready, 1)

        def unit_features(pe, u, j, hi, lo, kt, banks, first, last, tiles=4):
            s = j % RING
            pe.wait_ge(lo_ready, u + 1)
            for k in range(UK):
                for f in range(tiles):
                    o = banks[f // 2][:, (f % 2) * SEQ:(f % 2 + 1) * SEQ]
                    cols = slice(k * UN + f * P, k * UN + (f + 1) * P)
                    for n, (w, m) in enumerate(((w_hi, hi), (w_hi, lo), (w_lo, hi))):
                        mm = nc.tensor.matmul(o, w[:, s, cols], m[:, kt + k, :],
                                              start=first and k == 0 and n == 0 and f % 2 == 0,
                                              stop=last and k == UK - 1 and n == 2, skip_group_check=True)
            return mm

        def unit_tokens(pe, u, j, kt, banks, first, last, c0=0, cols=UN, wait=True):
            s = j % RING
            if wait:
                pe.wait_ge(lo_ready, u + 1)
            for k in range(UK):
                for m in range(2):
                    for n, (w, a) in enumerate(((w_hi, h_hi), (w_lo, h_hi), (w_hi, h_lo))):
                        mm = nc.tensor.matmul(banks[m][:, 0:cols], a[:, kt + k, m * P:(m + 1) * P],
                                              w[:, s, k * UN + c0:k * UN + c0 + cols],
                                              start=first and k == 0 and n == 0,
                                              stop=last and k == UK - 1 and n == 2, skip_group_check=True)
            return mm

        def chunk_pe(pe, ev, u, c, q, kind, first_two):
            if not first_two:
                pe.wait_ge(*ev[0](c - 1))
                pe.wait_ge(*ev[1](c - 1))
            banks = bank[2 * q:2 * q + 2]
            for j in range(8):
                if kind == "F":
                    mm = unit_features(pe, u + j, j, h_hi, h_lo, 2 * j, banks, j == 0, j == 7)
                elif kind == "T":
                    mm = unit_tokens(pe, u + j, j, 2 * j, banks, j == 0, j == 7)
                elif kind == "M":
                    unit_features(pe, u + j, j, h_hi, h_lo, 2 * j, banks, j == 0, j == 7, tiles=1)
                    mm = unit_tokens(pe, u + j, j, 2 * j, (banks[1], bank[4]), j == 0, j == 7, P, P, wait=False)
                mm.then_inc(unit_done, 1)

        def chunk_split(eng, split, u):
            for j in range(8):
                split(eng, u + j, j)

        def F_act(act, ev, u, q, dst):
            act.wait_ge(unit_done, u + 8)
            nc.scalar.activation(dst, bank[2 * q][:, :].rearrange("p (a b) -> p a b", a=2),
                                 ACT.Copy).then_inc(ev[0].sem, 1)

        def F_dve(dve, ev, u, q, dst):
            dve.wait_ge(unit_done, u + 8)
            nc.vector.tensor_copy(dst, bank[2 * q + 1][:, :].rearrange("p (a b) -> p a b", a=2))\
                .then_inc(ev[1].sem, 1)

        def features_pe(pe, ev, u0, chunks):
            chunk_pe(pe, ev, u0, 0, 0, "F", True)
            chunk_pe(pe, ev, u0 + 8, 1, 1, "F", True)
            if chunks >= 4:
                with pe.Fori(1, chunks // 2) as i:
                    for q in range(2):
                        chunk_pe(pe, ev, i * 16 + (u0 + 8 * q), i * 2 + q, q, "F", False)
            if chunks % 2:
                chunk_pe(pe, ev, u0 + 8 * (chunks - 1), chunks - 1, 0, "F", False)

        def features_act(act, ev, u0, chunks, dst, t0=0):
            for q in range(2):
                chunk_split(act, split_hi, u0 + 8 * q)
                F_act(act, ev, u0 + 8 * q, q, dst[:, t0 + 4 * q:t0 + 4 * q + 2, :])
            if chunks >= 4:
                with act.Fori(1, chunks // 2) as i:
                    for q in range(2):
                        chunk_split(act, split_hi, i * 16 + (u0 + 8 * q))
                        F_act(act, ev, i * 16 + (u0 + 8 * q), q, dst[:, bass.ds(i * 8 + (t0 + 4 * q), 2), :])
            if chunks % 2:
                u, t = u0 + 8 * (chunks - 1), t0 + 4 * (chunks - 1)
                chunk_split(act, split_hi, u)
                F_act(act, ev, u, 0, dst[:, t:t + 2, :])

        def features_dve(dve, ev, u0, chunks, dst, t0=0):
            for q in range(2):
                chunk_split(dve, split_lo, u0 + 8 * q)
                F_dve(dve, ev, u0 + 8 * q, q, dst[:, t0 + 4 * q + 2:t0 + 4 * q + 4, :])
            if chunks >= 4:
                with dve.Fori(1, chunks // 2) as i:
                    for q in range(2):
                        chunk_split(dve, split_lo, i * 16 + (u0 + 8 * q))
                        F_dve(dve, ev, i * 16 + (u0 + 8 * q), q, dst[:, bass.ds(i * 8 + (t0 + 4 * q + 2), 2), :])
            if chunks % 2:
                u, t = u0 + 8 * (chunks - 1), t0 + 4 * (chunks - 1) + 2
                chunk_split(dve, split_lo, u)
                F_dve(dve, ev, u, 0, dst[:, t:t + 2, :])

        def tokens_pe(pe, ev, u0, c0, chunks):
            for c in range(chunks):
                chunk_pe(pe, ev, u0 + 8 * c, c0 + c, (c0 + c) % 2, "T", c0 + c < 2)

        def tokens_act(act, ev, u0, c0, chunks, dst):
            for c in range(chunks):
                chunk_split(act, split_hi, u0 + 8 * c)
                act.wait_ge(unit_done, u0 + 8 * c + 8)
                nc.scalar.activation(dst(0, c), bank[2 * ((c0 + c) % 2)][:, :], ACT.Copy).then_inc(ev[0].sem, 1)

        def tokens_dve(dve, ev, u0, c0, chunks, dst):
            for c in range(chunks):
                chunk_split(dve, split_lo, u0 + 8 * c)
                dve.wait_ge(unit_done, u0 + 8 * c + 8)
                nc.vector.tensor_copy(dst(1, c), bank[2 * ((c0 + c) % 2) + 1][:, :]).then_inc(ev[1].sem, 1)

        pool_of_signals = {}

        def sems(stage, names):
            return {n: Signal(sem(f"{stage}_{n}"), 0) for n in names.split()}

        def shared(kind, **totals):
            got = {}
            for n, total in totals.items():
                if (kind, n) not in pool_of_signals:
                    pool_of_signals[kind, n] = [sem(f"{kind}_{n}"), 0]
                s, before = pool_of_signals[kind, n]
                got[n] = Signal(s, before)
                pool_of_signals[kind, n][1] = before + total
            return got

        def halves(chunks):
            S = shared("read", by_act=chunks, by_dve=chunks)
            return S["by_act"], S["by_dve"]

        def rms_pe(pe, S, tiles, sq, groups):
            done = 0
            for g, (a, n) in enumerate(groups):
                if g >= 2:
                    pe.wait_ge(*S["root"](g - 1))
                for t in range(a, a + n):
                    pe.wait_ge(*S["square"](done + 1))
                    mm = nc.tensor.matmul(bank[4 + g % 2][:, 0:SEQ], ones, sq[:, done % 4, :],
                                          start=t == a, stop=t == a + n - 1)
                    mm.then_inc(S["sum"].sem, 1)
                    done += 1

        def rms_act(act, S, src, sq, sd, groups):
            done = 0
            for g, (a, n) in enumerate(groups):
                for t in range(a, a + n):
                    if done >= 4:
                        act.wait_ge(*S["sum"](done - 3))
                    nc.scalar.activation(sq[:, done % 4, :], src[:, t, :], ACT.Square).then_inc(S["square"].sem, 1)
                    done += 1
                act.wait_ge(*S["sum"](done))
                nc.scalar.activation(sd[:, g, :], bank[4 + g % 2][:, 0:SEQ], ACT.Sqrt, bias=eps_col,
                                     scale=1.0 / (n * P)).then_inc(S["root"].sem, 1)

        def rms_dve(dve, S, src, sd, tmp, gain, groups, put_lo):
            done = 0
            for g, (a, n) in enumerate(groups):
                dve.wait_ge(*S["root"](g + 1))
                nc.vector.reciprocal(sd[:, g, :], sd[:, g, :]).then_inc(S["recip"].sem, 1)
                dve.wait_ge(*S["recip"](g + 1))
                for t in range(a, a + n):
                    nc.vector.scalar_tensor_tensor(tmp[:, t, :], src[:, t, :], vcol(gain, t), sd[:, g, :],
                                                   ALU.mult, ALU.mult).then_inc(S["scaled"].sem, 1)
                    done += 1
                    if done % 2 == 0 and done >= 4:
                        put_lo(done // 2 - 2)
            put_lo(done // 2 - 1)

        def to_moving_act(act, S, tmp, hi, pairs):
            for p in range(pairs):
                act.wait_ge(*S["scaled"](2 * p + 2))
                nc.scalar.activation(hi[:, 2 * p:2 * p + 2, :], tmp[:, 2 * p:2 * p + 2, :], ACT.Copy)\
                    .then_inc(S["hi"].sem, 1)

        def to_moving_dve(dve, S, tmp, hi, lo):
            def put(p):
                dve.wait_ge(*S["hi"](p + 1))
                nc.vector.tensor_tensor(lo[:, 2 * p:2 * p + 2, :], tmp[:, 2 * p:2 * p + 2, :],
                                        hi[:, 2 * p:2 * p + 2, :].bitcast(F32), ALU.subtract)\
                    .then_inc(S["lo"].sem, 1)
            return put

        eps_col, ln_eps_col = small[:, 150:151], small[:, 151:152]
        stages = []

        S0 = sems("start", "c e r_pe r_act table rows hi lo")
        stg_mem = at(0, NT, SEQ)
        oh = at(4096, 3, TABW, parts=(0, 33))
        tb = at(5632, 40, parts=(0, 33))
        rows = [at(5700 + 512 * n, TABW, parts=(0, r)) for n, r in enumerate((8, 16, 16))]
        tab_cols = ((0, 8), (8, 24), (24, 40))

        def start_load(pool):
            pool.dma_start(stg_mem, memT).then_inc(S0["c"].sem, 16)
            pool.dma_start(oh, onehots[:, 0:3, :]).then_inc(S0["c"].sem, 16)
            pool.dma_start(tb, tabs).then_inc(S0["c"].sem, 16)
            pool.dma_start(x[:, :, :], xT).then_inc(S0["c"].sem, 16)
            pool.dma_start(vec[:, :], vecs).then_inc(S0["c"].sem, 16)
            pool.dma_start(sq_c[:, :, :], squares).then_inc(S0["c"].sem, 16)
            pool.wait_ge(*S0["r_act"](3))
            for n, (a, b) in enumerate(tab_cols):
                pool.dma_start(row_dram[a:b], rows[n]).then_inc(S0["table"].sem, 16)
            pool.wait_ge(*S0["table"](48))
            for h in range(40):
                pool.dma_start(bias_dram[h], row_dram[h:h + 1].broadcast_to([P, TABW]))\
                    .then_inc(S0["rows"].sem, 16)
            pool.wait_ge(*S0["rows"](16 * 40))

        def start_pe(pe):
            pe.wait_ge(*S0["c"](96))
            for n, (a, b) in enumerate(tab_cols):
                nc.tensor.matmul(bank[4 + n][0:b - a, :], tb[:, a:b], oh[:, n, :], start=True, stop=True)\
                    .then_inc(S0["r_pe"].sem, 1)

        def start_act(act):
            act.wait_ge(*S0["c"](96))
            for n in range(4):
                nc.scalar.activation(h_hi[:, 4 * n:4 * n + 4, :], stg_mem[:, 4 * n:4 * n + 4, :], ACT.Copy)\
                    .then_inc(S0["hi"].sem, 1)
            for n, (a, b) in enumerate(tab_cols):
                act.wait_ge(*S0["r_pe"](n + 1))
                nc.scalar.activation(rows[n], bank[4 + n][0:b - a, :], ACT.Copy).then_inc(S0["r_act"].sem, 1)
            for u in range(LEAD):
                act.wait_ge(raw_ready[u], 16)
                nc.scalar.activation(w_hi[:, u, :], raw[:, u, :], ACT.Copy).then_inc(hi_ready, 1)

        def start_dve(dve):
            nc.vector.memset(eps_col, EPS).then_inc(S0["e"].sem, 1)
            nc.vector.memset(ln_eps_col, LN_EPS).then_inc(S0["e"].sem, 1)
            dve.wait_ge(*S0["c"](96))
            for n in range(4):
                dve.wait_ge(*S0["hi"](n + 1))
                nc.vector.tensor_tensor(h_lo[:, 4 * n:4 * n + 4, :], stg_mem[:, 4 * n:4 * n + 4, :],
                                        h_hi[:, 4 * n:4 * n + 4, :].bitcast(F32), ALU.subtract)\
                    .then_inc(S0["lo"].sem, 1)
            for u in range(LEAD):
                dve.wait_ge(hi_ready, u + 1)
                nc.vector.tensor_tensor(w_lo[:, u, :], raw[:, u, :], w_hi[:, u, :].bitcast(F32),
                                        ALU.subtract).then_inc(lo_ready, 1)

        stages.append(("start", start_pe, start_act, start_dve, start_load))

        ev_mem = halves(4)
        UM = STREAM["mem"]

        def mem_pe(pe):
            features_pe(pe, ev_mem, UM, 2)
            tokens_pe(pe, ev_mem, UM + 16, 2, 2)

        def mem_act(act):
            features_act(act, ev_mem, UM, 2, kmT)
            tokens_act(act, ev_mem, UM + 16, 2, 2, lambda m, c: vm[:, m, c * UN:(c + 1) * UN])

        def mem_dve(dve):
            features_dve(dve, ev_mem, UM, 2, kmT)
            tokens_dve(dve, ev_mem, UM + 16, 2, 2, lambda m, c: vm[:, m, c * UN:(c + 1) * UN])

        stages.append(("mem", mem_pe, mem_act, mem_dve, None))

        def norm_stage(name, src, gain, groups, tmp, sq, sd):
            G = len(groups)
            S = shared("norm", square=NT, sum=NT, root=G, recip=G, scaled=NT, hi=NT // 2, lo=NT // 2)

            def pe_(pe):
                rms_pe(pe, S, None, sq, groups)

            def act_(act):
                rms_act(act, S, src, sq, sd, groups)
                to_moving_act(act, S, tmp, h_hi, NT // 2)

            def dve_(dve):
                rms_dve(dve, S, src, sd, tmp, gain, groups, to_moving_dve(dve, S, tmp, h_hi, h_lo))

            stages.append((name, pe_, act_, dve_, None))

        norm_stage("norm1", x, "attn_norm", [(0, NT)], at(0, NT, SEQ), at(4096, 4, SEQ), at(5120, 3, SEQ))

        qk = at(0, 30, SEQ)
        v1 = at(7680, 2, 1664)
        oT = at(11008, NT, SEQ)
        WK = 15104
        logit = at(WK, 2, 2, SEQ)
        prob = at(WK + 1024, 2, 2, SEQ)
        probT = at(WK + 2048, 2, 2 * SEQ - P)
        bias = at(WK + 2816, 2, 2, SEQ)
        ev_proj = halves(11)
        UP = STREAM["proj"]

        def proj_pe(pe):
            features_pe(pe, ev_proj, UP, 7)
            chunk_pe(pe, ev_proj, UP + 56, 7, 1, "M", False)
            tokens_pe(pe, ev_proj, UP + 64, 8, 3)

        def proj_act(act):
            features_act(act, ev_proj, UP, 7, qk)
            chunk_split(act, split_hi, UP + 56)
            act.wait_ge(unit_done, UP + 64)
            nc.scalar.activation(qk[:, 28, :], bank[2][:, 0:SEQ], ACT.Copy).then_inc(ev_proj[0].sem, 1)
            tokens_act(act, ev_proj, UP + 64, 8, 3, lambda m, c: v1[:, m, P + c * UN:P + (c + 1) * UN])

        def proj_dve(dve):
            features_dve(dve, ev_proj, UP, 7, qk)
            chunk_split(dve, split_lo, UP + 56)
            dve.wait_ge(unit_done, UP + 64)
            nc.vector.tensor_copy(v1[:, 1, 0:P], bank[4][:, 0:P])
            nc.vector.tensor_copy(v1[:, 0, 0:P], bank[3][:, 0:P]).then_inc(ev_proj[1].sem, 1)
            tokens_dve(dve, ev_proj, UP + 64, 8, 3, lambda m, c: v1[:, m, P + c * UN:P + (c + 1) * UN])

        stages.append(("proj", proj_pe, proj_act, proj_dve, None))

        SH = sems("headnorm", "square sum root recip scaled swap sinks")
        pairs = [(0, 2, "aq"), (2, 2, "aq"), (28, 1, "ak")] + [(t, 2, "cq") for t in range(12, 20, 2)] \
            + [(t, 2, "ck") for t in range(20, 28, 2)]
        hsq, hsd = at(WK, 2, 2, SEQ), at(WK + 1024, 2, 2, SEQ)
        sink_col = small[:, 0:8]

        def head_load(pool):
            pool.dma_start(sink_col, sinks.broadcast_to([P, 8])).then_inc(SH["sinks"].sem, 16)
            pool.wait_ge(*SH["scaled"](5))
            pool.dma_start(qk[HD:P, 29, :], qk[0:HD, 28, :]).then_inc(SH["swap"].sem, 16)
            pool.dma_start(qk[0:HD, 29, :], qk[HD:P, 28, :]).then_inc(SH["swap"].sem, 16)

        def head_pe(pe):
            for n, (t, k, _) in enumerate(pairs):
                pe.wait_ge(*SH["square"](n + 1))
                if n >= 2:
                    pe.wait_ge(*SH["root"](n - 1))
                nc.tensor.matmul(bank[4 + n % 2][:, 0:k * SEQ], blocks,
                                 hsq[:, n % 2, 0:k, :].rearrange("p a b -> p (a b)"), start=True, stop=True)\
                    .then_inc(SH["sum"].sem, 1)

        def head_act(act):
            for n in range(len(pairs) + 1):
                if n < len(pairs):
                    t, k, _ = pairs[n]
                    if n >= 2:
                        act.wait_ge(*SH["sum"](n - 1))
                    nc.scalar.activation(hsq[:, n % 2, 0:k, :], qk[:, t:t + k, :], ACT.Square)\
                        .then_inc(SH["square"].sem, 1)
                if n >= 1:
                    k = pairs[n - 1][1]
                    act.wait_ge(*SH["sum"](n))
                    if n >= 3:
                        act.wait_ge(*SH["scaled"](sum(p[1] for p in pairs[:n - 2])))
                    nc.scalar.activation(hsd[:, (n - 1) % 2, 0:k, :],
                                         bank[4 + (n - 1) % 2][:, 0:k * SEQ].rearrange("p (a b) -> p a b", a=k),
                                         ACT.Sqrt, bias=eps_col, scale=1.0 / HD).then_inc(SH["root"].sem, 1)

        def head_dve(dve):
            for n, (t, k, gain) in enumerate(pairs):
                dve.wait_ge(*SH["root"](n + 1))
                nc.vector.reciprocal(hsd[:, n % 2, 0:k, :], hsd[:, n % 2, 0:k, :]).then_inc(SH["recip"].sem, 1)
                dve.wait_ge(*SH["recip"](n + 1))
                for j in range(k):
                    nc.vector.scalar_tensor_tensor(qk[:, t + j, :], qk[:, t + j, :], vcol(gain),
                                                   hsd[:, n % 2, j, :], ALU.mult, ALU.mult)\
                        .then_inc(SH["scaled"].sem, 1)

        stages.append(("headnorm", head_pe, head_act, head_dve, head_load))

        sinks_signal, extra_signal = Signal(sem("sinks_negated"), 0), Signal(sem("stage_tiles"), 0)

        def softmax_stage(name, jobs, scale, outs_ev, probT, load_extra=None):
            J = len(jobs)
            weighted_jobs = sum(j.get("weights") is not None for j in jobs)
            loads = sum(j.get("load") is not None for j in jobs)
            S = shared("softmax", score=J, logit=sum(j["reader"] == "logit" for j in jobs), peak=J, neg=J, prob=J,
                       weight=weighted_jobs, sum=sum(bool(j.get("floor")) + (j.get("sink") is not None) for j in jobs),
                       recip=J, norm=J, transposed=J, probT=J, out=J, evac=sum(j["last"] for j in jobs),
                       bias0=32 * ((loads + 1) // 2), bias1=32 * (loads // 2))
            S["sinks"] = sinks_signal
            S["extra"] = extra_signal
            nb = [0]
            for j in jobs:
                j["bias_n"] = nb[0] = nb[0] + (1 if j.get("load") is not None else 0)
            mx, ng, sm, rc = (small[:, 8 + 4 * n:12 + 4 * n].rearrange("p (a b) -> p a b", a=2) for n in range(4))
            es = small[:, 24:28].rearrange("p (a b) -> p a b", a=2)
            wsm = small[:, 28:32].rearrange("p (a b) -> p a b", a=2)

            def load(pool):
                if load_extra:
                    load_extra(pool, S)
                for n, j in enumerate(jobs):
                    if j.get("load") is None:
                        continue
                    b = (j["bias_n"] - 1) % 2
                    users = [m for m, o in enumerate(jobs) if o.get("buf") is not None
                             and o["bias_n"] == j["bias_n"] - 2]
                    if users:
                        pool.wait_ge(*S["logit"](users[-1] + 1))
                    g = bias_dram[j["load"]].rearrange("a b -> (a b)")
                    for m in range(2):
                        pool.dma_start(bias[:, b, m, :], bass.AP(
                            tensor=g.tensor, offset=g.offset + 255 - P * m, ap=[[TABW - 1, P], [1, SEQ]]))\
                            .then_inc(S[f"bias{b}"].sem, 16)

            def pe_(pe):
                def scores(n):
                    j = jobs[n]
                    w = j["width"]
                    if n >= 2:
                        pe.wait_ge(*S[j["reader"]](n - 1))
                    for m in range(2):
                        ops = j["scores"](m)
                        for i, (q, k) in enumerate(ops):
                            mm = nc.tensor.matmul(bank[4 + n % 2][:, m * SEQ:m * SEQ + w], q, k,
                                                  start=i == 0, stop=i == len(ops) - 1)
                    mm.then_inc(S["score"].sem, 1)

                scores(0)
                for n, j in enumerate(jobs):
                    if n + 1 < J:
                        scores(n + 1)
                    pe.wait_ge(*S["norm"](n + 1))
                    if n >= 1:
                        pe.wait_ge(*S["probT"](n))
                    at_ = 0
                    for kt, m in j["parts"]:
                        kw = min(P, j["width"])
                        mm = nc.tensor.transpose(bank[6][0:kw, at_ * P:(at_ + 1) * P],
                                                 prob[:, n % 2, m, kt * P:kt * P + kw], ident)
                        at_ += 1
                    mm.then_inc(S["transposed"].sem, 1)
                    pe.wait_ge(*S["probT"](n + 1))
                    if j["ev_wait"] is not None:
                        pe.wait_ge(*S["evac"](j["ev_wait"]))
                    for mm in j["pv"](n % 2):
                        pass
                    mm.then_inc(S["out"].sem, 1)

            def act_(act):
                done = 0
                for n in range(J + 1):
                    if n < J:
                        j = jobs[n]
                        w = j["width"]
                        act.wait_ge(*S["neg"](n + 1))
                        if n >= 2:
                            act.wait_ge(*S["transposed"](n - 1))
                        for m in range(2):
                            src = (logit[:, n % 2, m, 0:w] if j["reader"] == "logit"
                                   else bank[4 + n % 2][:, m * SEQ:m * SEQ + w])
                            i = nc.scalar.activation(prob[:, n % 2, m, 0:w], src, ACT.Exp, bias=ng[:, n % 2, m:m + 1],
                                                     scale=1.0 if j["reader"] == "logit" else scale,
                                                     accum_out=sm[:, n % 2, m:m + 1])
                        if j.get("sink") is not None:
                            i = nc.scalar.activation(es[:, n % 2, :], ng[:, n % 2, :], ACT.Exp,
                                                     bias=sink_col[:, j["sink"]:j["sink"] + 1])
                        i.then_inc(S["prob"].sem, 1)
                    if n >= 1:
                        j = jobs[n - 1]
                        kw, cnt = min(P, j["width"]), len(j["parts"])
                        act.wait_ge(*S["transposed"](n))
                        if n >= 3:
                            act.wait_ge(*S["out"](n - 2))
                        nc.scalar.activation(probT[0:kw, (n - 1) % 2, 0:cnt * P], bank[6][0:kw, 0:cnt * P],
                                             ACT.Copy).then_inc(S["probT"].sem, 1)

            def dve_(dve):
                def logits(n):
                    j = jobs[n]
                    w = j["width"]
                    dve.wait_ge(*S["score"](n + 1))
                    src = bank[4 + n % 2][:, :].rearrange("p (a b) -> p a b", a=2)[:, :, 0:w]
                    if j["reader"] == "logit":
                        if j["bias_n"]:
                            dve.wait_ge(*S[f"bias{(j['bias_n'] - 1) % 2}"](32 * ((j["bias_n"] + 1) // 2)))
                        if n >= 2:
                            dve.wait_ge(*S["prob"](n - 1))
                        b = bias[:, j["buf"], :, :] if j.get("buf") is not None else j["tile"]
                        nc.vector.scalar_tensor_tensor(logit[:, n % 2, :, 0:w], src, scale, b[:, :, 0:w],
                                                       ALU.mult, ALU.add).then_inc(S["logit"].sem, 1)
                        dve.wait_ge(*S["logit"](n + 1))
                        src = logit[:, n % 2, :, 0:w]
                    if n >= 2:
                        dve.wait_ge(*S["prob"](n - 1))
                    nc.vector.tensor_reduce(mx[:, n % 2, :], src, AX, ALU.max).then_inc(S["peak"].sem, 1)
                    dve.wait_ge(*S["peak"](n + 1))
                    if j.get("sink") is not None:
                        i = nc.vector.tensor_scalar(ng[:, n % 2, :], mx[:, n % 2, :], -1.0,
                                                    nsink[:, j["sink"]:j["sink"] + 1], ALU.mult, ALU.min)
                    else:
                        i = nc.vector.tensor_scalar(ng[:, n % 2, :], mx[:, n % 2, :],
                                                    -1.0 if j["reader"] == "logit" else -scale, None, ALU.mult)
                    i.then_inc(S["neg"].sem, 1)

                weighted = added = 0
                nsink = small[:, 32:40]
                if jobs[0].get("sink") is not None:
                    nc.vector.tensor_scalar(nsink, sink_col, -1.0, None, ALU.mult).then_inc(S["sinks"].sem, 1)
                    dve.wait_ge(*S["sinks"](1))
                if load_extra:
                    dve.wait_ge(*S["extra"](load_extra.count))
                logits(0)
                done = 0
                for n, j in enumerate(jobs):
                    if n + 1 < J:
                        logits(n + 1)
                    if n >= 1 and jobs[n - 1]["last"]:
                        outs_ev(dve, S, n - 1, done)
                        done += 1
                    w = j["width"]
                    dve.wait_ge(*S["prob"](n + 1))
                    s = sm[:, n % 2, :]
                    if j.get("weights") is not None:
                        for m in range(2):
                            i = nc.vector.scalar_tensor_tensor(prob[:, n % 2, m, 0:w], prob[:, n % 2, m, 0:w], 1.0,
                                                               j["weights"][:, m, 0:w], ALU.mult, ALU.mult,
                                                               accum_out=wsm[:, n % 2, m:m + 1])
                        i.then_inc(S["weight"].sem, 1)
                        weighted += 1
                        dve.wait_ge(*S["weight"](weighted))
                        s = wsm[:, n % 2, :]
                        if j.get("floor"):
                            nc.vector.tensor_scalar(s, s, 1e-30, None, ALU.max).then_inc(S["sum"].sem, 1)
                            added += 1
                            dve.wait_ge(*S["sum"](added))
                    if j.get("sink") is not None:
                        nc.vector.tensor_tensor(s, s, es[:, n % 2, :], ALU.add).then_inc(S["sum"].sem, 1)
                        added += 1
                        dve.wait_ge(*S["sum"](added))
                    nc.vector.reciprocal(rc[:, n % 2, :], s).then_inc(S["recip"].sem, 1)
                    dve.wait_ge(*S["recip"](n + 1))
                    for m in range(2):
                        i = nc.vector.tensor_scalar(prob[:, n % 2, m, 0:w], prob[:, n % 2, m, 0:w],
                                                    rc[:, n % 2, m:m + 1],
                                                    j["gate"][:, m:m + 1] if j.get("gate") is not None else None,
                                                    ALU.mult, ALU.mult if j.get("gate") is not None else ALU.bypass)
                    i.then_inc(S["norm"].sem, 1)
                outs_ev(dve, S, J - 1, done)

            stages.append((name, pe_, act_, dve_, load))

        CAUSAL = [(0, 0), (0, 1), (1, 1)]

        def causal_pv(dst, val, start, stop):
            def go(b):
                pt = probT[:, b, :]
                yield nc.tensor.matmul(dst(0), val(0), pt[:, 0:P], start=start, stop=stop, skip_group_check=True)
                yield nc.tensor.matmul(dst(1), val(0), pt[:, P:2 * P], start=False, stop=False, skip_group_check=True)
                yield nc.tensor.matmul(dst(1), val(1), pt[:, 2 * P:3 * P], start=False, stop=stop,
                                       skip_group_check=True)
            return go

        def head_dst(h):
            return lambda m: bank[7][HD * (h % 2):HD * (h % 2) + HD, m * P:(m + 1) * P]

        def head_evac(dst):
            def go(dve, S, n, done):
                h = jobs_head[id(dst)][done]
                dve.wait_ge(*S["out"](n + 1))
                nc.vector.tensor_copy(dst(h), bank[7][HD * (h % 2):HD * (h % 2) + HD, 0:SEQ]).then_inc(S["evac"].sem, 1)
            return go

        jobs_head = {}

        def a_job(h):
            p, kv = h % 2, h // 4
            rows_ = slice(HD * p, HD * p + HD)
            return dict(scores=lambda m: [(qk[rows_, h // 2, m * P:(m + 1) * P],
                                           qk[rows_, 28 if kv % 2 == p else 29, :])],
                        width=SEQ, reader="logit", load=h, buf=h % 2, sink=h, parts=CAUSAL, last=True,
                        ev_wait=h - 1 if h >= 2 else None,
                        pv=causal_pv(head_dst(h), lambda kt: v1[:, kt, kv * HD:(kv + 1) * HD], True, True))

        dst_a = lambda h: oT[HD * (h % 2):HD * (h % 2) + HD, h // 2, :]
        jobs_head[id(dst_a)] = list(range(8))
        softmax_stage("att_a", [a_job(h) for h in range(8)], HD ** -0.5, head_evac(dst_a), probT)

        count = at(0, 2, SEQ)

        def c_load(pool, S):
            pool.dma_start(count, masks[:, 4:6, :]).then_inc(S["extra"].sem, 16)
        c_load.count = 16

        def c_job(h):
            rows_ = slice(HD * (h % 2), HD * (h % 2) + HD)
            return dict(scores=lambda m: [(qk[rows_, 12 + h // 2, m * P:(m + 1) * P], qk[rows_, 20 + h // 2, :])],
                        width=SEQ, reader="logit", load=8 + h, buf=h % 2, parts=CAUSAL, last=True, weights=count,
                        ev_wait=h - 1 if h >= 2 else None,
                        pv=causal_pv(head_dst(h), lambda kt: v1[:, kt, 640 + h * HD:640 + (h + 1) * HD], True, True))

        dst_c = lambda h: oT[HD * (h % 2):HD * (h % 2) + HD, 8 + h // 2, :]
        jobs_head[id(dst_c)] = list(range(16))
        softmax_stage("att_c", [c_job(h) for h in range(16)], HD ** -0.5, head_evac(dst_c), probT, c_load)

        SB = sems("att_b", "masks score size small log soft masked suffix arg arg2 w out evac big")
        m01, mneg = bias[:, 0, :, :], bias[:, 1, :, :]
        za, zb, zc = logit, prob, at(12 * SEQ, 2, 2, SEQ)

        def b_load(pool):
            pool.dma_start(bias[:, :, :, :].rearrange("p a b c -> p (a b) c"), masks[:, 0:4, :]).then_inc(SB["masks"].sem, 16)

        def b_pe(pe):
            def scores(h):
                rows_ = slice(HD * (h % 2), HD * (h % 2) + HD)
                if h >= 2:
                    pe.wait_ge(*SB["arg"](h - 1))
                for kt in range(2):
                    mm = nc.tensor.matmul(bank[4 + h % 2][:, kt * SEQ:(kt + 1) * SEQ],
                                          qk[rows_, 8 + h // 2, kt * P:(kt + 1) * P], qk[rows_, 4 + h // 2, :],
                                          start=True, stop=True)
                mm.then_inc(SB["score"].sem, 1)
            scores(0)
            for h in range(8):
                if h < 7:
                    scores(h + 1)
                pe.wait_ge(*SB["masked"](h + 1))
                if h >= 1:
                    pe.wait_ge(*SB["arg2"](h))
                sp = za[:, h % 2, :, :]
                nc.tensor.matmul(bank[6][:, 0:SEQ], tri, sp[:, 0, :], start=True, stop=False)
                nc.tensor.matmul(bank[6][:, 0:SEQ], ones, sp[:, 1, :], start=False, stop=True)
                nc.tensor.matmul(bank[6][:, SEQ:2 * SEQ], tri, sp[:, 1, :], start=True, stop=True)\
                    .then_inc(SB["suffix"].sem, 1)
                pe.wait_ge(*SB["w"](h + 1))
                if h >= 2:
                    pe.wait_ge(*SB["evac"](h - 1))
                o = bank[7][HD * (h % 2):HD * (h % 2) + HD, :]
                w = zb[:, h % 2, :, :]
                nc.tensor.matmul(o[:, 0:SEQ], v1[:, 0, P + h * HD:P + (h + 1) * HD], w[:, 0, :],
                                 start=True, stop=False, skip_group_check=True)
                nc.tensor.matmul(o[:, P:SEQ], v1[:, 1, P + h * HD:P + (h + 1) * HD], w[:, 1, P:SEQ],
                                 start=False, stop=True, skip_group_check=True).then_inc(SB["out"].sem, 1)

        def b_act(act):
            for h in range(9):
                if h < 8:
                    act.wait_ge(*SB["size"](h + 1))
                    nc.scalar.activation(zb[:, h % 2, :, :], za[:, h % 2, :, :], ACT.Exp, scale=HD ** -0.5)\
                        .then_inc(SB["small"].sem, 1)
                    act.wait_ge(*SB["small"](h + 1))
                    if h >= 2:
                        act.wait_ge(*SB["soft"](h - 1))
                    nc.scalar.activation(zc[:, h % 2, :, :], zb[:, h % 2, :, :], ACT.Ln, bias=1.0)\
                        .then_inc(SB["log"].sem, 1)
                if h >= 1:
                    act.wait_ge(*SB["arg2"](h))
                    nc.scalar.activation(zb[:, (h - 1) % 2, :, :], zb[:, (h - 1) % 2, :, :], ACT.Exp)\
                        .then_inc(SB["w"].sem, 1)

        def b_dve(dve):
            def bank3(b):
                return bank[b][:, :].rearrange("p (a b) -> p a b", a=2)

            def size(h):
                dve.wait_ge(*SB["score"](h + 1))
                if h >= 2:
                    dve.wait_ge(*SB["suffix"](h - 1))
                    dve.wait_ge(*SB["out"](h - 1))
                nc.vector.tensor_scalar(za[:, h % 2, :, :], bank3(4 + h % 2), -1.0, None, ALU.mult)\
                    .then_inc(SB["big"].sem, 1)
                dve.wait_ge(*SB["big"](2 * h + 1))
                nc.vector.tensor_tensor(za[:, h % 2, :, :], za[:, h % 2, :, :], bank3(4 + h % 2), ALU.min)\
                    .then_inc(SB["size"].sem, 1)

            dve.wait_ge(*SB["masks"](16))
            size(0)
            for h in range(8):
                b = bank3(4 + h % 2)
                dve.wait_ge(*SB["log"](h + 1))
                nc.vector.tensor_scalar(za[:, h % 2, :, :], b, 0.0, HD ** -0.5, ALU.max, ALU.mult)\
                    .then_inc(SB["big"].sem, 1)
                dve.wait_ge(*SB["big"](2 * h + 2))
                nc.vector.tensor_tensor(za[:, h % 2, :, :], za[:, h % 2, :, :], zc[:, h % 2, :, :], ALU.add)\
                    .then_inc(SB["soft"].sem, 1)
                dve.wait_ge(*SB["soft"](h + 1))
                nc.vector.tensor_tensor(za[:, h % 2, :, :], za[:, h % 2, :, :], m01, ALU.mult)\
                    .then_inc(SB["masked"].sem, 1)
                nc.vector.scalar_tensor_tensor(zb[:, h % 2, :, :], b, HD ** -0.5, mneg, ALU.mult, ALU.add)\
                    .then_inc(SB["arg"].sem, 1)
                if h < 7:
                    size(h + 1)
                if h >= 1:
                    dve.wait_ge(*SB["out"](h))
                    nc.vector.tensor_copy(dst_b(h - 1), bank[7][HD * ((h - 1) % 2):HD * ((h - 1) % 2) + HD, 0:SEQ])\
                        .then_inc(SB["evac"].sem, 1)
                dve.wait_ge(*SB["suffix"](h + 1))
                dve.wait_ge(*SB["arg"](h + 1))
                nc.vector.tensor_tensor(zb[:, h % 2, :, :], zb[:, h % 2, :, :], bank3(6), ALU.subtract)\
                    .then_inc(SB["arg2"].sem, 1)
            dve.wait_ge(*SB["out"](8))
            nc.vector.tensor_copy(dst_b(7), bank[7][HD:P, 0:SEQ]).then_inc(SB["evac"].sem, 1)

        dst_b = lambda h: oT[HD * (h % 2):HD * (h % 2) + HD, 4 + h // 2, :]
        stages.append(("att_b", b_pe, b_act, b_dve, b_load))

        norm_stage("normmix", oT, "mix_gain", [(0, 4), (4, 4), (8, 8)], at(0, NT, SEQ), at(4096, 4, SEQ),
                   at(5120, 3, SEQ))

        def residual_stage(name, u0, write):
            S = shared("residual", ev=8)

            def chunk(pe, u, c, q, first_two):
                if not first_two:
                    pe.wait_ge(*S["ev"](c * 2 - 2))
                for j in range(8):
                    unit_features(pe, u + j, j, h_hi, h_lo, 2 * j, bank[2 * q:2 * q + 2], j == 0, j == 7)\
                        .then_inc(unit_done, 1)

            def pe_(pe):
                chunk(pe, u0, 0, 0, True)
                chunk(pe, u0 + 8, 1, 1, True)
                chunk(pe, u0 + 16, 2, 0, False)
                chunk(pe, u0 + 24, 3, 1, False)

            def act_(act):
                for u in range(u0, u0 + 32):
                    if u + LEAD < UNITS:
                        split_hi(act, u, u - u0)

            def dve_(dve):
                for c in range(4):
                    for j in range(8):
                        if u0 + 8 * c + j + LEAD < UNITS:
                            split_lo(dve, u0 + 8 * c + j, j)
                    dve.wait_ge(unit_done, u0 + 8 * c + 8)
                    for b in range(2):
                        t = 4 * c + 2 * b
                        nc.vector.tensor_tensor(x[:, t:t + 2, :], x[:, t:t + 2, :],
                                                bank[2 * (c % 2) + b][:, :].rearrange("p (a b) -> p a b", a=2),
                                                ALU.add).then_inc(S["ev"].sem, 1)

            stages.append((name, pe_, act_, dve_, None))

        residual_stage("wout", STREAM["wout"], x)

        norm_stage("norm2", x, "ffn_norm", [(0, NT)], at(0, NT, SEQ), at(4096, 4, SEQ), at(5120, 3, SEQ))

        gT = at(0, NF, SEQ)
        cv = at(11264, 2, 4, SEQ)
        SU = sems("up", "centre conv1 conv2 silu prod")
        UU = STREAM["up"]
        CW, CB = VEC["conv_w"][0], VEC["conv_b"][0]

        def up_pe(pe):
            for k in range(2):
                for j in range(8):
                    unit_features(pe, UU + 8 * k + j, j, h_hi, h_lo, 2 * j, bank[2 * k:2 * k + 2],
                                  j == 0, j == 7).then_inc(unit_done, 1)
            with pe.Fori(1, 11) as i:
                for k in range(2):
                    pe.wait_ge(*SU["conv2"](i * 8 + (4 * k - 4)))
                    for j in range(8):
                        unit_features(pe, i * 16 + (UU + 8 * k + j), j, h_hi, h_lo, 2 * j,
                                      bank[2 * k:2 * k + 2], j == 0, j == 7).then_inc(unit_done, 1)

        def up_turn_act(act, i, first):
            for k in range(2):
                u = i * 16 + (UU + 8 * k)
                chunk_split(act, split_hi, u)
                act.wait_ge(unit_done, u + 8)
                if not first:
                    act.wait_ge(*SU["prod"](i))
                for f in range(4):
                    c = i * 4 + (44 * k + f)
                    nc.scalar.activation(cv[:, k, f, :], bank[2 * k + f // 2][:, (f % 2) * SEQ:(f % 2 + 1) * SEQ],
                                         ACT.Identity, bias=vec[:, bass.ds(c + CB, 1)],
                                         scale=vec[:, bass.ds(c + (CW + 2 * 88), 1)]).then_inc(SU["centre"].sem, 1)
            act.wait_ge(*SU["conv2"](i * 8 + 4))
            nc.scalar.activation(cv[:, 0, :, :], cv[:, 0, :, :], ACT.Silu).then_inc(SU["silu"].sem, 1)

        def up_act(act):
            up_turn_act(act, 0, True)
            with act.Fori(1, 11) as i:
                up_turn_act(act, i, False)

        def up_dve(dve):
            with dve.Fori(0, 11) as i:
                for k in range(2):
                    u = i * 16 + (UU + 8 * k)
                    chunk_split(dve, split_lo, u)
                    for f in range(4):
                        c = i * 4 + (44 * k + f)
                        b = bank[2 * k + f // 2][:, (f % 2) * SEQ:(f % 2 + 1) * SEQ]
                        dve.wait_ge(*SU["centre"](i * 8 + (4 * k + (2 if f < 2 else 4))))
                        nc.vector.scalar_tensor_tensor(cv[:, k, f, 1:SEQ], b[:, 0:SEQ - 1],
                                                       vec[:, bass.ds(c + (CW + 88), 1)], cv[:, k, f, 1:SEQ],
                                                       ALU.mult, ALU.add).then_inc(SU["conv1"].sem, 1)
                    for f in range(4):
                        c = i * 4 + (44 * k + f)
                        b = bank[2 * k + f // 2][:, (f % 2) * SEQ:(f % 2 + 1) * SEQ]
                        dve.wait_ge(*SU["conv1"](i * 8 + (4 * k + f + 1)))
                        nc.vector.scalar_tensor_tensor(cv[:, k, f, 2:SEQ], b[:, 0:SEQ - 2],
                                                       vec[:, bass.ds(c + CW, 1)], cv[:, k, f, 2:SEQ],
                                                       ALU.mult, ALU.add).then_inc(SU["conv2"].sem, 1)
                        if f == 3:
                            dve.wait_ge(*SU["conv2"](i * 8 + (4 * k + 4)))
                dve.wait_ge(*SU["silu"](i + 1))
                nc.vector.tensor_tensor(gT[:, bass.ds(i * 4, 4), :], cv[:, 0, :, :], cv[:, 1, :, :], ALU.mult)\
                    .then_inc(SU["prod"].sem, 1)

        stages.append(("up", up_pe, up_act, up_dve, None))

        SD = sems("down", "g_hi g_lo ev_a ev_d")
        UD = STREAM["down"]

        def down_turn(pe, i, buf, j0, first, last):
            pe.wait_ge(*SD["g_lo"](i + 1))
            for j in range(4):
                unit_features(pe, i * 4 + (UD + j), j, o_hi[:, 2 * buf:2 * buf + 2, :], o_lo[:, 2 * buf:2 * buf + 2, :],
                              0, bank[2 * j:2 * j + 2], first, last).then_inc(unit_done, 1)

        def down_pe(pe):
            down_turn(pe, 0, 0, 0, True, False)
            down_turn(pe, 1, 1, 4, False, False)
            with pe.Fori(1, 10) as i:
                for b in range(2):
                    down_turn(pe, i * 2 + b, b, 4 * b, False, False)
            down_turn(pe, 20, 0, 0, False, False)
            down_turn(pe, 21, 1, 4, False, True)

        def down_turn_act(act, i, b, first):
            if not first:
                act.wait_ge(unit_done, i * 4 + (UD - 4))
            nc.scalar.activation(o_hi[:, 2 * b:2 * b + 2, :], gT[:, bass.ds(i * 2, 2), :], ACT.Copy)\
                .then_inc(SD["g_hi"].sem, 1)

        def down_act(act):
            down_turn_act(act, 0, 0, True)
            down_turn_act(act, 1, 1, True)
            for b in range(2):
                for j in range(4):
                    split_hi(act, UD + 4 * b + j, j)
            with act.Fori(1, 11) as i:
                for b in range(2):
                    down_turn_act(act, i * 2 + b, b, False)
                    for j in range(4):
                        split_hi(act, i * 8 + (UD + 4 * b + j), j)

        def down_turn_dve(dve, i, b, first):
            dve.wait_ge(*SD["g_hi"](i + 1))
            if not first:
                dve.wait_ge(unit_done, i * 4 + (UD - 4))
            nc.vector.tensor_tensor(o_lo[:, 2 * b:2 * b + 2, :], gT[:, bass.ds(i * 2, 2), :],
                                    o_hi[:, 2 * b:2 * b + 2, :].bitcast(F32), ALU.subtract).then_inc(SD["g_lo"].sem, 1)

        def down_dve(dve):
            down_turn_dve(dve, 0, 0, True)
            down_turn_dve(dve, 1, 1, True)
            for b in range(2):
                for j in range(4):
                    split_lo(dve, UD + 4 * b + j, j)
            with dve.Fori(1, 11) as i:
                for b in range(2):
                    down_turn_dve(dve, i * 2 + b, b, False)
                    for j in range(4):
                        split_lo(dve, i * 8 + (UD + 4 * b + j), j)
            dve.wait_ge(unit_done, UD + 88)
            for b in range(8):
                nc.vector.tensor_tensor(x[:, 2 * b:2 * b + 2, :], x[:, 2 * b:2 * b + 2, :],
                                        bank[b][:, :].rearrange("p (a b) -> p a b", a=2), ALU.add)\
                    .then_inc(SD["ev_d"].sem, 1)

        stages.append(("down", down_pe, down_act, down_dve, None))

        SX = shared("split", hi=4, lo=4)

        def splitx_act(act):
            for n in range(4):
                nc.scalar.activation(h_hi[:, 4 * n:4 * n + 4, :], x[:, 4 * n:4 * n + 4, :], ACT.Copy)\
                    .then_inc(SX["hi"].sem, 1)

        def splitx_dve(dve):
            for n in range(4):
                dve.wait_ge(*SX["hi"](n + 1))
                nc.vector.tensor_tensor(h_lo[:, 4 * n:4 * n + 4, :], x[:, 4 * n:4 * n + 4, :],
                                        h_hi[:, 4 * n:4 * n + 4, :].bitcast(F32), ALU.subtract)\
                    .then_inc(SX["lo"].sem, 1)

        stages.append(("split_x", lambda pe: None, splitx_act, splitx_dve, None))

        merged = at(0, NT, SEQ)
        B0 = 4096

        def merge_stage(name, u0, first):
            S = shared("merge", sig=8, prod=8, add=0 if first else 8)
            sig, prod = at(B0, 2, 2, SEQ), at(B0 + 1024, 2, 2, SEQ)

            def turn_pe(pe, i, first_turn):
                if not first_turn:
                    pe.wait_ge(*S["sig"](i * 2))
                for j in range(8):
                    unit_features(pe, i * 12 + (u0 + j), j, h_hi, h_lo, 2 * j, bank[0:2], j == 0, j == 7)\
                        .then_inc(unit_done, 1)
                if not first_turn:
                    pe.wait_ge(*S["prod"](i * 2))
                for j in range(4):
                    unit_features(pe, i * 12 + (u0 + 8 + j), j, o_hi, o_lo, 2 * j, bank[2:4], j == 0, j == 3)\
                        .then_inc(unit_done, 1)

            def pe_(pe):
                turn_pe(pe, 0, True)
                with pe.Fori(1, 4) as i:
                    turn_pe(pe, i, False)

            def turn_act(act, i, first_turn):
                for j in range(12):
                    split_hi(act, i * 12 + (u0 + j), j)
                    if j == 7:
                        act.wait_ge(unit_done, i * 12 + (u0 + 8))
                        if not first_turn:
                            act.wait_ge(*S["prod"](i * 2))
                        for b in range(2):
                            nc.scalar.activation(sig[:, b, :, :], bank[b][:, :].rearrange("p (a b) -> p a b", a=2),
                                                 ACT.Sigmoid).then_inc(S["sig"].sem, 1)

            def act_(act):
                turn_act(act, 0, True)
                with act.Fori(1, 4) as i:
                    turn_act(act, i, False)

            def dve_(dve):
                with dve.Fori(0, 4) as i:
                    for j in range(12):
                        split_lo(dve, i * 12 + (u0 + j), j)
                    dve.wait_ge(unit_done, i * 12 + (u0 + 12))
                    dve.wait_ge(*S["sig"](i * 2 + 2))
                    for b in range(2):
                        d = merged[:, bass.ds(i * 4 + 2 * b, 2), :]
                        src = bank[2 + b][:, :].rearrange("p (a b) -> p a b", a=2)
                        if first:
                            nc.vector.tensor_tensor(d, src, sig[:, b, :, :], ALU.mult).then_inc(S["prod"].sem, 1)
                        else:
                            nc.vector.tensor_tensor(prod[:, b, :, :], src, sig[:, b, :, :], ALU.mult)\
                                .then_inc(S["prod"].sem, 1)
                            dve.wait_ge(*S["prod"](i * 2 + (b + 1)))
                            nc.vector.tensor_tensor(d, d, prod[:, b, :, :], ALU.add).then_inc(S["add"].sem, 1)

            stages.append((name, pe_, act_, dve_, None))

        def product_stage(name, src, gate_tiles, extra=None):
            S = shared("product", silu=1, scaled=8, hi=4, lo=4)

            def act_(act):
                nc.scalar.activation(gate_tiles, gate_tiles, ACT.Silu).then_inc(S["silu"].sem, 1)
                to_moving_act(act, S, src, o_hi, 4)

            def dve_(dve):
                dve.wait_ge(*S["silu"](1))
                put = to_moving_dve(dve, S, src, o_hi, o_lo)
                for p in range(4):
                    nc.vector.tensor_tensor(src[:, 2 * p:2 * p + 2, :], src[:, 2 * p:2 * p + 2, :],
                                            gate_tiles[:, 2 * p:2 * p + 2, :], ALU.mult).then_inc(S["scaled"].sem, 2)
                    if p >= 1:
                        put(p - 1)
                put(3)

            stages.append((name, lambda pe: None, act_, dve_, None))

        ua, ga = at(B0, 8, SEQ), at(B0 + 2048, 8, SEQ)
        va = at(B0 + 4096, 2, 1024)
        sw = at(B0 + 6144, 8, P)
        lnr = at(B0 + 7168, 2, 1024)
        sbr = at(B0 + 9216, 8 * P, parts=(0, 1))
        ev_a = halves(6)
        UA = STREAM["p_a"]
        SA = sems("gmlp", "load gelu st ag sd rc n g b u mask mixed prod")

        def pa_load(pool):
            pool.dma_start(sw, sgu_wT).then_inc(SA["load"].sem, 16)
            pool.dma_start(lnr, ln_rows.broadcast_to([P, 2 * 1024]).rearrange("p (a b) -> p a b", a=2))\
                .then_inc(SA["load"].sem, 16)
            pool.dma_start(sbr, sgu_b).then_inc(SA["load"].sem, 16)

        uag = at(B0, 16, SEQ)

        def pa_pe(pe):
            features_pe(pe, ev_a, UA, 4)
            tokens_pe(pe, ev_a, UA + 32, 4, 2)

        def pa_act(act):
            features_act(act, ev_a, UA, 4, uag)
            tokens_act(act, ev_a, UA + 32, 4, 2, lambda m, c: va[:, m, c * UN:(c + 1) * UN])

        def pa_dve(dve):
            features_dve(dve, ev_a, UA, 4, uag)
            tokens_dve(dve, ev_a, UA + 32, 4, 2, lambda m, c: va[:, m, c * UN:(c + 1) * UN])

        stages.append(("p_a", pa_pe, pa_act, pa_dve, pa_load))

        stat = small[:, 40:64].rearrange("p (a b) -> p a b", a=2)
        mv = small[:, 64:68].rearrange("p (a b) -> p a b", a=2)
        rs = small[:, 68:70]

        def gmlp_act(act):
            for m in range(2):
                nc.scalar.activation(va[:, m, :], va[:, m, :], ACT.Gelu_apprx_tanh).then_inc(SA["gelu"].sem, 1)
            nc.scalar.activation(ua, ua, ACT.Gelu_apprx_tanh).then_inc(SA["u"].sem, 1)
            for m in range(2):
                act.wait_ge(*SA["ag"](m + 1))
                nc.scalar.activation(rs[:, m:m + 1], mv[:, m, 1:2], ACT.Sqrt, bias=ln_eps_col).then_inc(SA["sd"].sem, 1)

        def gmlp_dve(dve):
            dve.wait_ge(*SA["load"](48))
            nc.vector.tensor_tensor(sw, sw, causal.unsqueeze(1).broadcast_to([P, 8, P]), ALU.mult)\
                .then_inc(SA["mask"].sem, 1)
            for m in range(2):
                dve.wait_ge(*SA["gelu"](m + 1))
                for c in range(2):
                    nc.vector.bn_stats(stat[:, m, 6 * c:6 * c + 6], va[:, m, c * 512:(c + 1) * 512])\
                        .then_inc(SA["st"].sem, 1)
                dve.wait_ge(*SA["st"](2 * m + 2))
                nc.vector.bn_aggr(mv[:, m, :], stat[:, m, :]).then_inc(SA["ag"].sem, 1)
            for m in range(2):
                dve.wait_ge(*SA["sd"](m + 1))
                dve.wait_ge(*SA["ag"](m + 1))
                nc.vector.reciprocal(rs[:, m:m + 1], rs[:, m:m + 1]).then_inc(SA["rc"].sem, 1)
                dve.wait_ge(*SA["rc"](m + 1))
                nc.vector.tensor_scalar(va[:, m, :], va[:, m, :], mv[:, m, 0:1], rs[:, m:m + 1], ALU.subtract,
                                        ALU.mult).then_inc(SA["n"].sem, 1)
                dve.wait_ge(*SA["n"](m + 1))
                nc.vector.tensor_tensor(va[:, m, :], va[:, m, :], lnr[:, 0, :], ALU.mult).then_inc(SA["g"].sem, 1)
                dve.wait_ge(*SA["g"](m + 1))
                nc.vector.tensor_tensor(va[:, m, :], va[:, m, :], lnr[:, 1, :], ALU.add).then_inc(SA["b"].sem, 1)
            dve.wait_ge(*SA["u"](1))
            for g in range(4):
                dve.wait_ge(*SA["mixed"](g + 1))
                nc.vector.tensor_tensor(ua[:, 2 * g:2 * g + 2, :], ua[:, 2 * g:2 * g + 2, :],
                                        bank[4 + g][:, :].rearrange("p (a b) -> p a b", a=2), ALU.mult)\
                    .then_inc(SA["prod"].sem, 1)

        def gmlp_pe(pe):
            pe.wait_ge(*SA["mask"](1))
            pe.wait_ge(*SA["b"](2))
            for g in range(8):
                for c in range(2):
                    o = bank[4 + g // 2][:, (g % 2) * SEQ + c * P:(g % 2) * SEQ + (c + 1) * P]
                    nc.tensor.matmul(o, va[:, c, g * P:(g + 1) * P], sw[:, g, :], start=True, stop=False)
                    mm = nc.tensor.matmul(o, ones[0:1, :], sbr[:, g * P:(g + 1) * P], start=False, stop=True)
                if g % 2:
                    mm.then_inc(SA["mixed"].sem, 1)

        stages.append(("gmlp", gmlp_pe, gmlp_act, gmlp_dve, None))
        product_stage("o_a", ua, ga)
        merge_stage("m_a", STREAM["m_a"], True)

        xb, gb, xc = at(B0, 8, SEQ), at(B0 + 2048, 8, SEQ), at(B0 + 4096, 8, SEQ)
        lw = at(B0 + 6144, 2, 8, P)
        iv, av, tv = at(B0 + 8192, 8, SEQ), at(B0 + 10240, 8, SEQ), at(B0 + 12288, 8, SEQ)
        rv = xb
        xgb = at(B0, 16, SEQ)
        ev_b = halves(4)
        UB = STREAM["p_b"]
        SL = sems("lru", "load c0 c1 c2 c3 mm i chain spn t a2 f s g1 g2 scan al ex2")

        def pb_load(pool):
            pool.dma_start(lw, lru_w).then_inc(SL["load"].sem, 16)

        stages.append(("p_b", lambda pe: features_pe(pe, ev_b, UB, 4),
                       lambda act: features_act(act, ev_b, UB, 4, xgb),
                       lambda dve: features_dve(dve, ev_b, UB, 4, xgb), pb_load))
        C2, C2B = VEC["conv2_w"][0], VEC["conv2_b"][0]
        lam = vec[:, VEC["lru_lam"][0]:VEC["lru_lam"][0] + 8]
        T = [small[:, 72 + 8 * n:80 + 8 * n] for n in range(7)]
        LOG_TERMS = 9

        def lru_act(act):
            act.wait_ge(*SL["al"](1))
            nc.scalar.activation(T[0], T[0], ACT.Exp).then_inc(SL["ex2"].sem, 1)
            for t in range(8):
                act.wait_ge(*SL["mm"](t + 1))
                nc.scalar.activation(rv[:, t, :], bank[4 + t % 4][:, 0:SEQ], ACT.Sigmoid, bias=vcol("lru_ba", t))
                nc.scalar.activation(iv[:, t, :], bank[4 + t % 4][:, SEQ:2 * SEQ], ACT.Sigmoid,
                                     bias=vcol("lru_bx", t)).then_inc(SL["i"].sem, 1)
            act.wait_ge(*SL["i"](8))
            act.wait_ge(*SL["spn"](1))
            for t in range(8):
                nc.scalar.activation(av[:, t, :], rv[:, t, :], ACT.Exp, scale=T[5][:, t:t + 1])
                nc.scalar.activation(tv[:, t, :], rv[:, t, :], ACT.Tanh, scale=T[6][:, t:t + 1]).then_inc(SL["t"].sem, 1)
            for t in range(4):
                act.wait_ge(*SL["f"](t + 1))
                nc.scalar.activation(tv[:, 2 * t:2 * t + 2, :], tv[:, 2 * t:2 * t + 2, :], ACT.Sqrt).then_inc(SL["s"].sem, 1)

        def lru_dve(dve):
            n = [0]

            def link(i):
                n[0] += 1
                i.then_inc(SL["chain"].sem, 1)
                dve.wait_ge(*SL["chain"](n[0]))
            link(nc.vector.tensor_scalar(T[1], lam, -1.0, None, ALU.mult))
            nc.vector.tensor_tensor(T[0], T[1], lam, ALU.min).then_inc(SL["al"].sem, 1)
            dve.wait_ge(*SL["ex2"](1))
            link(nc.vector.tensor_scalar(T[2], T[0], 2.0, None, ALU.add))
            link(nc.vector.reciprocal(T[2], T[2]))
            link(nc.vector.tensor_tensor(T[2], T[2], T[0], ALU.mult))
            link(nc.vector.tensor_tensor(T[3], T[2], T[2], ALU.mult))
            link(nc.vector.memset(T[4], 2.0 / (2 * LOG_TERMS + 1)))
            for k in range(LOG_TERMS - 1, -1, -1):
                link(nc.vector.tensor_tensor(T[4], T[4], T[3], ALU.mult))
                link(nc.vector.tensor_scalar(T[4], T[4], 2.0 / (2 * k + 1), None, ALU.add))
            link(nc.vector.tensor_tensor(T[4], T[4], T[2], ALU.mult))
            link(nc.vector.tensor_scalar(T[1], T[1], 0.0, None, ALU.max))
            link(nc.vector.tensor_tensor(T[4], T[4], T[1], ALU.add))
            link(nc.vector.tensor_scalar(T[5], T[4], -8.0, None, ALU.mult))
            nc.vector.tensor_scalar(T[6], T[4], 8.0, None, ALU.mult).then_inc(SL["spn"].sem, 1)
            for tap in range(4):
                d = 3 - tap if tap else 0
                for t in range(8):
                    w = vec[:, C2 + 8 * (3 - tap) + t:C2 + 8 * (3 - tap) + t + 1]
                    if tap == 0:
                        nc.vector.tensor_scalar(xc[:, t, :], xb[:, t, :], w, vec[:, C2B + t:C2B + t + 1], ALU.mult,
                                                ALU.add).then_inc(SL["c0"].sem, 1)
                    else:
                        dve.wait_ge(*SL[f"c{tap - 1}"](t + 1))
                        nc.vector.scalar_tensor_tensor(xc[:, t, tap:SEQ], xb[:, t, 0:SEQ - tap], w,
                                                       xc[:, t, tap:SEQ], ALU.mult, ALU.add).then_inc(SL[f"c{tap}"].sem, 1)
            for t in range(4):
                dve.wait_ge(*SL["t"](2 * t + 2))
                two = slice(2 * t, 2 * t + 2)
                nc.vector.tensor_tensor(rv[:, two, :], av[:, two, :], av[:, two, :], ALU.mult).then_inc(SL["a2"].sem, 1)
                dve.wait_ge(*SL["a2"](t + 1))
                nc.vector.scalar_tensor_tensor(tv[:, two, :], rv[:, two, :], 1.0, tv[:, two, :], ALU.add, ALU.mult)\
                    .then_inc(SL["f"].sem, 1)
                nc.vector.tensor_tensor(iv[:, two, :], iv[:, two, :], xc[:, two, :], ALU.mult).then_inc(SL["g1"].sem, 1)
            for t in range(4):
                two = slice(2 * t, 2 * t + 2)
                dve.wait_ge(*SL["s"](t + 1))
                dve.wait_ge(*SL["g1"](t + 1))
                nc.vector.tensor_tensor(iv[:, two, :], iv[:, two, :], tv[:, two, :], ALU.mult).then_inc(SL["g2"].sem, 1)
            for t in range(8):
                dve.wait_ge(*SL["g2"](t // 2 + 1))
                nc.vector.tensor_tensor_scan(xc[:, t, :], av[:, t, :], iv[:, t, :], 0.0, ALU.mult, ALU.add)\
                    .then_inc(SL["scan"].sem, 1)

        def lru_pe(pe):
            pe.wait_ge(*SL["load"](16))
            for t in range(8):
                pe.wait_ge(*SL["c3"](t + 1))
                if t >= 4:
                    pe.wait_ge(*SL["i"](t - 3))
                for n in range(2):
                    mm = nc.tensor.matmul(bank[4 + t % 4][:, n * SEQ:(n + 1) * SEQ], lw[:, n, t, :], xc[:, t, :],
                                          start=True, stop=True)
                mm.then_inc(SL["mm"].sem, 1)

        stages.append(("lru", lru_pe, lru_act, lru_dve, None))
        product_stage("o_b", xc, gb)
        merge_stage("m_b", STREAM["m_b"], False)

        qm, gm = at(B0, 8, SEQ), at(B0 + 2048, 8, SEQ)
        om = at(B0 + 4096, 8, SEQ)
        W2 = B0 + 6144 + 4864
        ev_m = halves(4)
        UQ = STREAM["p_m"]
        qgm = at(B0, 16, SEQ)
        stages.append(("p_m", lambda pe: features_pe(pe, ev_m, UQ, 4),
                       lambda act: features_act(act, ev_m, UQ, 4, qgm),
                       lambda dve: features_dve(dve, ev_m, UQ, 4, qgm), None))
        m_probT = at(WK + 2048, 2, 4 * P)

        def m_pv(h):
            def go(b):
                for d in range(2):
                    for kt in range(2):
                        yield nc.tensor.matmul(bank[7][:, d * SEQ:(d + 1) * SEQ],
                                               vm[:, kt, h * SEQ + d * P:h * SEQ + (d + 1) * P],
                                               m_probT[:, b, kt * SEQ:(kt + 1) * SEQ], start=kt == 0, stop=kt == 1)
            return go

        def m_job(h):
            return dict(scores=lambda m: [(qm[:, 2 * h + d, m * P:(m + 1) * P], kmT[:, 2 * h + d, :]) for d in range(2)],
                        width=SEQ, reader="prob", parts=[(0, 0), (0, 1), (1, 0), (1, 1)], last=True,
                        ev_wait=h if h >= 1 else None, pv=m_pv(h))

        def m_evac(dve, S, n, done):
            dve.wait_ge(*S["out"](n + 1))
            nc.vector.tensor_copy(om[:, 2 * n:2 * n + 2, :], bank[7][:, :].rearrange("p (a b) -> p a b", a=2))\
                .then_inc(S["evac"].sem, 1)

        softmax_stage("att_m", [m_job(h) for h in range(4)], SEQ ** -0.5, m_evac, m_probT)
        product_stage("o_m", om, gm)
        merge_stage("m_m", STREAM["m_m"], False)

        C0 = B0
        qc = at(C0, 8, SEQ)
        cmpT = at(C0 + 2048, 4, SEQ)
        ksw = at(C0 + 3072, 4, SEQ)
        gc = at(C0 + 4096, 8, SEQ)
        swp = at(C0 + 6144, 4, SEQ)
        vsw = at(C0 + 7168, 2, 512)
        onc = at(C0 + 8192, 8, SEQ)
        zz = at(C0 + 8192, 2, 4 * SEQ)
        w1 = at(C0 + 10240, 4096)
        qgc = at(C0, 24, SEQ)
        glr = kmT[:, 0:3, :].rearrange("p a b -> p (a b)")
        w2 = vm[:, 0, 0:256].rearrange("p (a b c) -> p a b c", a=2, b=2)
        kcT = vm[:, 0, 256:316]
        vcs = vm[0:15, 0, 320:576]
        hid = vm[:, 0, 576:816].rearrange("p (a b c) -> p a b c", a=2, b=2)
        pec = vm[:, 0, 816:820].rearrange("p (a b) -> p a b", a=2)
        cmk = vm[:, 1, 0:30].rearrange("p (a b) -> p a b", a=2)
        cb = vm[:, 1, 64:544].rearrange("p (h m n) -> p h m n", m=2, n=15)
        gts = vm[:, 1, 544:640].rearrange("p (m g) -> p m g", m=2)
        glb = vm[:, 1, 640:688]
        oh2 = kmT[0:33, 4:6, :].rearrange("p a b -> p (a b)")
        tb2 = kmT[0:33, 6, 0:40]
        gl_hi = w_gl_hi = None
        ev_c = halves(7)
        UC = STREAM["p_c"]
        SC = sems("nsa", "load swap gate gl bias cbev z w1k w1v hid pe h kc kcv g2")

        def pc_load(pool):
            pool.dma_start(glr.rearrange("p (a b) -> p a b", a=NT), gl_w).then_inc(SC["load"].sem, 16)
            pool.dma_start(glb, gl_b.broadcast_to([P, 48])).then_inc(SC["load"].sem, 16)
            pool.dma_start(oh2, onehots[:, 3, :]).then_inc(SC["load"].sem, 16)
            pool.dma_start(tb2, tabs).then_inc(SC["load"].sem, 16)
            pool.dma_start(cmk, cmask).then_inc(SC["load"].sem, 16)
            pool.dma_start(w2[:, 0, :, :], cmp_w2k).then_inc(SC["load"].sem, 16)
            pool.dma_start(w2[:, 1, :, :], cmp_w2v).then_inc(SC["load"].sem, 16)

        def pc_pe(pe):
            features_pe(pe, ev_c, UC, 6)
            tokens_pe(pe, ev_c, UC + 48, 6, 1)

        def pc_act(act):
            features_act(act, ev_c, UC, 6, qgc)
            tokens_act(act, ev_c, UC + 48, 6, 1, lambda m, c: vsw[:, m, :])

        def pc_dve(dve):
            features_dve(dve, ev_c, UC, 6, qgc)
            tokens_dve(dve, ev_c, UC + 48, 6, 1, lambda m, c: vsw[:, m, :])

        stages.append(("p_c", pc_pe, pc_act, pc_dve, pc_load))

        def cmp_load(pool):
            for t in range(4):
                pool.dma_start(swp[HD:P, t, :], ksw[0:HD, t, :]).then_inc(SC["swap"].sem, 16)
                pool.dma_start(swp[0:HD, t, :], ksw[HD:P, t, :]).then_inc(SC["swap"].sem, 16)
            for n in range(2):
                for h in range(4):
                    src = cmpT[HD * (h % 2):HD * (h % 2) + HD, 2 * n + h // 2, :]
                    pool.dma_start(zz[0:HD, n, h * SEQ:(h + 1) * SEQ], src).then_inc(SC["z"].sem, 16)
                    pool.dma_start(zz[HD:P, n, h * SEQ:(h + 1) * SEQ - 1], src[:, 1:SEQ]).then_inc(SC["z"].sem, 16)
            pool.dma_start(w1, cmp_w1[0]).then_inc(SC["w1k"].sem, 16)
            pool.wait_ge(*SC["hid"](1))
            pool.dma_start(w1, cmp_w1[1]).then_inc(SC["w1v"].sem, 16)
            pool.wait_ge(*SC["swap"](128))
            pool.wait_ge(*SC["z"](256))

        def cmp_pe(pe):
            pe.wait_ge(*SC["load"](112))
            for m in range(2):
                for t in range(NT):
                    mm = nc.tensor.matmul(bank[4][:, 48 * m:48 * m + 48], x[:, t, m * P:(m + 1) * P],
                                          glr[:, 48 * t:48 * t + 48], start=t == 0, stop=t == NT - 1)
            mm.then_inc(SC["gl"].sem, 1)
            for m in range(2):
                for n in range(15):
                    a = SEQ + P * m - 16 * n - 31
                    mm = nc.tensor.matmul(bank[5][:, (m * 15 + n) * 16:(m * 15 + n + 1) * 16],
                                          oh2[:, a:a + P], tb2[:, 24:40], start=True, stop=True)
            mm.then_inc(SC["bias"].sem, 1)
            pe.wait_ge(*SC["z"](256))
            for n, w in enumerate(("w1k", "w1v")):
                pe.wait_ge(*SC[w](16))
                pv = VEC["cmp_pe_k" if n == 0 else "cmp_pe_v"][0]
                for o in range(2):
                    if n:
                        pe.wait_ge(*SC["h"](2))
                    for j in range(16):
                        w_ = w1[:, j * 256 + o * P:j * 256 + (o + 1) * P]
                        blocks_ = zz[:, n, :].rearrange("p (h s) -> p h s", h=4)[:, :, 2 * j:2 * j + 225:16]
                        nc.tensor.matmul(bank[6 + o][:, 0:60], w_, blocks_, start=j == 0, stop=j == 15,
                                         skip_group_check=True)
                        mm = nc.tensor.matmul(bank[6 + o][:, 60:61], w_, vec[:, pv + j:pv + j + 1], start=False,
                                              stop=j == 15, skip_group_check=True)
                mm.then_inc(SC["hid"].sem, 1)
            pe.wait_ge(*SC["h"](4))
            pe.wait_ge(*SC["g2"](1))
            for half in range(2):
                for o in range(2):
                    mm = nc.tensor.matmul(bank[4][HD * half:HD * half + HD, 0:60], w2[:, 0, o, :], hid[:, 0, o, :],
                                          start=o == 0, stop=o == 1)
            for h in range(4):
                for o in range(2):
                    mm = nc.tensor.matmul(bank[6][0:15, h * HD:(h + 1) * HD], hid[:, 1, o, h * 15:(h + 1) * 15],
                                          w2[:, 1, o, :], start=o == 0, stop=o == 1)
            mm.then_inc(SC["kc"].sem, 1)

        def cmp_act(act):
            for n in range(2):
                act.wait_ge(*SC["hid"](n + 1))
                for o in range(2):
                    nc.scalar.activation(pec[:, n, o:o + 1], bank[6 + o][:, 60:61], ACT.Copy).then_inc(SC["pe"].sem, 1)
                    act.wait_ge(*SC["pe"](2 * n + o + 1))
                    nc.scalar.activation(hid[:, n, o, :], bank[6 + o][:, 0:60], ACT.Silu, bias=pec[:, n, o:o + 1])\
                        .then_inc(SC["h"].sem, 1)
            act.wait_ge(*SC["kc"](1))
            nc.scalar.activation(kcT, bank[4][:, 0:60], ACT.Copy)
            nc.scalar.activation(vcs, bank[6][0:15, 0:256], ACT.Copy).then_inc(SC["kcv"].sem, 1)
            act.wait_ge(*SC["g2"](1))
            nc.scalar.activation(gts, gts, ACT.Sigmoid).then_inc(SC["gate"].sem, 1)

        def cmp_dve(dve):
            dve.wait_ge(*SC["load"](112))
            dve.wait_ge(*SC["gl"](1))
            nc.vector.tensor_tensor(gts, bank[4][:, 0:96].rearrange("p (m g) -> p m g", m=2),
                                    glb.unsqueeze(1).broadcast_to([P, 2, 48]), ALU.add).then_inc(SC["g2"].sem, 1)
            dve.wait_ge(*SC["bias"](1))
            nc.vector.tensor_copy(cb, bank[5][:, 0:480].rearrange("p (m n h) -> p h m n", m=2, n=15))\
                .then_inc(SC["cbev"].sem, 1)

        stages.append(("compress", cmp_pe, cmp_act, cmp_dve, cmp_load))

        njobs = []
        for h in range(16):
            p, kv = h % 2, h // 4
            rows_ = slice(HD * p, HD * p + HD)
            dst = head_dst(h)
            for br in range(3):
                j = dict(parts=CAUSAL, width=SEQ, reader="logit", last=br == 2, gate=gts[:, :, 16 * ((br + 1) % 3) + h],
                         ev_wait=h - 1 if h >= 2 and br == 0 else None)
                if br < 2:
                    kk = ksw if kv % 2 == p else swp
                    j["scores"] = (lambda m, kk=kk, rows_=rows_, h=h, t=2 * br + kv // 2:
                                   [(qc[rows_, h // 2, m * P:(m + 1) * P], kk[rows_, t, :])])
                    j["buf"] = h % 2
                    if br == 0:
                        j["load"] = 24 + h
                    j["pv"] = causal_pv(dst, lambda kt, c=br * SEQ + kv * HD: vsw[:, kt, c:c + HD], br == 0, False)
                else:
                    j.update(width=15, tile=cb[:, h, :, :], parts=[(0, 0), (0, 1)], weights=cmk, floor=True)
                    j["scores"] = (lambda m, rows_=rows_, h=h, kv=kv:
                                   [(qc[rows_, h // 2, m * P:(m + 1) * P], kcT[rows_, kv * 15:(kv + 1) * 15])])

                    def pv(b, h=h, kv=kv):
                        yield nc.tensor.matmul(bank[7][HD * (h % 2):HD * (h % 2) + HD, 0:SEQ],
                                               vcs[:, kv * HD:(kv + 1) * HD], probT[0:15, b, 0:SEQ],
                                               start=False, stop=True, skip_group_check=True)
                    j["pv"] = pv
                njobs.append(j)
        dst_n = lambda h: onc[HD * (h % 2):HD * (h % 2) + HD, h // 2, :]
        jobs_head[id(dst_n)] = list(range(16))
        softmax_stage("att_n", njobs, HD ** -0.5, head_evac(dst_n), probT)
        product_stage("o_c", onc, gc)
        merge_stage("m_c", STREAM["m_c"], False)

        SM = shared("split", hi=4, lo=5)

        def splitm_act(act):
            for n in range(4):
                nc.scalar.activation(h_hi[:, 4 * n:4 * n + 4, :], merged[:, 4 * n:4 * n + 4, :], ACT.Copy)\
                    .then_inc(SM["hi"].sem, 1)

        def splitm_dve(dve):
            for n in range(4):
                dve.wait_ge(*SM["hi"](n + 1))
                nc.vector.tensor_tensor(h_lo[:, 4 * n:4 * n + 4, :], merged[:, 4 * n:4 * n + 4, :],
                                        h_hi[:, 4 * n:4 * n + 4, :].bitcast(F32), ALU.subtract)\
                    .then_inc(SM["lo"].sem, 1)
            nc.vector.tensor_scalar(x[:, :, :], x[:, :, :], 2.0 ** 0.25, None, ALU.mult).then_inc(SM["lo"].sem, 1)

        stages.append(("split_m", lambda pe: None, splitm_act, splitm_dve, None))
        residual_stage("out2", STREAM["out2"], x)

        SN = sems("ln", "sum mean cent square ssum root recip a b out")
        lsq, lmean, lsd = at(0, 4, SEQ), at(1024, SEQ), at(1280, SEQ)

        def ln_pe(pe):
            for t in range(NT):
                mm = nc.tensor.matmul(bank[4][:, 0:SEQ], ones, x[:, t, :], start=t == 0, stop=t == NT - 1)
            mm.then_inc(SN["sum"].sem, 1)
            for t in range(NT):
                pe.wait_ge(*SN["square"](t + 1))
                nc.tensor.matmul(bank[5][:, 0:SEQ], ones, lsq[:, t % 4, :], start=t == 0, stop=t == NT - 1)\
                    .then_inc(SN["ssum"].sem, 1)

        def ln_act(act):
            act.wait_ge(*SN["sum"](1))
            nc.scalar.activation(lmean, bank[4][:, 0:SEQ], ACT.Copy, scale=1.0 / DM).then_inc(SN["mean"].sem, 1)
            for t in range(NT):
                act.wait_ge(*SN["cent"](t + 1))
                if t >= 4:
                    act.wait_ge(*SN["ssum"](t - 3))
                nc.scalar.activation(lsq[:, t % 4, :], x[:, t, :], ACT.Square).then_inc(SN["square"].sem, 1)
            act.wait_ge(*SN["ssum"](NT))
            nc.scalar.activation(lsd, bank[5][:, 0:SEQ], ACT.Sqrt, bias=ln_eps_col, scale=1.0 / DM)\
                .then_inc(SN["root"].sem, 1)
            for t in range(NT):
                act.wait_ge(*SN["a"](t + 1))
                nc.scalar.activation(x[:, t, :], x[:, t, :], ACT.Identity, bias=vcol("ln_b", t)).then_inc(SN["b"].sem, 1)
                if t % 4 == 3:
                    act.wait_ge(*SN["b"](t + 1))
                    act.dma_start(out[:, t - 3:t + 1, :], x[:, t - 3:t + 1, :]).then_inc(SN["out"].sem, 16)
            act.wait_ge(*SN["out"](64))

        def ln_dve(dve):
            dve.wait_ge(*SN["mean"](1))
            for t in range(NT):
                nc.vector.tensor_tensor(x[:, t, :], x[:, t, :], lmean, ALU.subtract).then_inc(SN["cent"].sem, 1)
            dve.wait_ge(*SN["root"](1))
            nc.vector.reciprocal(lsd, lsd).then_inc(SN["recip"].sem, 1)
            dve.wait_ge(*SN["recip"](1))
            dve.wait_ge(*SN["cent"](NT))
            for t in range(NT):
                dve.wait_ge(*SN["square"](t + 1))
                nc.vector.scalar_tensor_tensor(x[:, t, :], x[:, t, :], vcol("ln_g", t), lsd, ALU.mult, ALU.mult)\
                    .then_inc(SN["a"].sem, 1)

        stages.append(("ln", ln_pe, ln_act, ln_dve, None))

        block = ctx.enter_context(nc.Block())

        def finish_stage(eng, n):
            eng.drain().then_inc(stage_done, 1)
            eng.wait_ge(stage_done, 3 * (n + 1))

        @block.sync
        def _(sp):
            for s in range(RING):
                sp.dma_start(raw[:, s, :], W[s]).then_inc(raw_ready[s], 16)
            with sp.Fori(1, UNITS // RING) as i:
                for s in range(RING):
                    sp.wait_ge(lo_ready, i * RING + (s - RING + 1))
                    sp.dma_start(raw[:, s, :], W[i * RING + s]).then_inc(raw_ready[s], 16)
            for s in range(RING):
                sp.wait_ge(raw_ready[s], 16 * (UNITS // RING))

        @block.gpsimd
        def _(pool):
            for n, s in enumerate(stages):
                if s[4]:
                    if n:
                        pool.wait_ge(stage_done, 3 * n)
                    s[4](pool)

        @block.scalar
        def _(act):
            for n, s in enumerate(stages):
                if s[0] == "norm1":
                    act.wait_ge(*S0["e"](2))
                    act.wait_ge(*S0["rows"](16 * 40))
                s[2](act)
                finish_stage(act, n)

        @block.vector
        def _(dve):
            for n, s in enumerate(stages):
                if s[0] == "norm1":
                    dve.wait_ge(*S0["rows"](16 * 40))
                if s[0] == "att_a":
                    dve.wait_ge(*SH["sinks"](16))
                s[3](dve)
                finish_stage(dve, n)

        @block.tensor
        def _(pe):
            for n, s in enumerate(stages):
                if s[0] == "att_a":
                    pe.wait_ge(*SH["swap"](32))
                if s[0] == "att_n":
                    pe.wait_ge(*SC["swap"](128))
                s[1](pe)
                finish_stage(pe, n)


def shape_constants():
    f = np.float32
    k, q = np.arange(P)[:, None], np.arange(P)[None, :]
    squares = np.stack([np.ones((P, P)), k // HD == q // HD, k == q, k >= q, q >= k], 1).astype(f)
    key, tok = np.arange(P)[:, None, None] + P * np.arange(2)[None, :, None], np.arange(SEQ)[None, None, :]
    before = key < tok
    dist = np.arange(P)[:, None, None] + P * np.arange(2)[None, :, None] - np.arange(SEQ)[None, None, :]

    def times(d):
        return np.where(d < 0, 0, (d <= P) * 1 + (d % 4 == 0) + (d % 16 == 0))

    masks = np.concatenate([before, np.where(before, 0, NEG), times(dist)], 1).astype(f)
    tok2 = np.arange(P)[:, None, None] + P * np.arange(2)[None, :, None]
    cmask = (tok2 - (16 * np.arange(15)[None, None, :] + 31) >= 0).astype(f)

    def bucket(d, most):
        d = np.maximum(d, 0)
        large = 16 + (np.log(np.maximum(d, 1).astype(f) / f(16)) / f(math.log(most / 16)) * f(16)).astype(np.int32)
        return np.where(d < 16, d, np.minimum(large, 31))

    def onehot(d, ok, most):
        t = np.zeros((33, TABW), f)
        t[np.where(ok, bucket(d, most), 32), np.arange(TABW)] = 1
        return t

    d = 255 - np.arange(TABW)
    up = np.arange(TABW) - SEQ
    onehots = np.stack([onehot(d, (d >= 0) & (d < P), 2048), onehot(d, times(d) > 0, 2048), onehot(d, d >= 0, 1024),
                        onehot(up, up >= 0, 1024)], 1)
    return squares, masks, cmask, onehots


def lay_out(i):
    a = {k: np.asarray(v) for k, v in i.items()}

    def units(w, rows_first=False):
        kk, n = w.shape
        v = w.reshape(kk // (UK * P), UK, P, n // UN, UN)
        return v.transpose((0, 3, 2, 1, 4) if rows_first else (3, 0, 2, 1, 4)).reshape(-1, P, UK * UN)

    w = a["w_in"][0]
    off = np.cumsum([0, 512, 128, 128, 512, 512, 512, 1024, 1024, 1024])
    aq, ak, av, bq, bk, bv, cq, ck, cv = (w[:, off[n]:off[n + 1]] for n in range(9))
    pad = np.zeros((DM, 256), np.float32)
    parts = [units(a["w_mem_kv_2"][0]),
             units(np.concatenate([aq, bq, bk, cq, ck, ak, av, pad, bv, cv], 1)),
             units(a["w_out"][0])]
    wu = a["w_up"][0]
    for c in range(11):
        parts += [units(wu[:, c * UN:(c + 1) * UN]), units(wu[:, NF * P + c * UN:NF * P + (c + 1) * UN])]
    parts.append(units(a["w_down"][0], True))
    w = a["w_in_2"][0]
    br = a["w_branch_2"][0]

    def merge(n):
        for c in range(4):
            g = 10800 + n * DM + c * UN
            yield units(w[:, g:g + UN])
            yield units(br[n][:, c * UN:(c + 1) * UN])

    parts += [units(np.concatenate([w[:, 0:1024], w[:, 2048:3072], w[:, 1024:2048]], 1)), *merge(0)]
    parts += [units(w[:, 3072:5120]), *merge(1)]
    parts += [units(w[:, 8752:10800]), *merge(3)]
    parts += [units(np.concatenate([w[:, 5120:6656], w[:, 6656:6912], w[:, 7168:7424], w[:, 7728:8752],
                                    w[:, 6912:7168], w[:, 7424:7680]], 1)), *merge(2)]
    parts.append(units(a["w_out_2"][0]))

    def cols(v):
        return v.reshape(-1, P).T

    def twice(v):
        return np.concatenate([v, v])[:, None]

    def pairs(v):
        return v.reshape(16, 2, HD, -1).transpose(1, 2, 0, 3).reshape(P, -1)

    vec = [cols(a["attn_norm"][0]), cols(a["ffn_norm"][0]), cols(a["mix_out_gain"][0]), twice(a["a_q_gain"][0]),
           twice(a["a_k_gain"][0]), twice(a["c_q_gain"][0]), twice(a["c_k_gain"][0]), cols(a["conv_w"][0]),
           cols(a["conv_b"][0]), cols(a["conv_w_2"][0]), cols(a["conv_b_2"][0]), cols(a["lru_ba_2"][0]),
           cols(a["lru_bx_2"][0]), cols(a["lru_lambda_2"][0]), cols(a["ln_g_2"][0]), cols(a["ln_b_2"][0]),
           pairs(a["cmp_pe_k_2"][0]), pairs(a["cmp_pe_v_2"][0])]
    squares, masks, cmask, onehots = shape_constants()
    tabs = np.concatenate([np.concatenate([a["rel_bias_table"], a["rel_bias_2"]], 1),
                           np.full((1, 40), NEG, np.float32)], 0)

    def tiles(v):
        return v.T.reshape(-1, P, SEQ).transpose(1, 0, 2)

    return {
        "W": np.concatenate(parts, 0), "xT": tiles(a["x"][0]), "memT": tiles(a["mem_2"][0]),
        "vecs": np.concatenate(vec, 1), "squares": squares, "masks": masks, "cmask": cmask, "onehots": onehots,
        "tabs": tabs, "sinks": a["a_sinks"], "ln_rows": np.concatenate([a["sgu_ln_g_2"], a["sgu_ln_b_2"]], 1),
        "sgu_wT": a["sgu_w_2"][0].transpose(2, 0, 1), "sgu_b": a["sgu_b_2"].reshape(1, -1),
        "lru_w": np.stack([a["lru_wa_2"][0], a["lru_wx_2"][0]], 0).transpose(2, 0, 1, 3),
        "gl_w": w[:, 7680:7728].reshape(NT, P, 48).transpose(1, 0, 2), "gl_b": a["nsa_gate_b_2"],
        "cmp_w1": np.stack([pairs(a["cmp_w1_k_2"][0].reshape(32, HD, 256)),
                            pairs(a["cmp_w1_v_2"][0].reshape(32, HD, 256))], 0),
        "cmp_w2k": a["cmp_w2_k_2"][0].reshape(2, P, HD).transpose(1, 0, 2),
        "cmp_w2v": a["cmp_w2_v_2"][0].reshape(2, P, HD).transpose(1, 0, 2),
    }


def kernel(**inputs):
    from concourse import bacc
    from concourse.bass_utils import run_bass_kernel_spmd

    nc = bacc.Bacc("TRN2", target_bir_lowering=False, num_devices=1)
    arrays = {k: np.ascontiguousarray(v) for k, v in lay_out(inputs).items()}
    args = [nc.dram_tensor(k, v.shape, mybir.dt.from_np(v.dtype), kind="ExternalInput").ap()
            for k, v in arrays.items()]
    out = nc.dram_tensor("out", (P, NT, SEQ), F32, kind="ExternalOutput").ap()
    two_blocks(nc, *args, out)
    r = run_bass_kernel_spmd(nc, [arrays], core_ids=[0])
    y = r.results[0]["out"]
    return np.ascontiguousarray(y.transpose(1, 0, 2).reshape(DM, SEQ).T)[None]
```

```python
import math
from contextlib import ExitStack
from itertools import islice

import numpy as np
import concourse.bass as bass
from concourse import mybir

F32 = mybir.dt.float32
F32R = mybir.dt.float32r
ACT = mybir.ActivationFunctionType
ALU = mybir.AluOpType
AX = mybir.AxisListType.X

P = 128
SEQ = 256
DM = 2048
NT = DM // P
HD = 64
NF = 44
UK, UN = 2, 512
RING = 4
LEAD = 3
NEG = -1.0e30
TABW = 512
EPS, LN_EPS = 1e-6, 1e-5

STREAM = {}
_at = 0
for _name, _chunks, _per in (("proj", 11, 8), ("mem", 4, 8), ("wout", 4, 8), ("up", 22, 8),
                             ("down", 22, 4), ("p_a", 6, 8), ("p_m", 4, 8), ("m_a", 4, 12), ("p_c", 7, 8),
                             ("m_m", 4, 12), ("p_b", 4, 8), ("m_c", 4, 12), ("m_b", 4, 12), ("out2", 4, 8)):
    STREAM[_name] = _at
    _at += _chunks * _per
UNITS = _at

VEC = {}
_at = 0
for _name, _n in (("attn_norm", 16), ("ffn_norm", 16), ("mix_gain", 16), ("aq", 1), ("ak", 1), ("cq", 1),
                  ("ck", 1), ("conv_w", 3 * 88), ("conv_b", 88), ("conv2_w", 32), ("conv2_b", 8),
                  ("lru_ba", 8), ("lru_bx", 8), ("lru_lam", 8), ("ln_g", 16), ("ln_b", 16),
                  ("cmp_pe_k", 16), ("cmp_pe_v", 16)):
    VEC[_name] = (_at, _n)
    _at += _n
NVEC = _at


class Signal:

    def __init__(self, sem, base):
        self.sem, self.base = sem, base

    def __call__(self, n):
        return self.sem, n + self.base




def two_blocks(nc, W, xT, memT, vecs, squares, masks, cmask, onehots, tabs, sinks, ln_rows, sgu_wT, sgu_b,
               lru_w, gl_w, gl_b, cmp_w1, cmp_w2k, cmp_w2v, out):
    ctx = ExitStack()
    with ctx:
        def sb(name, shape, dt=F32):
            return ctx.enter_context(nc.sbuf_tensor(name, shape, dt))

        def sem(name):
            return ctx.enter_context(nc.semaphore(name))

        raw = sb("raw", [P, RING, UK * UN])
        w_hi = sb("w_hi", [P, RING, UK * UN], F32R)
        w_lo = sb("w_lo", [P, RING, UK * UN], F32R)
        x = sb("x", [P, NT, SEQ])
        h_hi = sb("h_hi", [P, NT, SEQ], F32R)
        h_lo = sb("h_lo", [P, NT, SEQ], F32R)
        o_hi = sb("o_hi", [P, 8, SEQ], F32R)
        o_lo = sb("o_lo", [P, 8, SEQ], F32R)
        kmT = sb("kmT", [P, 8, SEQ])
        vm = sb("vm", [P, 2, 1024])
        vec = sb("vec", [P, NVEC])
        sq_c = sb("sq_c", [P, 5, P])
        ones, blocks, ident, tri, causal = (sq_c[:, n, :] for n in range(5))
        small = sb("small", [P, 160])
        AW = 18950
        arena = sb("arena", [P, AW])
        bank = [ctx.enter_context(nc.psum_tensor(f"bank{n}", [P, 512], F32)) for n in range(8)]

        def at(off, *shape, parts=(0, P)):
            n = int(np.prod(shape))
            assert off + n <= AW, (off, shape)
            v = arena[parts[0]:parts[1], off:off + n]
            if len(shape) == 2:
                v = v.rearrange("p (a b) -> p a b", a=shape[0])
            elif len(shape) == 3:
                v = v.rearrange("p (a b c) -> p a b c", a=shape[0], b=shape[1])
            return v

        def vcol(name, n=0):
            o, cnt = VEC[name]
            assert n < cnt
            return vec[:, o + n:o + n + 1]

        row_dram = nc.dram_tensor("row_dram", (40, TABW), F32, kind="Internal").ap()
        bias_dram = nc.dram_tensor("bias_dram", (40, P, TABW), F32, kind="Internal").ap()

        raw_ready = [sem(f"raw_ready{n}") for n in range(RING)]
        hi_ready, lo_ready, unit_done = sem("hi_ready"), sem("lo_ready"), sem("unit_done")
        stage_done = sem("stage_done")

        def split_hi(act, u, j):
            s = (j + LEAD) % RING
            v = u + LEAD
            act.wait_ge(raw_ready[s], (v - s) * (16 // RING) + 16)
            if not (isinstance(v, int) and v < RING):
                act.wait_ge(unit_done, v - RING + 1)
            nc.scalar.activation(w_hi[:, s, :], raw[:, s, :], ACT.Copy).then_inc(hi_ready, 1)

        def split_lo(dve, u, j):
            s = (j + LEAD) % RING
            v = u + LEAD
            dve.wait_ge(hi_ready, v + 1)
            if not (isinstance(v, int) and v < RING):
                dve.wait_ge(unit_done, v - RING + 1)
            nc.vector.tensor_tensor(w_lo[:, s, :], raw[:, s, :], w_hi[:, s, :].bitcast(F32),
                                    ALU.subtract).then_inc(lo_ready, 1)

        def unit_features(pe, u, j, hi, lo, kt, banks, first, last, tiles=4):
            s = j % RING
            pe.wait_ge(lo_ready, u + 1)
            for k in range(UK):
                for f in range(tiles):
                    o = banks[f // 2][:, (f % 2) * SEQ:(f % 2 + 1) * SEQ]
                    cols = slice(k * UN + f * P, k * UN + (f + 1) * P)
                    for n, (w, m) in enumerate(((w_hi, hi), (w_hi, lo), (w_lo, hi))):
                        mm = nc.tensor.matmul(o, w[:, s, cols], m[:, kt + k, :],
                                              start=first and k == 0 and n == 0 and f % 2 == 0,
                                              stop=last and k == UK - 1 and n == 2, skip_group_check=True)
            return mm

        def unit_tokens(pe, u, j, kt, banks, first, last, c0=0, cols=UN, wait=True):
            s = j % RING
            if wait:
                pe.wait_ge(lo_ready, u + 1)
            for k in range(UK):
                for m in range(2):
                    for n, (w, a) in enumerate(((w_hi, h_hi), (w_lo, h_hi), (w_hi, h_lo))):
                        mm = nc.tensor.matmul(banks[m][:, 0:cols], a[:, kt + k, m * P:(m + 1) * P],
                                              w[:, s, k * UN + c0:k * UN + c0 + cols],
                                              start=first and k == 0 and n == 0,
                                              stop=last and k == UK - 1 and n == 2, skip_group_check=True)
            return mm

        def chunk_steps_pe(pe, ev, u, c, q, kind, first_two, ready=None):
            if not first_two:
                pe.wait_ge(*ev[0](c - 1))
                pe.wait_ge(*ev[1](c - 1))
            banks = bank[2 * q:2 * q + 2]
            for j in range(8):
                if ready:
                    pe.wait_ge(*ready(j + 1))
                if kind == "F":
                    mm = unit_features(pe, u + j, j, h_hi, h_lo, 2 * j, banks, j == 0, j == 7)
                elif kind == "T":
                    mm = unit_tokens(pe, u + j, j, 2 * j, banks, j == 0, j == 7)
                elif kind == "M":
                    unit_features(pe, u + j, j, h_hi, h_lo, 2 * j, banks, j == 0, j == 7, tiles=1)
                    mm = unit_tokens(pe, u + j, j, 2 * j, (banks[1], bank[4]), j == 0, j == 7, P, P, wait=False)
                mm.then_inc(unit_done, 1)
                yield

        def chunk_pe(*args):
            run(chunk_steps_pe(*args))

        def steps_pe(pe, ev, u0, kinds, ready=None, c0=0):
            for c, kind in enumerate(kinds):
                yield from chunk_steps_pe(pe, ev, u0 + 8 * c, c0 + c, (c0 + c) % 2, kind, c0 + c < 2,
                                          ready if c == 0 else None)

        def steps_act(act, ev, u0, kinds, dst, c0=0):
            for c, kind in enumerate(kinds):
                for j in range(8):
                    split_hi(act, u0 + 8 * c + j, j)
                    if j == 7:
                        act.wait_ge(unit_done, u0 + 8 * c + 8)
                        src = bank[2 * ((c0 + c) % 2)][:, :]
                        nc.scalar.activation(dst(0, c), src.rearrange("p (a b) -> p a b", a=2) if kind == "F" else src,
                                             ACT.Copy).then_inc(ev[0].sem, 1)
                    yield

        def steps_dve(dve, ev, u0, kinds, dst, c0=0):
            for c, kind in enumerate(kinds):
                for j in range(8):
                    split_lo(dve, u0 + 8 * c + j, j)
                    if j == 7:
                        dve.wait_ge(unit_done, u0 + 8 * c + 8)
                        src = bank[2 * ((c0 + c) % 2) + 1][:, :]
                        nc.vector.tensor_copy(dst(1, c), src.rearrange("p (a b) -> p a b", a=2) if kind == "F" else src)\
                            .then_inc(ev[1].sem, 1)
                    yield

        def to_tiles(dst):
            return lambda half, c: dst[:, 4 * c + 2 * half:4 * c + 2 * half + 2, :]

        def chunk_split(eng, split, u):
            for j in range(8):
                split(eng, u + j, j)

        def F_act(act, ev, u, q, dst):
            act.wait_ge(unit_done, u + 8)
            nc.scalar.activation(dst, bank[2 * q][:, :].rearrange("p (a b) -> p a b", a=2),
                                 ACT.Copy).then_inc(ev[0].sem, 1)

        def F_dve(dve, ev, u, q, dst):
            dve.wait_ge(unit_done, u + 8)
            nc.vector.tensor_copy(dst, bank[2 * q + 1][:, :].rearrange("p (a b) -> p a b", a=2))\
                .then_inc(ev[1].sem, 1)

        def features_pe(pe, ev, u0, chunks, ready=None):
            chunk_pe(pe, ev, u0, 0, 0, "F", True, ready)
            chunk_pe(pe, ev, u0 + 8, 1, 1, "F", True)
            if chunks >= 4:
                with pe.Fori(1, chunks // 2) as i:
                    for q in range(2):
                        chunk_pe(pe, ev, i * 16 + (u0 + 8 * q), i * 2 + q, q, "F", False)
            if chunks % 2:
                chunk_pe(pe, ev, u0 + 8 * (chunks - 1), chunks - 1, 0, "F", False)

        def features_act(act, ev, u0, chunks, dst, t0=0):
            for q in range(2):
                chunk_split(act, split_hi, u0 + 8 * q)
                F_act(act, ev, u0 + 8 * q, q, dst[:, t0 + 4 * q:t0 + 4 * q + 2, :])
            if chunks >= 4:
                with act.Fori(1, chunks // 2) as i:
                    for q in range(2):
                        chunk_split(act, split_hi, i * 16 + (u0 + 8 * q))
                        F_act(act, ev, i * 16 + (u0 + 8 * q), q, dst[:, bass.ds(i * 8 + (t0 + 4 * q), 2), :])
            if chunks % 2:
                u, t = u0 + 8 * (chunks - 1), t0 + 4 * (chunks - 1)
                chunk_split(act, split_hi, u)
                F_act(act, ev, u, 0, dst[:, t:t + 2, :])

        def features_dve(dve, ev, u0, chunks, dst, t0=0):
            for q in range(2):
                chunk_split(dve, split_lo, u0 + 8 * q)
                F_dve(dve, ev, u0 + 8 * q, q, dst[:, t0 + 4 * q + 2:t0 + 4 * q + 4, :])
            if chunks >= 4:
                with dve.Fori(1, chunks // 2) as i:
                    for q in range(2):
                        chunk_split(dve, split_lo, i * 16 + (u0 + 8 * q))
                        F_dve(dve, ev, i * 16 + (u0 + 8 * q), q, dst[:, bass.ds(i * 8 + (t0 + 4 * q + 2), 2), :])
            if chunks % 2:
                u, t = u0 + 8 * (chunks - 1), t0 + 4 * (chunks - 1) + 2
                chunk_split(dve, split_lo, u)
                F_dve(dve, ev, u, 0, dst[:, t:t + 2, :])

        def tokens_pe(pe, ev, u0, c0, chunks):
            for c in range(chunks):
                chunk_pe(pe, ev, u0 + 8 * c, c0 + c, (c0 + c) % 2, "T", c0 + c < 2)

        def tokens_act(act, ev, u0, c0, chunks, dst):
            for c in range(chunks):
                chunk_split(act, split_hi, u0 + 8 * c)
                act.wait_ge(unit_done, u0 + 8 * c + 8)
                nc.scalar.activation(dst(0, c), bank[2 * ((c0 + c) % 2)][:, :], ACT.Copy).then_inc(ev[0].sem, 1)

        def tokens_dve(dve, ev, u0, c0, chunks, dst):
            for c in range(chunks):
                chunk_split(dve, split_lo, u0 + 8 * c)
                dve.wait_ge(unit_done, u0 + 8 * c + 8)
                nc.vector.tensor_copy(dst(1, c), bank[2 * ((c0 + c) % 2) + 1][:, :]).then_inc(ev[1].sem, 1)

        pool_of_signals = {}

        def sems(stage, names):
            return {n: Signal(sem(f"{stage}_{n}"), 0) for n in names.split()}

        def shared(kind, **totals):
            got = {}
            for n, total in totals.items():
                if (kind, n) not in pool_of_signals:
                    pool_of_signals[kind, n] = [sem(f"{kind}_{n}"), 0]
                s, before = pool_of_signals[kind, n]
                got[n] = Signal(s, before)
                pool_of_signals[kind, n][1] = before + total
            return got

        def halves(chunks):
            S = shared("read", by_act=chunks, by_dve=chunks)
            return S["by_act"], S["by_dve"]

        def rms_pe(pe, S, tiles, sq, groups):
            done = 0
            for g, (a, n) in enumerate(groups):
                if g >= 2:
                    pe.wait_ge(*S["root"](g - 1))
                for t in range(a, a + n):
                    pe.wait_ge(*S["square"](done + 1))
                    mm = nc.tensor.matmul(bank[4 + g % 2][:, 0:SEQ], ones, sq[:, done % 4, :],
                                          start=t == a, stop=t == a + n - 1)
                    mm.then_inc(S["sum"].sem, 1)
                    done += 1

        def rms_act(act, S, src, sq, sd, groups, arrived=None, between=None):
            done = 0
            for g, (a, n) in enumerate(groups):
                for t in range(a, a + n):
                    if arrived:
                        arrived(act, t)
                    if done >= 4:
                        act.wait_ge(*S["sum"](done - 3))
                    nc.scalar.activation(sq[:, done % 4, :], src[:, t, :], ACT.Square).then_inc(S["square"].sem, 1)
                    done += 1
                if between:
                    between(act)
                act.wait_ge(*S["sum"](done))
                nc.scalar.activation(sd[:, g, :], bank[4 + g % 2][:, 0:SEQ], ACT.Sqrt, bias=eps_col,
                                     scale=1.0 / (n * P)).then_inc(S["root"].sem, 1)

        def rms_dve(dve, S, src, sd, tmp, gain, groups, put_lo):
            done = 0
            for g, (a, n) in enumerate(groups):
                dve.wait_ge(*S["root"](g + 1))
                nc.vector.reciprocal(sd[:, g, :], sd[:, g, :]).then_inc(S["recip"].sem, 1)
                dve.wait_ge(*S["recip"](g + 1))
                for t in range(a, a + n):
                    nc.vector.scalar_tensor_tensor(tmp[:, t, :], src[:, t, :], vcol(gain, t), sd[:, g, :],
                                                   ALU.mult, ALU.mult).then_inc(S["scaled"].sem, 1)
                    done += 1
                    if done % 2 == 0 and done >= 4:
                        put_lo(done // 2 - 2)
            put_lo(done // 2 - 1)

        def to_moving_act(act, S, tmp, hi, pairs):
            for p in range(pairs):
                act.wait_ge(*S["scaled"](2 * p + 2))
                nc.scalar.activation(hi[:, 2 * p:2 * p + 2, :], tmp[:, 2 * p:2 * p + 2, :], ACT.Copy)\
                    .then_inc(S["hi"].sem, 1)

        def to_moving_dve(dve, S, tmp, hi, lo):
            def put(p):
                dve.wait_ge(*S["hi"](p + 1))
                nc.vector.tensor_tensor(lo[:, 2 * p:2 * p + 2, :], tmp[:, 2 * p:2 * p + 2, :],
                                        hi[:, 2 * p:2 * p + 2, :].bitcast(F32), ALU.subtract)\
                    .then_inc(S["lo"].sem, 1)
            return put

        eps_col, ln_eps_col = small[:, 150:151], small[:, 151:152]

        def weave(main, n_main, side, n_side, start=0):
            done = 0
            for k, _ in enumerate(main):
                while done < n_side and done * (n_main - start) < (k + 1 - start) * n_side:
                    next(side)
                    done += 1
            for _ in side:
                done += 1
            assert done == n_side, (done, n_side)

        def run(steps):
            for _ in steps:
                pass

        def then(*parts):
            for p in parts:
                yield from p
        stages = []

        S0 = sems("start", "e x0 x1 x2 x3 c t m r_pe r_act table rows hi lo")
        oh = at(11008, 3, TABW, parts=(0, 33))
        tb = at(12544, 40, parts=(0, 33))
        rows = [at(12608 + 512 * n, TABW, parts=(0, r)) for n, r in enumerate((8, 16, 16))]
        tab_cols = ((0, 8), (8, 24), (24, 40))
        vm_tiles = vm[:, :, :].rearrange("p a b -> p (a b)").rearrange("p (a b) -> p a b", a=8)

        def start_load(pool):
            pool.dma_start(sq_c[:, :, :], squares).then_inc(S0["c"].sem, 16)
            pool.dma_start(vec[:, :], vecs).then_inc(S0["c"].sem, 16)
            pool.dma_start(oh, onehots[:, 0:3, :]).then_inc(S0["t"].sem, 16)
            pool.dma_start(tb, tabs).then_inc(S0["t"].sem, 16)
            pool.dma_start(kmT[:, :, :], memT[:, 0:8, :]).then_inc(S0["m"].sem, 16)
            pool.dma_start(vm_tiles, memT[:, 8:16, :]).then_inc(S0["m"].sem, 16)
            pool.wait_ge(*S0["r_act"](3))
            for n, (a, b) in enumerate(tab_cols):
                pool.dma_start(row_dram[a:b], rows[n]).then_inc(S0["table"].sem, 16)
            pool.wait_ge(*S0["table"](48))
            for h in range(40):
                pool.dma_start(bias_dram[h], row_dram[h:h + 1].broadcast_to([P, TABW]))\
                    .then_inc(S0["rows"].sem, 16)
            pool.wait_ge(*S0["rows"](16 * 40))

        def start_pe(pe):
            pe.wait_ge(*S0["c"](32))

        def start_act(act):
            act.wait_ge(*S0["e"](2))

        def x_arrived(act, t):
            if t % 4 == 0:
                act.wait_ge(*S0[f"x{t // 4}"](16))

        def first_split_act(act):
            for u in range(LEAD):
                act.wait_ge(raw_ready[u], 16)
                nc.scalar.activation(w_hi[:, u, :], raw[:, u, :], ACT.Copy).then_inc(hi_ready, 1)

        def start_dve(dve):
            nc.vector.memset(eps_col, EPS).then_inc(S0["e"].sem, 1)
            nc.vector.memset(ln_eps_col, LN_EPS).then_inc(S0["e"].sem, 1)
            for u in range(LEAD):
                dve.wait_ge(hi_ready, u + 1)
                nc.vector.tensor_tensor(w_lo[:, u, :], raw[:, u, :], w_hi[:, u, :].bitcast(F32),
                                        ALU.subtract).then_inc(lo_ready, 1)
            dve.wait_ge(*S0["c"](32))

        def rows_pe(pe):
            pe.wait_ge(*S0["t"](32))
            for n, (a, b) in enumerate(tab_cols):
                nc.tensor.matmul(bank[5 + n][0:b - a, :], tb[:, a:b], oh[:, n, :], start=True, stop=True)\
                    .then_inc(S0["r_pe"].sem, 1)

        def rows_act(act):
            for n, (a, b) in enumerate(tab_cols):
                act.wait_ge(*S0["r_pe"](n + 1))
                nc.scalar.activation(rows[n], bank[5 + n][0:b - a, :], ACT.Copy).then_inc(S0["r_act"].sem, 1)

        def norm_parts(src, gain, groups, tmp, sq, sd, arrived=None, between=None):
            G = len(groups)
            S = shared("norm", square=NT, sum=NT, root=G, recip=G, scaled=NT, hi=NT // 2, lo=NT // 2)

            def pe_(pe):
                rms_pe(pe, S, None, sq, groups)

            def act_(act):
                rms_act(act, S, src, sq, sd, groups, arrived, between)
                to_moving_act(act, S, tmp, h_hi, NT // 2)

            def dve_(dve):
                rms_dve(dve, S, src, sd, tmp, gain, groups, to_moving_dve(dve, S, tmp, h_hi, h_lo))

            return pe_, act_, dve_, S["lo"]

        norm1 = norm_parts(x, "attn_norm", [(0, NT)], at(0, NT, SEQ), at(4096, 4, SEQ), at(5120, 3, SEQ),
                           x_arrived, first_split_act)

        qk = at(0, 30, SEQ)
        v1 = at(7680, 2, 1664)
        oT = at(11008, NT, SEQ)
        WK = 15104
        CW3 = 3 * P
        rings = at(WK, 4, CW3), at(WK + 4 * CW3, 2, CW3)
        bias_ac = [at(WK + (6 + n) * CW3, CW3) for n in range(2)]
        count = at(WK + 8 * CW3, CW3)
        ev_proj = halves(11)
        UP = STREAM["proj"]

        def v_dst(half, c):
            return v1[:, half, P + c * UN:P + (c + 1) * UN]

        def proj_pe(pe):
            start_pe(pe)
            norm1[0](pe)
            rows_pe(pe)
            features_pe(pe, ev_proj, UP, 7, norm1[3])
            chunk_pe(pe, ev_proj, UP + 56, 7, 1, "M", False)
            weave(steps_pe(pe, ev_proj, UP + 64, "TTT", None, 8), 24, head_pe(pe), NP + 2)

        def proj_act(act):
            start_act(act)
            norm1[1](act)
            rows_act(act)
            features_act(act, ev_proj, UP, 7, qk)
            chunk_split(act, split_hi, UP + 56)
            act.wait_ge(unit_done, UP + 64)
            nc.scalar.activation(qk[:, 28, :], bank[2][:, 0:SEQ], ACT.Copy).then_inc(ev_proj[0].sem, 1)
            act.wait_ge(*ev_proj[1](8))
            weave(steps_act(act, ev_proj, UP + 64, "TTT", v_dst, 8), 24, head_act(act), NP + 2)

        def proj_dve(dve):
            start_dve(dve)
            norm1[2](dve)
            features_dve(dve, ev_proj, UP, 7, qk)
            chunk_split(dve, split_lo, UP + 56)
            dve.wait_ge(unit_done, UP + 64)
            nc.vector.tensor_copy(v1[:, 1, 0:P], bank[4][:, 0:P])
            nc.vector.tensor_copy(v1[:, 0, 0:P], bank[3][:, 0:P]).then_inc(ev_proj[1].sem, 1)
            dve.wait_ge(*ev_proj[0](8))
            weave(steps_dve(dve, ev_proj, UP + 64, "TTT", v_dst, 8), 24, head_dve(dve), NP + 2)


        ev_mem = halves(4)
        UM = STREAM["mem"]
        mem = {}
        MEM_UNITS = 20, 12

        def mem_dst(half, c):
            return to_tiles(kmT)(half, c) if c < 2 else vm[:, half, (c - 2) * UN:(c - 1) * UN]

        def mem_pe(pe):
            mem["pe"] = steps_pe(pe, ev_mem, UM, "FFTT", lambda n: S0["lo"]((n + 1) // 2))

        def mem_act(act):
            act.wait_ge(*S0["m"](32))
            for n in range(4):
                src = kmT[:, 4 * n:4 * n + 4, :] if n < 2 else vm_tiles[:, 4 * n - 8:4 * n - 4, :]
                nc.scalar.activation(h_hi[:, 4 * n:4 * n + 4, :], src, ACT.Copy).then_inc(S0["hi"].sem, 1)
            mem["act"] = steps_act(act, ev_mem, UM, "FFTT", mem_dst)

        def mem_dve(dve):
            for n in range(4):
                src = kmT[:, 4 * n:4 * n + 4, :] if n < 2 else vm_tiles[:, 4 * n - 8:4 * n - 4, :]
                dve.wait_ge(*S0["hi"](n + 1))
                nc.vector.tensor_tensor(h_lo[:, 4 * n:4 * n + 4, :], src, h_hi[:, 4 * n:4 * n + 4, :].bitcast(F32),
                                        ALU.subtract).then_inc(S0["lo"].sem, 1)
            mem["dve"] = steps_dve(dve, ev_mem, UM, "FFTT", mem_dst)

        def beside(main, n_main, side, n_side):
            weave(islice(main, n_main), n_main, side, n_side)

        SH = sems("headnorm", "square sum root recip scaled swap sinks")
        pairs = [(0, 2, "aq"), (2, 2, "aq"), (28, 1, "ak")] + [(t, 2, "cq") for t in range(12, 20, 2)] \
            + [(t, 2, "ck") for t in range(20, 28, 2)]
        hsq, hsd = at(WK, 2, 2, SEQ), at(WK + 1024, 2, 2, SEQ)
        sink_col = small[:, 0:8]

        def proj_load(pool):
            start_load(pool)
            pool.dma_start(sink_col, sinks.broadcast_to([P, 8])).then_inc(SH["sinks"].sem, 16)
            pool.wait_ge(*SH["scaled"](5))
            pool.dma_start(qk[HD:P, 29, :], qk[0:HD, 28, :]).then_inc(SH["swap"].sem, 16)
            pool.dma_start(qk[0:HD, 29, :], qk[HD:P, 28, :]).then_inc(SH["swap"].sem, 16)

        NP = len(pairs)

        def head_pe(pe):
            for n in range(NP + 2):
                if n < NP:
                    k = pairs[n][1]
                    pe.wait_ge(*SH["square"](n + 1))
                    if n >= 2:
                        pe.wait_ge(*SH["root"](n - 1))
                    nc.tensor.matmul(bank[4 + n % 2][:, 0:k * SEQ], blocks,
                                     hsq[:, n % 2, 0:k, :].rearrange("p a b -> p (a b)"), start=True, stop=True)\
                        .then_inc(SH["sum"].sem, 1)
                yield

        def head_act(act):
            for n in range(NP + 2):
                if n < NP:
                    t, k, _ = pairs[n]
                    if n >= 2:
                        act.wait_ge(*SH["sum"](n - 1))
                    nc.scalar.activation(hsq[:, n % 2, 0:k, :], qk[:, t:t + k, :], ACT.Square)\
                        .then_inc(SH["square"].sem, 1)
                if 1 <= n <= NP:
                    k = pairs[n - 1][1]
                    act.wait_ge(*SH["sum"](n))
                    if n >= 3:
                        act.wait_ge(*SH["scaled"](sum(p[1] for p in pairs[:n - 2])))
                    nc.scalar.activation(hsd[:, (n - 1) % 2, 0:k, :],
                                         bank[4 + (n - 1) % 2][:, 0:k * SEQ].rearrange("p (a b) -> p a b", a=k),
                                         ACT.Sqrt, bias=eps_col, scale=1.0 / HD).then_inc(SH["root"].sem, 1)
                yield

        def head_dve(dve):
            for step in range(NP + 2):
                n = step - 2
                if n >= 0:
                    t, k, gain = pairs[n]
                    dve.wait_ge(*SH["root"](n + 1))
                    nc.vector.reciprocal(hsd[:, n % 2, 0:k, :], hsd[:, n % 2, 0:k, :]).then_inc(SH["recip"].sem, 1)
                    dve.wait_ge(*SH["recip"](n + 1))
                    for j in range(k):
                        nc.vector.scalar_tensor_tensor(qk[:, t + j, :], qk[:, t + j, :], vcol(gain),
                                                       hsd[:, n % 2, j, :], ALU.mult, ALU.mult)\
                            .then_inc(SH["scaled"].sem, 1)
                yield

        stages.append(("proj", proj_pe, proj_act, proj_dve, proj_load))

        sinks_signal, tiles_signal = Signal(sem("sinks_negated"), 0), Signal(sem("stage_tiles"), 0)

        def softmax(jobs, scale, evac, rings, bias=None, load_extra=None):
            J = len(jobs)
            lp, pt = rings
            loads = sum(j.get("load") is not None for j in jobs)
            S = shared("softmax", score=J, logit=J, peak=J, neg=J, prob=J,
                       weight=sum(j.get("weights") is not None for j in jobs),
                       sum=sum(bool(j.get("floor")) + (j.get("sink") is not None) for j in jobs),
                       recip=J, norm=J, transposed=J, probT=J, out=J, evac=sum(j["last"] for j in jobs),
                       bias0=32 * ((loads + 1) // 2), bias1=32 * (loads // 2))
            nb = heads = weights = sums = 0
            for n, j in enumerate(jobs):
                nb += j.get("load") is not None
                j["bias_n"] = nb
                j["heads"] = heads
                heads += j["last"]
                j["weight_n"] = weights = weights + (j.get("weights") is not None)
                j["sum_n"] = sums
                sums += bool(j.get("floor")) + (j.get("sink") is not None)
            mx, ng, sm, rc, es, wsm = (small[:, 8 + 8 * k:16 + 8 * k].rearrange("p (a b) -> p a b", a=4)
                                       for k in range(6))
            nsink = small[:, 56:64]

            def load(pool):
                if load_extra:
                    load_extra(pool, tiles_signal)
                for n, j in enumerate(jobs):
                    if j.get("load") is None:
                        continue
                    b = (j["bias_n"] - 1) % 2
                    users = [m for m, o in enumerate(jobs) if o.get("buf") is not None
                             and o["bias_n"] == j["bias_n"] - 2]
                    if users:
                        pool.wait_ge(*S["logit"](users[-1] + 1))
                    g = bias_dram[j["load"]].rearrange("a b -> (a b)")
                    for m in range(2):
                        pool.dma_start(bias[b][:, m * P:P + 2 * m * P], bass.AP(
                            tensor=g.tensor, offset=g.offset + 255 - P * m, ap=[[TABW - 1, P], [1, P + P * m]]))\
                            .then_inc(S[f"bias{b}"].sem, 16)

            def pe_(pe):
                for slot in range(J + 8):
                    n = slot
                    if 0 <= n < J:
                        if n >= 2:
                            pe.wait_ge(*S["logit"](n - 1))
                        for m, (c, w) in enumerate(jobs[n]["segs"]):
                            ops = jobs[n]["scores"](m)
                            for i, (q, k) in enumerate(ops):
                                mm = nc.tensor.matmul(bank[4 + n % 2][:, c:c + w], q, k, start=i == 0,
                                                      stop=i == len(ops) - 1)
                        mm.then_inc(S["score"].sem, 1)
                    n = slot - 6
                    if 0 <= n < J:
                        j = jobs[n]
                        pe.wait_ge(*S["probT"](n + 1))
                        if j["heads"] >= j["out_regions"]:
                            pe.wait_ge(*S["evac"](j["heads"] - j["out_regions"] + 1))
                        for mm in j["pv"](pt[:, n % 2, :]):
                            pass
                        mm.then_inc(S["out"].sem, 1)
                    n = slot - 4
                    if 0 <= n < J:
                        pe.wait_ge(*S["norm"](n + 1))
                        if n >= 1:
                            pe.wait_ge(*S["probT"](n))
                        for t, (c, kw) in enumerate(jobs[n]["parts"]):
                            mm = nc.tensor.transpose(bank[6][0:kw, t * P:(t + 1) * P], lp[:, n % 4, c:c + kw], ident)
                        mm.then_inc(S["transposed"].sem, 1)
                    yield

            def act_(act):
                for slot in range(J + 8):
                    n = slot - 5
                    if 0 <= n < J:
                        j = jobs[n]
                        kw, cnt = j["parts"][0][1], len(j["parts"])
                        act.wait_ge(*S["transposed"](n + 1))
                        if n >= 2:
                            act.wait_ge(*S["out"](n - 1))
                        nc.scalar.activation(pt[0:kw, n % 2, 0:cnt * P], bank[6][0:kw, 0:cnt * P], ACT.Copy)\
                            .then_inc(S["probT"].sem, 1)
                    n = slot - 2
                    if 0 <= n < J:
                        j = jobs[n]
                        act.wait_ge(*S["neg"](n + 1))
                        for m, (c, w) in enumerate(j["segs"]):
                            i = nc.scalar.activation(lp[:, n % 4, c:c + w], lp[:, n % 4, c:c + w], ACT.Exp,
                                                     bias=ng[:, n % 4, m:m + 1], accum_out=sm[:, n % 4, m:m + 1])
                        if j.get("sink") is not None:
                            i = nc.scalar.activation(es[:, n % 4, :], ng[:, n % 4, :], ACT.Exp,
                                                     bias=sink_col[:, j["sink"]:j["sink"] + 1])
                        i.then_inc(S["prob"].sem, 1)
                    yield

            def dve_(dve):
                if jobs[0].get("sink") is not None:
                    nc.vector.tensor_scalar(nsink, sink_col, -1.0, None, ALU.mult).then_inc(sinks_signal.sem, 1)
                    dve.wait_ge(*sinks_signal(1))
                if load_extra:
                    dve.wait_ge(*tiles_signal(16))
                for slot in range(J + 8):
                    n = slot - 7
                    if 0 <= n < J and jobs[n]["last"]:
                        dve.wait_ge(*S["out"](n + 1))
                        evac(jobs[n]["heads"]).then_inc(S["evac"].sem, 1)
                    n = slot - 1
                    if 0 <= n < J:
                        j = jobs[n]
                        segs = j["segs"]
                        w = segs[1][0] + segs[1][1]
                        dve.wait_ge(*S["score"](n + 1))
                        if n >= 4:
                            dve.wait_ge(*S["transposed"](n - 3))
                        lg = lp[:, n % 4, 0:w]
                        if j.get("buf") is not None or j.get("tile") is not None:
                            if j.get("buf") is not None:
                                dve.wait_ge(*S[f"bias{j['buf']}"](32 * ((j["bias_n"] + 1) // 2)))
                            b = bias[j["buf"]] if j.get("buf") is not None else j["tile"]
                            i = nc.vector.scalar_tensor_tensor(lg, bank[4 + n % 2][:, 0:w], scale, b, ALU.mult, ALU.add)
                        else:
                            i = nc.vector.tensor_scalar(lg, bank[4 + n % 2][:, 0:w], scale, None, ALU.mult)
                        i.then_inc(S["logit"].sem, 1)
                        dve.wait_ge(*S["logit"](n + 1))
                        if segs[0][1] == segs[1][1]:
                            i = nc.vector.tensor_reduce(mx[:, n % 4, :], lg.rearrange("p (a b) -> p a b", a=2), AX, ALU.max)
                        else:
                            for m, (c, w) in enumerate(segs):
                                i = nc.vector.tensor_reduce(mx[:, n % 4, m:m + 1], lp[:, n % 4, c:c + w], AX, ALU.max)
                        i.then_inc(S["peak"].sem, 1)
                        dve.wait_ge(*S["peak"](n + 1))
                        if j.get("sink") is not None:
                            i = nc.vector.tensor_scalar(ng[:, n % 4, :], mx[:, n % 4, :], -1.0,
                                                        nsink[:, j["sink"]:j["sink"] + 1], ALU.mult, ALU.min)
                        else:
                            i = nc.vector.tensor_scalar(ng[:, n % 4, :], mx[:, n % 4, :], -1.0, None, ALU.mult)
                        i.then_inc(S["neg"].sem, 1)
                    n = slot - 3
                    if 0 <= n < J:
                        j = jobs[n]
                        dve.wait_ge(*S["prob"](n + 1))
                        s, added = sm[:, n % 4, :], j["sum_n"]
                        if j.get("weights") is not None:
                            for m, (c, w) in enumerate(j["segs"]):
                                i = nc.vector.scalar_tensor_tensor(lp[:, n % 4, c:c + w], lp[:, n % 4, c:c + w], 1.0,
                                                                   j["weights"][:, c:c + w], ALU.mult, ALU.mult,
                                                                   accum_out=wsm[:, n % 4, m:m + 1])
                            i.then_inc(S["weight"].sem, 1)
                            dve.wait_ge(*S["weight"](j["weight_n"]))
                            s = wsm[:, n % 4, :]
                        if j.get("floor"):
                            nc.vector.tensor_scalar(s, s, 1e-30, None, ALU.max).then_inc(S["sum"].sem, 1)
                            added += 1
                            dve.wait_ge(*S["sum"](added))
                        if j.get("sink") is not None:
                            nc.vector.tensor_tensor(s, s, es[:, n % 4, :], ALU.add).then_inc(S["sum"].sem, 1)
                            added += 1
                            dve.wait_ge(*S["sum"](added))
                        nc.vector.reciprocal(rc[:, n % 4, :], s).then_inc(S["recip"].sem, 1)
                        dve.wait_ge(*S["recip"](n + 1))
                        gate = j.get("gate")
                        for m, (c, w) in enumerate(j["segs"]):
                            i = nc.vector.tensor_scalar(lp[:, n % 4, c:c + w], lp[:, n % 4, c:c + w],
                                                        rc[:, n % 4, m:m + 1],
                                                        gate[:, m:m + 1] if gate is not None else None, ALU.mult,
                                                        ALU.mult if gate is not None else ALU.bypass)
                        i.then_inc(S["norm"].sem, 1)
                    yield

            return pe_, act_, dve_, load, J + 8

        CAUSAL = dict(segs=[(0, P), (P, SEQ)], parts=[(0, P), (P, P), (2 * P, P)])

        def causal_pv(dst, val, start, stop):
            def go(pt):
                yield nc.tensor.matmul(dst(0), val(0), pt[:, 0:P], start=start, stop=stop, skip_group_check=True)
                yield nc.tensor.matmul(dst(1), val(0), pt[:, P:2 * P], start=False, stop=False, skip_group_check=True)
                yield nc.tensor.matmul(dst(1), val(1), pt[:, 2 * P:3 * P], start=False, stop=stop,
                                       skip_group_check=True)
            return go

        def head_dst(h):
            return lambda m: bank[7][HD * (h % 2):HD * (h % 2) + HD, m * P:(m + 1) * P]

        def head_evac(dst):
            return lambda h: nc.vector.tensor_copy(dst(h), bank[7][HD * (h % 2):HD * (h % 2) + HD, 0:SEQ])

        def a_job(h):
            p, kv = h % 2, h // 4
            rows_ = slice(HD * p, HD * p + HD)
            return dict(scores=lambda m: [(qk[rows_, h // 2, m * P:(m + 1) * P],
                                           qk[rows_, 28 if kv % 2 == p else 29, 0:P + m * P])],
                        load=h, buf=h % 2, sink=h, last=True, out_regions=2, **CAUSAL,
                        pv=causal_pv(head_dst(h), lambda kt: v1[:, kt, kv * HD:(kv + 1) * HD], True, True))

        def count_load(pool, signal):
            pool.dma_start(count, masks[:, 2 * CW3:3 * CW3]).then_inc(signal.sem, 16)

        def c_job(h):
            rows_ = slice(HD * (h % 2), HD * (h % 2) + HD)
            return dict(scores=lambda m: [(qk[rows_, 12 + h // 2, m * P:(m + 1) * P],
                                           qk[rows_, 20 + h // 2, 0:P + m * P])],
                        load=8 + h, buf=h % 2, weights=count, last=True, out_regions=2, **CAUSAL,
                        pv=causal_pv(head_dst(h), lambda kt: v1[:, kt, 640 + h * HD:640 + (h + 1) * HD], True, True))

        def dst_ac(h):
            return oT[HD * (h % 2):HD * (h % 2) + HD, h // 2 if h < 8 else 4 + h // 2, :]

        att_ac = softmax([a_job(h) for h in range(8)] + [c_job(h) for h in range(16)], HD ** -0.5,
                         head_evac(dst_ac), rings, bias_ac, count_load)
        def att_ac_pe(pe):
            mem_pe(pe)
            beside(mem["pe"], MEM_UNITS[0], att_ac[0](pe), att_ac[4])

        def att_ac_act(act):
            mem_act(act)
            beside(mem["act"], MEM_UNITS[0], att_ac[1](act), att_ac[4])

        def att_ac_dve(dve):
            mem_dve(dve)
            beside(mem["dve"], MEM_UNITS[0], att_ac[2](dve), att_ac[4])

        stages.append(("att_ac", att_ac_pe, att_ac_act, att_ac_dve, att_ac[3]))

        SB = sems("att_b", "masks score zs zm small log soft masked arg suffix arg2 w out evac")
        m01, mneg = at(WK, CW3), at(WK + CW3, CW3)
        spr = at(WK + 2 * CW3, 4, CW3)
        zr = at(12 * SEQ, 7, CW3)
        BH = 8

        def b_load(pool):
            pool.dma_start(m01, masks[:, 0:CW3]).then_inc(SB["masks"].sem, 16)
            pool.dma_start(mneg, masks[:, CW3:2 * CW3]).then_inc(SB["masks"].sem, 16)

        def b_pe(pe):
            for slot in range(BH + 9):
                h = slot
                if 0 <= h < BH:
                    rows_ = slice(HD * (h % 2), HD * (h % 2) + HD)
                    if h >= 2:
                        pe.wait_ge(*SB["zs"](h - 1))
                    for kt in range(2):
                        mm = nc.tensor.matmul(bank[4 + h % 2][:, kt * SEQ:SEQ + kt * P],
                                              qk[rows_, 8 + h // 2, kt * P:(kt + 1) * P],
                                              qk[rows_, 4 + h // 2, kt * P:SEQ], start=True, stop=True)
                    mm.then_inc(SB["score"].sem, 1)
                h = slot - 7
                if 0 <= h < BH:
                    pe.wait_ge(*SB["w"](h + 1))
                    if h >= 2:
                        pe.wait_ge(*SB["evac"](h - 1))
                    o = bank[7][HD * (h % 2):HD * (h % 2) + HD, :]
                    w = zr[:, h % 7, :]
                    nc.tensor.matmul(o[:, 0:SEQ], v1[:, 0, P + h * HD:P + (h + 1) * HD], w[:, 0:SEQ],
                                     start=True, stop=False, skip_group_check=True)
                    nc.tensor.matmul(o[:, P:SEQ], v1[:, 1, P + h * HD:P + (h + 1) * HD], w[:, SEQ:CW3],
                                     start=False, stop=True, skip_group_check=True).then_inc(SB["out"].sem, 1)
                h = slot - 4
                if 0 <= h < BH:
                    pe.wait_ge(*SB["masked"](h + 1))
                    if h >= 1:
                        pe.wait_ge(*SB["arg2"](h))
                    sp = spr[:, h % 4, :]
                    nc.tensor.matmul(bank[6][:, 0:SEQ], tri, sp[:, 0:SEQ], start=True, stop=False,
                                     skip_group_check=True)
                    nc.tensor.matmul(bank[6][:, P:SEQ], ones, sp[:, SEQ:CW3], start=False, stop=True,
                                     skip_group_check=True)
                    nc.tensor.matmul(bank[6][:, SEQ:CW3], tri, sp[:, SEQ:CW3], start=False, stop=True,
                                     skip_group_check=True).then_inc(SB["suffix"].sem, 1)
                yield

        def b_act(act):
            for slot in range(BH + 9):
                h = slot - 6
                if 0 <= h < BH:
                    act.wait_ge(*SB["arg2"](h + 1))
                    nc.scalar.activation(zr[:, h % 7, :], zr[:, h % 7, :], ACT.Exp).then_inc(SB["w"].sem, 1)
                h = slot - 2
                if 0 <= h < BH:
                    act.wait_ge(*SB["zm"](h + 1))
                    nc.scalar.activation(spr[:, h % 4, :], spr[:, h % 4, :], ACT.Exp).then_inc(SB["small"].sem, 1)
                    act.wait_ge(*SB["small"](h + 1))
                    nc.scalar.activation(spr[:, h % 4, :], spr[:, h % 4, :], ACT.Ln, bias=1.0)\
                        .then_inc(SB["log"].sem, 1)
                yield

        def b_dve(dve):
            dve.wait_ge(*SB["masks"](32))
            for slot in range(BH + 9):
                h = slot - 8
                if 0 <= h < BH:
                    dve.wait_ge(*SB["out"](h + 1))
                    nc.vector.tensor_copy(dst_b(h), bank[7][HD * (h % 2):HD * (h % 2) + HD, 0:SEQ])\
                        .then_inc(SB["evac"].sem, 1)
                h = slot - 1
                if 0 <= h < BH:
                    dve.wait_ge(*SB["score"](h + 1))
                    if h >= 7:
                        dve.wait_ge(*SB["out"](h - 6))
                    if h >= 4:
                        dve.wait_ge(*SB["suffix"](h - 3))
                    z = zr[:, h % 7, :]
                    nc.vector.tensor_scalar(z, bank[4 + h % 2][:, 0:CW3], HD ** -0.5, None, ALU.mult)\
                        .then_inc(SB["zs"].sem, 1)
                    dve.wait_ge(*SB["zs"](h + 1))
                    nc.vector.scalar_tensor_tensor(spr[:, h % 4, :], z, -1.0, z, ALU.mult, ALU.min)\
                        .then_inc(SB["zm"].sem, 1)
                h = slot - 3
                if 0 <= h < BH:
                    z, sp = zr[:, h % 7, :], spr[:, h % 4, :]
                    dve.wait_ge(*SB["log"](h + 1))
                    nc.vector.scalar_tensor_tensor(sp, z, 0.0, sp, ALU.max, ALU.add).then_inc(SB["soft"].sem, 1)
                    dve.wait_ge(*SB["soft"](h + 1))
                    nc.vector.tensor_tensor(sp, sp, m01, ALU.mult).then_inc(SB["masked"].sem, 1)
                    nc.vector.tensor_tensor(z, z, mneg, ALU.add).then_inc(SB["arg"].sem, 1)
                h = slot - 5
                if 0 <= h < BH:
                    dve.wait_ge(*SB["suffix"](h + 1))
                    dve.wait_ge(*SB["arg"](h + 1))
                    nc.vector.tensor_tensor(zr[:, h % 7, :], zr[:, h % 7, :], bank[6][:, 0:CW3], ALU.subtract)\
                        .then_inc(SB["arg2"].sem, 1)
                yield

        def dst_b(h):
            return oT[HD * (h % 2):HD * (h % 2) + HD, 4 + h // 2, :]

        stages.append(("att_b", lambda pe: beside(mem["pe"], MEM_UNITS[1], b_pe(pe), BH + 9),
                       lambda act: beside(mem["act"], MEM_UNITS[1], b_act(act), BH + 9),
                       lambda dve: beside(mem["dve"], MEM_UNITS[1], b_dve(dve), BH + 9), b_load))

        normmix = norm_parts(oT, "mix_gain", [(0, 4), (4, 4), (8, 8)], at(0, NT, SEQ), at(4096, 4, SEQ),
                             at(5120, 3, SEQ))

        def residual_stage(name, u0, before, x_ready=None):
            S = shared("residual", ev=8)

            def chunk(pe, u, c, q, first_two):
                if not first_two:
                    pe.wait_ge(*S["ev"](c * 2 - 2))
                for j in range(8):
                    if c == 0:
                        pe.wait_ge(*before[3](j + 1))
                    unit_features(pe, u + j, j, h_hi, h_lo, 2 * j, bank[2 * q:2 * q + 2], j == 0, j == 7)\
                        .then_inc(unit_done, 1)

            def pe_(pe):
                before[0](pe)
                chunk(pe, u0, 0, 0, True)
                chunk(pe, u0 + 8, 1, 1, True)
                chunk(pe, u0 + 16, 2, 0, False)
                chunk(pe, u0 + 24, 3, 1, False)

            def act_(act):
                before[1](act)
                for u in range(u0, u0 + 32):
                    if u + LEAD < UNITS:
                        split_hi(act, u, u - u0)

            def dve_(dve):
                before[2](dve)
                for c in range(4):
                    for j in range(8):
                        if u0 + 8 * c + j + LEAD < UNITS:
                            split_lo(dve, u0 + 8 * c + j, j)
                    dve.wait_ge(unit_done, u0 + 8 * c + 8)
                    if c == 0 and x_ready:
                        dve.wait_ge(*x_ready)
                    for b in range(2):
                        t = 4 * c + 2 * b
                        nc.vector.tensor_tensor(x[:, t:t + 2, :], x[:, t:t + 2, :],
                                                bank[2 * (c % 2) + b][:, :].rearrange("p (a b) -> p a b", a=2),
                                                ALU.add).then_inc(S["ev"].sem, 1)

            stages.append((name, pe_, act_, dve_, None))

        residual_stage("wout", STREAM["wout"], normmix)

        norm2 = norm_parts(x, "ffn_norm", [(0, NT)], at(0, NT, SEQ), at(4096, 4, SEQ), at(5120, 3, SEQ))

        gT = at(0, NF, SEQ)
        cv = at(11264, 2, 4, SEQ)
        SU = sems("up", "centre conv1 conv2 silu prod")
        UU = STREAM["up"]
        CW, CB = VEC["conv_w"][0], VEC["conv_b"][0]

        def up_pe(pe):
            norm2[0](pe)
            for k in range(2):
                for j in range(8):
                    if k == 0:
                        pe.wait_ge(*norm2[3](j + 1))
                    unit_features(pe, UU + 8 * k + j, j, h_hi, h_lo, 2 * j, bank[2 * k:2 * k + 2],
                                  j == 0, j == 7).then_inc(unit_done, 1)
            with pe.Fori(1, 11) as i:
                for k in range(2):
                    pe.wait_ge(*SU["conv2"](i * 8 + (4 * k - 4)))
                    for j in range(8):
                        unit_features(pe, i * 16 + (UU + 8 * k + j), j, h_hi, h_lo, 2 * j,
                                      bank[2 * k:2 * k + 2], j == 0, j == 7).then_inc(unit_done, 1)

        def up_turn_act(act, i, first):
            for k in range(2):
                u = i * 16 + (UU + 8 * k)
                chunk_split(act, split_hi, u)
                act.wait_ge(unit_done, u + 8)
                if not first:
                    act.wait_ge(*SU["prod"](i))
                for f in range(4):
                    c = i * 4 + (44 * k + f)
                    nc.scalar.activation(cv[:, k, f, :], bank[2 * k + f // 2][:, (f % 2) * SEQ:(f % 2 + 1) * SEQ],
                                         ACT.Identity, bias=vec[:, bass.ds(c + CB, 1)],
                                         scale=vec[:, bass.ds(c + (CW + 2 * 88), 1)]).then_inc(SU["centre"].sem, 1)
            act.wait_ge(*SU["conv2"](i * 8 + 4))
            nc.scalar.activation(cv[:, 0, :, :], cv[:, 0, :, :], ACT.Silu).then_inc(SU["silu"].sem, 1)

        def up_act(act):
            norm2[1](act)
            up_turn_act(act, 0, True)
            with act.Fori(1, 11) as i:
                up_turn_act(act, i, False)

        def up_dve(dve):
            norm2[2](dve)
            with dve.Fori(0, 11) as i:
                for k in range(2):
                    u = i * 16 + (UU + 8 * k)
                    chunk_split(dve, split_lo, u)
                    for f in range(4):
                        c = i * 4 + (44 * k + f)
                        b = bank[2 * k + f // 2][:, (f % 2) * SEQ:(f % 2 + 1) * SEQ]
                        dve.wait_ge(*SU["centre"](i * 8 + (4 * k + (2 if f < 2 else 4))))
                        nc.vector.scalar_tensor_tensor(cv[:, k, f, 1:SEQ], b[:, 0:SEQ - 1],
                                                       vec[:, bass.ds(c + (CW + 88), 1)], cv[:, k, f, 1:SEQ],
                                                       ALU.mult, ALU.add).then_inc(SU["conv1"].sem, 1)
                    for f in range(4):
                        c = i * 4 + (44 * k + f)
                        b = bank[2 * k + f // 2][:, (f % 2) * SEQ:(f % 2 + 1) * SEQ]
                        dve.wait_ge(*SU["conv1"](i * 8 + (4 * k + f + 1)))
                        nc.vector.scalar_tensor_tensor(cv[:, k, f, 2:SEQ], b[:, 0:SEQ - 2],
                                                       vec[:, bass.ds(c + CW, 1)], cv[:, k, f, 2:SEQ],
                                                       ALU.mult, ALU.add).then_inc(SU["conv2"].sem, 1)
                        if f == 3:
                            dve.wait_ge(*SU["conv2"](i * 8 + (4 * k + 4)))
                dve.wait_ge(*SU["silu"](i + 1))
                nc.vector.tensor_tensor(gT[:, bass.ds(i * 4, 4), :], cv[:, 0, :, :], cv[:, 1, :, :], ALU.mult)\
                    .then_inc(SU["prod"].sem, 1)

        stages.append(("up", up_pe, up_act, up_dve, None))

        SD = sems("down", "g_hi g_lo ev_a ev_d")
        UD = STREAM["down"]

        def down_turn(pe, i, buf, j0, first, last):
            pe.wait_ge(*SD["g_lo"](i + 1))
            for j in range(4):
                unit_features(pe, i * 4 + (UD + j), j, o_hi[:, 2 * buf:2 * buf + 2, :], o_lo[:, 2 * buf:2 * buf + 2, :],
                              0, bank[2 * j:2 * j + 2], first, last).then_inc(unit_done, 1)

        def down_pe(pe):
            down_turn(pe, 0, 0, 0, True, False)
            down_turn(pe, 1, 1, 4, False, False)
            with pe.Fori(1, 10) as i:
                for b in range(2):
                    down_turn(pe, i * 2 + b, b, 4 * b, False, False)
            down_turn(pe, 20, 0, 0, False, False)
            down_turn(pe, 21, 1, 4, False, True)

        def down_turn_act(act, i, b, first):
            if not first:
                act.wait_ge(unit_done, i * 4 + (UD - 4))
            nc.scalar.activation(o_hi[:, 2 * b:2 * b + 2, :], gT[:, bass.ds(i * 2, 2), :], ACT.Copy)\
                .then_inc(SD["g_hi"].sem, 1)

        def down_act(act):
            down_turn_act(act, 0, 0, True)
            down_turn_act(act, 1, 1, True)
            for b in range(2):
                for j in range(4):
                    split_hi(act, UD + 4 * b + j, j)
            with act.Fori(1, 11) as i:
                for b in range(2):
                    down_turn_act(act, i * 2 + b, b, False)
                    for j in range(4):
                        split_hi(act, i * 8 + (UD + 4 * b + j), j)

        def down_turn_dve(dve, i, b, first):
            dve.wait_ge(*SD["g_hi"](i + 1))
            if not first:
                dve.wait_ge(unit_done, i * 4 + (UD - 4))
            nc.vector.tensor_tensor(o_lo[:, 2 * b:2 * b + 2, :], gT[:, bass.ds(i * 2, 2), :],
                                    o_hi[:, 2 * b:2 * b + 2, :].bitcast(F32), ALU.subtract).then_inc(SD["g_lo"].sem, 1)

        def down_dve(dve):
            down_turn_dve(dve, 0, 0, True)
            down_turn_dve(dve, 1, 1, True)
            for b in range(2):
                for j in range(4):
                    split_lo(dve, UD + 4 * b + j, j)
            with dve.Fori(1, 11) as i:
                for b in range(2):
                    down_turn_dve(dve, i * 2 + b, b, False)
                    for j in range(4):
                        split_lo(dve, i * 8 + (UD + 4 * b + j), j)
            dve.wait_ge(unit_done, UD + 88)
            for b in range(8):
                nc.vector.tensor_tensor(x[:, 2 * b:2 * b + 2, :], x[:, 2 * b:2 * b + 2, :],
                                        bank[b][:, :].rearrange("p (a b) -> p a b", a=2), ALU.add)\
                    .then_inc(SD["ev_d"].sem, 1)

        stages.append(("down", down_pe, down_act, down_dve, None))

        SX = shared("split", hi=4, lo=4)

        def splitx_act(act):
            for n in range(4):
                nc.scalar.activation(h_hi[:, 4 * n:4 * n + 4, :], x[:, 4 * n:4 * n + 4, :], ACT.Copy)\
                    .then_inc(SX["hi"].sem, 1)

        def splitx_dve(dve):
            for n in range(4):
                dve.wait_ge(*SX["hi"](n + 1))
                nc.vector.tensor_tensor(h_lo[:, 4 * n:4 * n + 4, :], x[:, 4 * n:4 * n + 4, :],
                                        h_hi[:, 4 * n:4 * n + 4, :].bitcast(F32), ALU.subtract)\
                    .then_inc(SX["lo"].sem, 1)


        merged = at(0, NT, SEQ)
        M0, M1, C0 = 4096, 12288, 10240

        def merge_stage(name, u0, first, sig, side, o_ready=None, woven=4):
            S = shared("merge", sig=8, prod=8, add=0 if first else 8)
            n_side = side[3]
            over = 12 * woven if woven > 1 else 8

            def turn_pe(pe, i, first_turn):
                if not first_turn:
                    pe.wait_ge(*S["sig"](i * 2))
                for j in range(8):
                    unit_features(pe, i * 12 + (u0 + j), j, h_hi, h_lo, 2 * j, bank[0:2], j == 0, j == 7)\
                        .then_inc(unit_done, 1)
                    yield
                if not first_turn:
                    pe.wait_ge(*S["prod"](i * 2))
                elif o_ready:
                    pe.wait_ge(*o_ready)
                for j in range(4):
                    unit_features(pe, i * 12 + (u0 + 8 + j), j, o_hi, o_lo, 2 * j, bank[2:4], j == 0, j == 3)\
                        .then_inc(unit_done, 1)
                    yield

            def turn_act(act, i, first_turn):
                for j in range(12):
                    split_hi(act, i * 12 + (u0 + j), j)
                    if j == 7:
                        act.wait_ge(unit_done, i * 12 + (u0 + 8))
                        if not first_turn:
                            act.wait_ge(*S["prod" if first else "add"](i * 2))
                        for b in range(2):
                            nc.scalar.activation(sig[b], bank[b][:, :].rearrange("p (a b) -> p a b", a=2),
                                                 ACT.Sigmoid).then_inc(S["sig"].sem, 1)
                    yield

            def turn_dve(dve, i, first_turn):
                for j in range(12):
                    split_lo(dve, i * 12 + (u0 + j), j)
                    if j < 11:
                        yield
                dve.wait_ge(unit_done, i * 12 + (u0 + 12))
                dve.wait_ge(*S["sig"](i * 2 + 2))
                for b in range(2):
                    t = i * 4 + 2 * b
                    d = merged[:, t:t + 2, :] if isinstance(i, int) else merged[:, bass.ds(t, 2), :]
                    src = bank[2 + b][:, :].rearrange("p (a b) -> p a b", a=2)
                    nc.vector.tensor_tensor(d if first else sig[b], src, sig[b], ALU.mult).then_inc(S["prod"].sem, 1)
                    if not first:
                        dve.wait_ge(*S["prod"](i * 2 + (b + 1)))
                        nc.vector.tensor_tensor(d, d, sig[b], ALU.add).then_inc(S["add"].sem, 1)
                yield

            def program(turn, steps):
                def go(eng):
                    weave(then(*(turn(eng, i, i == 0) for i in range(woven))), over, steps(eng), n_side)
                    if woven < 4:
                        with eng.Fori(woven, 4) as i:
                            run(turn(eng, i, False))
                return go

            return program(turn_pe, side[0]), program(turn_act, side[1]), program(turn_dve, side[2])

        def product_steps(src, gate_tiles):
            S = shared("product", silu=1, scaled=8, hi=4, lo=4)

            def pe_(pe):
                yield from range(8)

            def act_(act):
                for step in range(8):
                    if step == 0:
                        nc.scalar.activation(gate_tiles, gate_tiles, ACT.Silu).then_inc(S["silu"].sem, 1)
                    p = step - 2
                    if 0 <= p < 4:
                        act.wait_ge(*S["scaled"](2 * p + 2))
                        nc.scalar.activation(o_hi[:, 2 * p:2 * p + 2, :], src[:, 2 * p:2 * p + 2, :], ACT.Copy)\
                            .then_inc(S["hi"].sem, 1)
                    yield

            def dve_(dve):
                put = to_moving_dve(dve, S, src, o_hi, o_lo)
                for step in range(8):
                    p = step - 1
                    if 0 <= p < 4:
                        if p == 0:
                            dve.wait_ge(*S["silu"](1))
                        nc.vector.tensor_tensor(src[:, 2 * p:2 * p + 2, :], src[:, 2 * p:2 * p + 2, :],
                                                gate_tiles[:, 2 * p:2 * p + 2, :], ALU.mult).then_inc(S["scaled"].sem, 2)
                    if 0 <= step - 3 < 4:
                        put(step - 3)
                    yield

            return pe_, act_, dve_, 8, S["lo"](4)

        def both(one, other):
            return tuple((lambda eng, n=n: then(one[n](eng), other[n](eng))) for n in range(3)) + (one[3] + other[3],)

        def projection(u0, kinds, ev, dst, side):
            n = 8 * len(kinds)
            return (lambda pe: weave(steps_pe(pe, ev, u0, kinds), n, side[0](pe), side[3]),
                    lambda act: weave(steps_act(act, ev, u0, kinds, dst), n, side[1](act), side[3]),
                    lambda dve: weave(steps_dve(dve, ev, u0, kinds, dst), n, side[2](dve), side[3]))

        ua, ga = at(0, 8, SEQ), at(2048, 8, SEQ)
        va = at(M1, 2, 1024)
        sw = at(M1 + 2048, 8, P)
        lnr = at(M1 + 3072, 2, 1024)
        sbr = at(M1 + 5120, 8 * P, parts=(0, 1))
        ev_a = halves(6)
        UA = STREAM["p_a"]
        SA = sems("gmlp", "load gelu st ag sd rc n g b u mask mixed prod")

        def pa_load(pool):
            pool.dma_start(sw, sgu_wT).then_inc(SA["load"].sem, 16)
            pool.dma_start(lnr, ln_rows.broadcast_to([P, 2 * 1024]).rearrange("p (a b) -> p a b", a=2))\
                .then_inc(SA["load"].sem, 16)
            pool.dma_start(sbr, sgu_b).then_inc(SA["load"].sem, 16)

        uag = at(0, 16, SEQ)

        def pa_pe(pe):
            features_pe(pe, ev_a, UA, 4, lambda n: SX["lo"]((n + 1) // 2))
            tokens_pe(pe, ev_a, UA + 32, 4, 2)

        def pa_act(act):
            splitx_act(act)
            features_act(act, ev_a, UA, 4, uag)
            tokens_act(act, ev_a, UA + 32, 4, 2, lambda m, c: va[:, m, c * UN:(c + 1) * UN])

        def pa_dve(dve):
            splitx_dve(dve)
            features_dve(dve, ev_a, UA, 4, uag)
            tokens_dve(dve, ev_a, UA + 32, 4, 2, lambda m, c: va[:, m, c * UN:(c + 1) * UN])

        stages.append(("p_a", pa_pe, pa_act, pa_dve, pa_load))

        stat = small[:, 64:88].rearrange("p (a b) -> p a b", a=2)
        mv = small[:, 88:92].rearrange("p (a b) -> p a b", a=2)
        rs = small[:, 92:94]
        GATING = 16

        def gmlp_act(act):
            for step in range(GATING):
                if step < 2:
                    nc.scalar.activation(va[:, step, :], va[:, step, :], ACT.Gelu_apprx_tanh).then_inc(SA["gelu"].sem, 1)
                if step in (4, 5):
                    m = step - 4
                    act.wait_ge(*SA["ag"](m + 1))
                    nc.scalar.activation(rs[:, m:m + 1], mv[:, m, 1:2], ACT.Sqrt, bias=ln_eps_col)\
                        .then_inc(SA["sd"].sem, 1)
                if step == 6:
                    nc.scalar.activation(ua, ua, ACT.Gelu_apprx_tanh).then_inc(SA["u"].sem, 1)
                yield

        def gmlp_dve(dve):
            for step in range(GATING):
                if step == 0:
                    dve.wait_ge(*SA["load"](48))
                    nc.vector.tensor_tensor(sw, sw, causal.unsqueeze(1).broadcast_to([P, 8, P]), ALU.mult)\
                        .then_inc(SA["mask"].sem, 1)
                if step in (2, 3):
                    m = step - 2
                    dve.wait_ge(*SA["gelu"](m + 1))
                    for c in range(2):
                        nc.vector.bn_stats(stat[:, m, 6 * c:6 * c + 6], va[:, m, c * 512:(c + 1) * 512])\
                            .then_inc(SA["st"].sem, 1)
                    dve.wait_ge(*SA["st"](2 * m + 2))
                    nc.vector.bn_aggr(mv[:, m, :], stat[:, m, :]).then_inc(SA["ag"].sem, 1)
                if step in (5, 6):
                    m = step - 5
                    dve.wait_ge(*SA["sd"](m + 1))
                    dve.wait_ge(*SA["ag"](m + 1))
                    nc.vector.reciprocal(rs[:, m:m + 1], rs[:, m:m + 1]).then_inc(SA["rc"].sem, 1)
                    dve.wait_ge(*SA["rc"](m + 1))
                    nc.vector.tensor_scalar(va[:, m, :], va[:, m, :], mv[:, m, 0:1], rs[:, m:m + 1], ALU.subtract,
                                            ALU.mult).then_inc(SA["n"].sem, 1)
                if step in (7, 8):
                    m = step - 7
                    dve.wait_ge(*SA["n"](m + 1))
                    nc.vector.tensor_tensor(va[:, m, :], va[:, m, :], lnr[:, 0, :], ALU.mult).then_inc(SA["g"].sem, 1)
                    dve.wait_ge(*SA["g"](m + 1))
                    nc.vector.tensor_tensor(va[:, m, :], va[:, m, :], lnr[:, 1, :], ALU.add).then_inc(SA["b"].sem, 1)
                if 12 <= step < 16:
                    g = step - 12
                    if g == 0:
                        dve.wait_ge(*SA["u"](1))
                    dve.wait_ge(*SA["mixed"](g + 1))
                    nc.vector.tensor_tensor(ua[:, 2 * g:2 * g + 2, :], ua[:, 2 * g:2 * g + 2, :],
                                            bank[4 + g][:, :].rearrange("p (a b) -> p a b", a=2), ALU.mult)\
                        .then_inc(SA["prod"].sem, 1)
                yield

        def gmlp_pe(pe):
            for step in range(GATING):
                if 10 <= step < 14:
                    if step == 10:
                        pe.wait_ge(*SA["mask"](1))
                        pe.wait_ge(*SA["b"](2))
                    for g in (2 * (step - 10), 2 * (step - 10) + 1):
                        for c in range(2):
                            o = bank[4 + g // 2][:, (g % 2) * SEQ + c * P:(g % 2) * SEQ + (c + 1) * P]
                            nc.tensor.matmul(o, va[:, c, g * P:(g + 1) * P], sw[:, g, :], start=True, stop=False)
                            mm = nc.tensor.matmul(o, ones[0:1, :], sbr[:, g * P:(g + 1) * P], start=False, stop=True)
                    mm.then_inc(SA["mixed"].sem, 1)
                yield

        qgm = at(M0, 16, SEQ)
        qm, gm = at(M0, 8, SEQ), at(M0 + 2048, 8, SEQ)
        om = at(M0 + 4096, 8, SEQ)
        ev_m = halves(4)
        product_a = product_steps(ua, ga)
        stages.append(("p_m", *projection(STREAM["p_m"], "FFFF", ev_m, to_tiles(qgm),
                                          both((gmlp_pe, gmlp_act, gmlp_dve, GATING), product_a)), None))
        m_rings = at(M1, 4, 2 * SEQ), at(M1 + 2048, 2, 2 * SEQ)

        def m_pv(h):
            def go(pt):
                for d in range(2):
                    for kt in range(2):
                        yield nc.tensor.matmul(bank[7][:, d * SEQ:(d + 1) * SEQ],
                                               vm[:, kt, h * SEQ + d * P:h * SEQ + (d + 1) * P],
                                               pt[:, kt * SEQ:(kt + 1) * SEQ], start=kt == 0, stop=kt == 1)
            return go

        def m_job(h):
            return dict(scores=lambda m: [(qm[:, 2 * h + d, m * P:(m + 1) * P], kmT[:, 2 * h + d, :]) for d in range(2)],
                        segs=[(0, SEQ), (SEQ, SEQ)], parts=[(0, P), (SEQ, P), (P, P), (SEQ + P, P)], last=True,
                        out_regions=1, pv=m_pv(h))

        att_m = softmax([m_job(h) for h in range(4)], SEQ ** -0.5, lambda h: nc.vector.tensor_copy(
            om[:, 2 * h:2 * h + 2, :], bank[7][:, :].rearrange("p (a b) -> p a b", a=2)), m_rings)
        sig_a = [at(M0 + 6144 + 512 * b, 2, SEQ) for b in range(2)]
        stages.append(("m_a", *merge_stage("m_a", STREAM["m_a"], True, sig_a, (*att_m[0:3], att_m[4])), None))

        qc = at(C0, 8, SEQ)
        cmpT = at(C0 + 2048, 4, SEQ)
        ksw = at(C0 + 3072, 4, SEQ)
        gc = at(C0 + 4096, 8, SEQ)
        swp = at(C0 + 6144, 4, SEQ)
        vsw = at(C0 + 7168, 2, 512)
        zz = at(M0, 2, 4 * SEQ)
        w1 = at(M0 + 2048, 4096)
        onc = at(M0 + 4096, 8, SEQ)
        qgc = at(C0, 24, SEQ)
        kmF = kmT[:, :, :].rearrange("p a b -> p (a b)")
        glr = kmF[:, 0:768]
        oh2 = kmF[0:33, 768:1280]
        tb2 = kmF[0:33, 1280:1320]
        w2 = vm[:, 0, 0:256].rearrange("p (a b c) -> p a b c", a=2, b=2)
        kcT = vm[:, 0, 256:316]
        vcs = vm[0:15, 0, 320:576]
        hid = vm[:, 0, 576:816].rearrange("p (a b c) -> p a b c", a=2, b=2)
        blk = kmF[:, 0:960].rearrange("p (j h n) -> p j h n", j=16, h=4)
        cmk = vm[:, 0, 820:850]
        glb = vm[:, 0, 850:898]
        gts = vm[:, 0, 900:996].rearrange("p (m g) -> p m g", m=2)
        cb = vm[:, 1, 0:480].rearrange("p (h c) -> p h c", h=16)
        sig_m = [kmF[:, 1320:1832].rearrange("p (a b) -> p a b", a=2),
                 vm[:, 1, 480:992].rearrange("p (a b) -> p a b", a=2)]
        n_rings = kmF[:, 0:4 * CW3].rearrange("p (a b) -> p a b", a=4), at(C0 + 2048, 2, CW3)
        bias_n = [vm[:, 1, 480:480 + CW3], at(C0 + 8192, CW3)]
        ev_c = halves(7)
        UC = STREAM["p_c"]
        SC = sems("nsa", "load swap gate gl bias cbev z w1k w1v hid blk h kc kcv g2")

        def pc_load(pool):
            pool.dma_start(glr.rearrange("p (a b) -> p a b", a=NT), gl_w).then_inc(SC["load"].sem, 16)
            pool.dma_start(glb, gl_b.broadcast_to([P, 48])).then_inc(SC["load"].sem, 16)
            pool.dma_start(oh2, onehots[:, 3, :]).then_inc(SC["load"].sem, 16)
            pool.dma_start(tb2, tabs).then_inc(SC["load"].sem, 16)
            pool.dma_start(cmk, cmask).then_inc(SC["load"].sem, 16)
            pool.dma_start(w2[:, 0, :, :], cmp_w2k).then_inc(SC["load"].sem, 16)
            pool.dma_start(w2[:, 1, :, :], cmp_w2v).then_inc(SC["load"].sem, 16)

        def c_dst(half, c):
            return to_tiles(qgc)(half, c) if c < 6 else vsw[:, half, :]

        product_m = product_steps(om, gm)
        stages.append(("p_c", *projection(UC, "FFFFFFT", ev_c, c_dst, product_m), pc_load))

        def cmp_load(pool):
            for t in range(4):
                pool.dma_start(swp[HD:P, t, :], ksw[0:HD, t, :]).then_inc(SC["swap"].sem, 16)
                pool.dma_start(swp[0:HD, t, :], ksw[HD:P, t, :]).then_inc(SC["swap"].sem, 16)
            for n in range(2):
                for h in range(4):
                    src = cmpT[HD * (h % 2):HD * (h % 2) + HD, 2 * n + h // 2, :]
                    pool.dma_start(zz[0:HD, n, h * SEQ:(h + 1) * SEQ], src).then_inc(SC["z"].sem, 16)
                    pool.dma_start(zz[HD:P, n, h * SEQ:(h + 1) * SEQ - 1], src[:, 1:SEQ]).then_inc(SC["z"].sem, 16)
            pool.dma_start(w1, cmp_w1[0]).then_inc(SC["w1k"].sem, 16)
            pool.wait_ge(*SC["hid"](1))
            pool.dma_start(w1, cmp_w1[1]).then_inc(SC["w1v"].sem, 16)
            pool.wait_ge(*SC["swap"](128))
            pool.wait_ge(*SC["z"](256))

        COMPRESSION = 48

        def cmp_hidden_pe(pe, o, js):
            for j in js:
                mm = nc.tensor.matmul(bank[6 + o][:, 0:60], w1[:, j * 256 + o * P:j * 256 + (o + 1) * P],
                                      blk[:, j, :, :].rearrange("p a b -> p (a b)"), start=j == 0, stop=j == 15)
            return mm

        def cmp_pe(pe):
            for step in range(COMPRESSION):
                if 2 <= step < 10:
                    if step == 2:
                        pe.wait_ge(*SC["load"](112))
                    m = (step - 2) // 4
                    for t in range(4 * ((step - 2) % 4), 4 * ((step - 2) % 4) + 4):
                        mm = nc.tensor.matmul(bank[4][:, 48 * m:48 * m + 48], x[:, t, m * P:(m + 1) * P],
                                              glr[:, 48 * t:48 * t + 48], start=t == 0, stop=t == NT - 1)
                    if step == 9:
                        mm.then_inc(SC["gl"].sem, 1)
                if 10 <= step < 15:
                    for k in range(6 * (step - 10), 6 * (step - 9)):
                        m, n = divmod(k, 15)
                        a = SEQ + P * m - 16 * n - 31
                        mm = nc.tensor.matmul(bank[5][:, k * 16:(k + 1) * 16], oh2[:, a:a + P], tb2[:, 24:40],
                                              start=True, stop=True)
                    if step == 14:
                        mm.then_inc(SC["bias"].sem, 1)
                for n, start in enumerate((18, 30)):
                    if start <= step < start + 8:
                        if step == start:
                            pe.wait_ge(*SC["blk"](4 * n + 4))
                            if n:
                                pe.wait_ge(*SC["h"](2))
                            pe.wait_ge(*SC["w1v" if n else "w1k"](16))
                        o, part = divmod(step - start, 4)
                        mm = cmp_hidden_pe(pe, o, range(4 * part, 4 * part + 4))
                        if step == start + 7:
                            mm.then_inc(SC["hid"].sem, 1)
                if step == 41:
                    pe.wait_ge(*SC["h"](4))
                    pe.wait_ge(*SC["g2"](1))
                    for half in range(2):
                        for o in range(2):
                            nc.tensor.matmul(bank[4][HD * half:HD * half + HD, 0:60], w2[:, 0, o, :],
                                             hid[:, 0, o, :], start=o == 0, stop=o == 1)
                    for h in range(4):
                        for o in range(2):
                            mm = nc.tensor.matmul(bank[6][0:15, h * HD:(h + 1) * HD], hid[:, 1, o, h * 15:(h + 1) * 15],
                                                  w2[:, 1, o, :], start=o == 0, stop=o == 1)
                    mm.then_inc(SC["kc"].sem, 1)
                yield

        def cmp_act(act):
            for step in range(COMPRESSION):
                if step in (27, 39):
                    n = 0 if step == 27 else 1
                    act.wait_ge(*SC["hid"](n + 1))
                    for o in range(2):
                        nc.scalar.activation(hid[:, n, o, :], bank[6 + o][:, 0:60], ACT.Silu).then_inc(SC["h"].sem, 1)
                if step == 12:
                    act.wait_ge(*SC["g2"](1))
                    nc.scalar.activation(gts, gts, ACT.Sigmoid).then_inc(SC["gate"].sem, 1)
                if step == 43:
                    act.wait_ge(*SC["kc"](1))
                    nc.scalar.activation(kcT, bank[4][:, 0:60], ACT.Copy)
                    nc.scalar.activation(vcs, bank[6][0:15, 0:256], ACT.Copy).then_inc(SC["kcv"].sem, 1)
                yield

        def cmp_dve(dve):
            for step in range(COMPRESSION):
                if step == 11:
                    dve.wait_ge(*SC["load"](112))
                    dve.wait_ge(*SC["gl"](1))
                    nc.vector.tensor_tensor(gts, bank[4][:, 0:96].rearrange("p (m g) -> p m g", m=2),
                                            glb.unsqueeze(1).broadcast_to([P, 2, 48]), ALU.add)\
                        .then_inc(SC["g2"].sem, 1)
                if step in (17, 27):
                    n = 0 if step == 17 else 1
                    if n == 0:
                        dve.wait_ge(*SC["z"](256))
                    else:
                        dve.wait_ge(*SC["hid"](1))
                    pv = VEC["cmp_pe_v" if n else "cmp_pe_k"][0]
                    for h in range(4):
                        z = zz[:, n, h * SEQ:(h + 1) * SEQ]
                        z = bass.AP(tensor=z.tensor, offset=z.offset, ap=[z.ap[0], [2, 16], [16, 15]])
                        nc.vector.tensor_tensor(blk[:, :, h, :], z, vec[:, pv:pv + 16].unsqueeze(2)
                                                .broadcast_to([P, 16, 15]), ALU.add).then_inc(SC["blk"].sem, 1)
                if step == 16:
                    dve.wait_ge(*SC["bias"](1))
                    nc.vector.tensor_copy(cb, bank[5][:, 0:480].rearrange("p (c h) -> p h c", h=16))\
                        .then_inc(SC["cbev"].sem, 1)
                yield

        stages.append(("m_m", *merge_stage("m_m", STREAM["m_m"], False, sig_m, (cmp_pe, cmp_act, cmp_dve, COMPRESSION)),
                       cmp_load))

        def n_job(h, br):
            p, kv = h % 2, h // 4
            rows_ = slice(HD * p, HD * p + HD)
            j = dict(last=br == 2, out_regions=2, gate=gts[:, :, 16 * ((br + 1) % 3) + h])
            if br < 2:
                kk, t = ksw if kv % 2 == p else swp, 2 * br + kv // 2
                c = br * SEQ + kv * HD
                j.update(scores=lambda m: [(qc[rows_, h // 2, m * P:(m + 1) * P], kk[rows_, t, 0:P + m * P])],
                         buf=h % 2, **CAUSAL,
                         pv=causal_pv(head_dst(h), lambda kt: vsw[:, kt, c:c + HD], br == 0, False))
                if br == 0:
                    j["load"] = 24 + h
            else:
                j.update(scores=lambda m: [(qc[rows_, h // 2, m * P:(m + 1) * P], kcT[rows_, kv * 15:(kv + 1) * 15])],
                         tile=cb[:, h, :], segs=[(0, 15), (15, 15)], parts=[(0, 15), (15, 15)], weights=cmk, floor=True,
                         pv=lambda pt: [nc.tensor.matmul(bank[7][HD * p:HD * p + HD, 0:SEQ],
                                                         vcs[:, kv * HD:(kv + 1) * HD], pt[0:15, 0:SEQ],
                                                         start=False, stop=True, skip_group_check=True)])
            return j

        def dst_n(h):
            return onc[HD * (h % 2):HD * (h % 2) + HD, h // 2, :]

        att_n = softmax([n_job(h, br) for h in range(16) for br in range(3)], HD ** -0.5, head_evac(dst_n),
                        n_rings, bias_n)
        xb, gb = at(M0, 8, SEQ), at(M0 + 2048, 8, SEQ)
        xc = at(C0, 8, SEQ)
        lw = at(C0 + 2048, 2, 8, P)
        av = at(C0 + 2048, 8, SEQ)
        iv, tv = at(C0 + 6144, 8, SEQ), onc
        rv = xb
        xgb = at(M0, 16, SEQ)
        ev_b = halves(4)
        UB = STREAM["p_b"]
        SL = sems("lru", "load c0 c1 c2 c3 mm i chain spn t a2 f s g1 g2 scan al ex2")

        def lw_load(pool):
            pool.dma_start(lw, lru_w).then_inc(SL["load"].sem, 16)

        stages.append(("p_b", *projection(UB, "FFFF", ev_b, to_tiles(xgb), (*att_n[0:3], att_n[4])), att_n[3]))
        product_c = product_steps(onc, gc)
        C2, C2B = VEC["conv2_w"][0], VEC["conv2_b"][0]
        lam = vec[:, VEC["lru_lam"][0]:VEC["lru_lam"][0] + 8]
        T = [small[:, 94 + 8 * n:102 + 8 * n] for n in range(7)]
        LOG_TERMS = 9

        LRU = 40

        def lru_pe(pe):
            for step in range(LRU):
                t = step - 4
                if 0 <= t < 8:
                    if t == 0:
                        pe.wait_ge(*SL["load"](16))
                    pe.wait_ge(*SL["c3"](t + 1))
                    if t >= 4:
                        pe.wait_ge(*SL["i"](t - 3))
                    for n in range(2):
                        mm = nc.tensor.matmul(bank[4 + t % 4][:, n * SEQ:(n + 1) * SEQ], lw[:, n, t, :], xc[:, t, :],
                                              start=True, stop=True)
                    mm.then_inc(SL["mm"].sem, 1)
                yield

        def lru_act(act):
            for step in range(LRU):
                if step == 1:
                    act.wait_ge(*SL["al"](1))
                    nc.scalar.activation(T[0], T[0], ACT.Exp).then_inc(SL["ex2"].sem, 1)
                t = step - 5
                if 0 <= t < 8:
                    act.wait_ge(*SL["mm"](t + 1))
                    nc.scalar.activation(rv[:, t, :], bank[4 + t % 4][:, 0:SEQ], ACT.Sigmoid, bias=vcol("lru_ba", t))
                    nc.scalar.activation(iv[:, t, :], bank[4 + t % 4][:, SEQ:2 * SEQ], ACT.Sigmoid,
                                         bias=vcol("lru_bx", t)).then_inc(SL["i"].sem, 1)
                p = step - 14
                if 0 <= p < 4:
                    if p == 0:
                        act.wait_ge(*SL["i"](8))
                        act.wait_ge(*SL["spn"](1))
                        act.wait_ge(*product_c[4])
                    for t in (2 * p, 2 * p + 1):
                        nc.scalar.activation(av[:, t, :], rv[:, t, :], ACT.Exp, scale=T[5][:, t:t + 1])
                        nc.scalar.activation(tv[:, t, :], rv[:, t, :], ACT.Tanh, scale=T[6][:, t:t + 1])\
                            .then_inc(SL["t"].sem, 1)
                t = step - 19
                if 0 <= t < 4:
                    act.wait_ge(*SL["f"](t + 1))
                    nc.scalar.activation(tv[:, 2 * t:2 * t + 2, :], tv[:, 2 * t:2 * t + 2, :], ACT.Sqrt)\
                        .then_inc(SL["s"].sem, 1)
                yield

        def lru_dve(dve):
            n = [0]

            def link(i):
                n[0] += 1
                i.then_inc(SL["chain"].sem, 1)
                dve.wait_ge(*SL["chain"](n[0]))
            for step in range(LRU):
                if step == 0:
                    link(nc.vector.tensor_scalar(T[1], lam, -1.0, None, ALU.mult))
                    nc.vector.tensor_tensor(T[0], T[1], lam, ALU.min).then_inc(SL["al"].sem, 1)
                if step == 2:
                    dve.wait_ge(*SL["ex2"](1))
                    link(nc.vector.tensor_scalar(T[2], T[0], 2.0, None, ALU.add))
                    link(nc.vector.reciprocal(T[2], T[2]))
                    link(nc.vector.tensor_tensor(T[2], T[2], T[0], ALU.mult))
                    link(nc.vector.tensor_tensor(T[3], T[2], T[2], ALU.mult))
                    link(nc.vector.memset(T[4], 2.0 / (2 * LOG_TERMS + 1)))
                if 3 <= step < 3 + LOG_TERMS:
                    k = LOG_TERMS - 1 - (step - 3)
                    link(nc.vector.tensor_tensor(T[4], T[4], T[3], ALU.mult))
                    link(nc.vector.tensor_scalar(T[4], T[4], 2.0 / (2 * k + 1), None, ALU.add))
                if step == 3 + LOG_TERMS:
                    link(nc.vector.tensor_tensor(T[4], T[4], T[2], ALU.mult))
                    link(nc.vector.tensor_scalar(T[1], T[1], 0.0, None, ALU.max))
                    link(nc.vector.tensor_tensor(T[4], T[4], T[1], ALU.add))
                    link(nc.vector.tensor_scalar(T[5], T[4], -8.0, None, ALU.mult))
                    nc.vector.tensor_scalar(T[6], T[4], 8.0, None, ALU.mult).then_inc(SL["spn"].sem, 1)
                t = step - 3
                if 0 <= t < 8:
                    for tap in range(4):
                        w = vec[:, C2 + 8 * (3 - tap) + t:C2 + 8 * (3 - tap) + t + 1]
                        if tap == 0:
                            nc.vector.tensor_scalar(xc[:, t, :], xb[:, t, :], w, vec[:, C2B + t:C2B + t + 1], ALU.mult,
                                                    ALU.add).then_inc(SL["c0"].sem, 1)
                        else:
                            dve.wait_ge(*SL[f"c{tap - 1}"](t + 1))
                            nc.vector.scalar_tensor_tensor(xc[:, t, tap:SEQ], xb[:, t, 0:SEQ - tap], w,
                                                           xc[:, t, tap:SEQ], ALU.mult, ALU.add)\
                                .then_inc(SL[f"c{tap}"].sem, 1)
                t = step - 16
                if 0 <= t < 4:
                    dve.wait_ge(*SL["t"](2 * t + 2))
                    two = slice(2 * t, 2 * t + 2)
                    nc.vector.tensor_tensor(rv[:, two, :], av[:, two, :], av[:, two, :], ALU.mult)\
                        .then_inc(SL["a2"].sem, 1)
                    dve.wait_ge(*SL["a2"](t + 1))
                    nc.vector.scalar_tensor_tensor(tv[:, two, :], rv[:, two, :], 1.0, tv[:, two, :], ALU.add, ALU.mult)\
                        .then_inc(SL["f"].sem, 1)
                    nc.vector.tensor_tensor(iv[:, two, :], iv[:, two, :], xc[:, two, :], ALU.mult)\
                        .then_inc(SL["g1"].sem, 1)
                t = step - 22
                if 0 <= t < 4:
                    two = slice(2 * t, 2 * t + 2)
                    dve.wait_ge(*SL["s"](t + 1))
                    dve.wait_ge(*SL["g1"](t + 1))
                    nc.vector.tensor_tensor(iv[:, two, :], iv[:, two, :], tv[:, two, :], ALU.mult)\
                        .then_inc(SL["g2"].sem, 1)
                t = step - 24
                if 0 <= t < 8:
                    dve.wait_ge(*SL["g2"](t // 2 + 1))
                    nc.vector.tensor_tensor_scan(xc[:, t, :], av[:, t, :], iv[:, t, :], 0.0, ALU.mult, ALU.add)\
                        .then_inc(SL["scan"].sem, 1)
                yield

        sig_b = [kmF[:, 512 * b:512 * b + 512].rearrange("p (a b) -> p a b", a=2) for b in range(2)]
        stages.append(("m_c", *merge_stage("m_c", STREAM["m_c"], False, sig_b,
                                           both(product_c, (lru_pe, lru_act, lru_dve, LRU)), product_c[4]), lw_load))
        product_b = product_steps(xc, gb)
        stages.append(("m_b", *merge_stage("m_b", STREAM["m_b"], False, sig_b, product_b, product_b[4], woven=1), None))

        SM = shared("split", hi=4, lo=5)

        def splitm_act(act):
            for n in range(4):
                nc.scalar.activation(h_hi[:, 4 * n:4 * n + 4, :], merged[:, 4 * n:4 * n + 4, :], ACT.Copy)\
                    .then_inc(SM["hi"].sem, 1)

        def splitm_dve(dve):
            for n in range(4):
                dve.wait_ge(*SM["hi"](n + 1))
                nc.vector.tensor_tensor(h_lo[:, 4 * n:4 * n + 4, :], merged[:, 4 * n:4 * n + 4, :],
                                        h_hi[:, 4 * n:4 * n + 4, :].bitcast(F32), ALU.subtract)\
                    .then_inc(SM["lo"].sem, 1)
            nc.vector.tensor_scalar(x[:, :, :], x[:, :, :], 2.0 ** 0.25, None, ALU.mult).then_inc(SM["lo"].sem, 1)

        residual_stage("out2", STREAM["out2"], (lambda pe: None, splitm_act, splitm_dve,
                                                lambda n: SM["lo"]((n + 1) // 2)), SM["lo"](5))

        SN = sems("ln", "sum mean cent square ssum root recip a b out")
        lsq, lmean, lsd = at(0, 4, SEQ), at(1024, SEQ), at(1280, SEQ)

        def ln_pe(pe):
            for t in range(NT):
                mm = nc.tensor.matmul(bank[4][:, 0:SEQ], ones, x[:, t, :], start=t == 0, stop=t == NT - 1)
            mm.then_inc(SN["sum"].sem, 1)
            for t in range(NT):
                pe.wait_ge(*SN["square"](t + 1))
                nc.tensor.matmul(bank[5][:, 0:SEQ], ones, lsq[:, t % 4, :], start=t == 0, stop=t == NT - 1)\
                    .then_inc(SN["ssum"].sem, 1)

        def ln_act(act):
            act.wait_ge(*SN["sum"](1))
            nc.scalar.activation(lmean, bank[4][:, 0:SEQ], ACT.Copy, scale=1.0 / DM).then_inc(SN["mean"].sem, 1)
            for t in range(NT):
                act.wait_ge(*SN["cent"](t + 1))
                if t >= 4:
                    act.wait_ge(*SN["ssum"](t - 3))
                nc.scalar.activation(lsq[:, t % 4, :], x[:, t, :], ACT.Square).then_inc(SN["square"].sem, 1)
            act.wait_ge(*SN["ssum"](NT))
            nc.scalar.activation(lsd, bank[5][:, 0:SEQ], ACT.Sqrt, bias=ln_eps_col, scale=1.0 / DM)\
                .then_inc(SN["root"].sem, 1)
            for t in range(NT):
                act.wait_ge(*SN["a"](t + 1))
                nc.scalar.activation(x[:, t, :], x[:, t, :], ACT.Identity, bias=vcol("ln_b", t)).then_inc(SN["b"].sem, 1)
                if t % 4 == 3:
                    act.wait_ge(*SN["b"](t + 1))
                    act.dma_start(out[:, t - 3:t + 1, :], x[:, t - 3:t + 1, :]).then_inc(SN["out"].sem, 16)
            act.wait_ge(*SN["out"](64))

        def ln_dve(dve):
            dve.wait_ge(*SN["mean"](1))
            for t in range(NT):
                nc.vector.tensor_tensor(x[:, t, :], x[:, t, :], lmean, ALU.subtract).then_inc(SN["cent"].sem, 1)
            dve.wait_ge(*SN["root"](1))
            nc.vector.reciprocal(lsd, lsd).then_inc(SN["recip"].sem, 1)
            dve.wait_ge(*SN["recip"](1))
            dve.wait_ge(*SN["cent"](NT))
            for t in range(NT):
                dve.wait_ge(*SN["square"](t + 1))
                nc.vector.scalar_tensor_tensor(x[:, t, :], x[:, t, :], vcol("ln_g", t), lsd, ALU.mult, ALU.mult)\
                    .then_inc(SN["a"].sem, 1)

        stages.append(("ln", ln_pe, ln_act, ln_dve, None))

        block = ctx.enter_context(nc.Block())

        def finish_stage(eng, n):
            eng.drain().then_inc(stage_done, 1)
            eng.wait_ge(stage_done, 3 * (n + 1))

        @block.sync
        def _(sp):
            for n in range(4):
                sp.dma_start(x[:, 4 * n:4 * n + 4, :], xT[:, 4 * n:4 * n + 4, :]).then_inc(S0[f"x{n}"].sem, 16)
            for s in range(RING):
                sp.dma_start(raw[:, s, :], W[s]).then_inc(raw_ready[s], 16)
            with sp.Fori(1, UNITS // RING) as i:
                for s in range(RING):
                    sp.wait_ge(lo_ready, i * RING + (s - RING + 1))
                    sp.dma_start(raw[:, s, :], W[i * RING + s]).then_inc(raw_ready[s], 16)
            for s in range(RING):
                sp.wait_ge(raw_ready[s], 16 * (UNITS // RING))

        @block.gpsimd
        def _(pool):
            for n, s in enumerate(stages):
                if s[4]:
                    if n:
                        pool.wait_ge(stage_done, 3 * n)
                    s[4](pool)

        @block.scalar
        def _(act):
            for n, s in enumerate(stages):
                s[2](act)
                finish_stage(act, n)

        @block.vector
        def _(dve):
            for n, s in enumerate(stages):
                if s[0] == "att_ac":
                    dve.wait_ge(*S0["rows"](16 * 40))
                    dve.wait_ge(*SH["sinks"](16))
                s[3](dve)
                finish_stage(dve, n)

        @block.tensor
        def _(pe):
            for n, s in enumerate(stages):
                if s[0] == "att_ac":
                    pe.wait_ge(*SH["swap"](32))
                if s[0] == "att_n":
                    pe.wait_ge(*SC["swap"](128))
                s[1](pe)
                finish_stage(pe, n)


def shape_constants():
    f = np.float32
    k, q = np.arange(P)[:, None], np.arange(P)[None, :]
    squares = np.stack([np.ones((P, P)), k // HD == q // HD, k == q, k >= q, q >= k], 1).astype(f)
    key, tok = np.arange(P)[:, None, None] + P * np.arange(2)[None, :, None], np.arange(SEQ)[None, None, :]
    before = key < tok
    dist = np.arange(P)[:, None, None] + P * np.arange(2)[None, :, None] - np.arange(SEQ)[None, None, :]

    def times(d):
        return np.where(d < 0, 0, (d <= P) * 1 + (d % 4 == 0) + (d % 16 == 0))

    def causal_tiles(v, first):
        return np.concatenate([v[:, 0, 0:first], v[:, 1, SEQ - (3 * P - first):]], 1)

    masks = np.concatenate([causal_tiles(before, SEQ), causal_tiles(np.where(before, 0, NEG), SEQ),
                            causal_tiles(times(dist), P)], 1).astype(f)
    tok2 = np.arange(P)[:, None, None] + P * np.arange(2)[None, :, None]
    cmask = (tok2 - (16 * np.arange(15)[None, None, :] + 31) >= 0).astype(f).reshape(P, 30)

    def bucket(d, most):
        d = np.maximum(d, 0)
        large = 16 + (np.log(np.maximum(d, 1).astype(f) / f(16)) / f(math.log(most / 16)) * f(16)).astype(np.int32)
        return np.where(d < 16, d, np.minimum(large, 31))

    def onehot(d, ok, most):
        t = np.zeros((33, TABW), f)
        t[np.where(ok, bucket(d, most), 32), np.arange(TABW)] = 1
        return t

    d = 255 - np.arange(TABW)
    up = np.arange(TABW) - SEQ
    onehots = np.stack([onehot(d, (d >= 0) & (d < P), 2048), onehot(d, times(d) > 0, 2048), onehot(d, d >= 0, 1024),
                        onehot(up, up >= 0, 1024)], 1)
    return squares, masks, cmask, onehots


def lay_out(i):
    a = {k: np.asarray(v) for k, v in i.items()}

    def units(w, rows_first=False):
        kk, n = w.shape
        v = w.reshape(kk // (UK * P), UK, P, n // UN, UN)
        return v.transpose((0, 3, 2, 1, 4) if rows_first else (3, 0, 2, 1, 4)).reshape(-1, P, UK * UN)

    w = a["w_in"][0]
    off = np.cumsum([0, 512, 128, 128, 512, 512, 512, 1024, 1024, 1024])
    aq, ak, av, bq, bk, bv, cq, ck, cv = (w[:, off[n]:off[n + 1]] for n in range(9))
    pad = np.zeros((DM, 256), np.float32)
    parts = [units(np.concatenate([aq, bq, bk, cq, ck, ak, av, pad, bv, cv], 1)),
             units(a["w_mem_kv_2"][0]), units(a["w_out"][0])]
    wu = a["w_up"][0]
    for c in range(11):
        parts += [units(wu[:, c * UN:(c + 1) * UN]), units(wu[:, NF * P + c * UN:NF * P + (c + 1) * UN])]
    parts.append(units(a["w_down"][0], True))
    w = a["w_in_2"][0]
    br = a["w_branch_2"][0]

    def merge(n):
        for c in range(4):
            g = 10800 + n * DM + c * UN
            yield units(w[:, g:g + UN])
            yield units(br[n][:, c * UN:(c + 1) * UN])

    parts += [units(np.concatenate([w[:, 0:1024], w[:, 2048:3072], w[:, 1024:2048]], 1))]
    parts += [units(w[:, 8752:10800]), *merge(0)]
    parts += [units(np.concatenate([w[:, 5120:6656], w[:, 6656:6912], w[:, 7168:7424], w[:, 7728:8752],
                                    w[:, 6912:7168], w[:, 7424:7680]], 1)), *merge(3)]
    parts += [units(w[:, 3072:5120]), *merge(2), *merge(1)]
    parts.append(units(a["w_out_2"][0]))

    def cols(v):
        return v.reshape(-1, P).T

    def twice(v):
        return np.concatenate([v, v])[:, None]

    def pairs(v):
        return v.reshape(16, 2, HD, -1).transpose(1, 2, 0, 3).reshape(P, -1)

    vec = [cols(a["attn_norm"][0]), cols(a["ffn_norm"][0]), cols(a["mix_out_gain"][0]), twice(a["a_q_gain"][0]),
           twice(a["a_k_gain"][0]), twice(a["c_q_gain"][0]), twice(a["c_k_gain"][0]), cols(a["conv_w"][0]),
           cols(a["conv_b"][0]), cols(a["conv_w_2"][0]), cols(a["conv_b_2"][0]), cols(a["lru_ba_2"][0]),
           cols(a["lru_bx_2"][0]), cols(a["lru_lambda_2"][0]), cols(a["ln_g_2"][0]), cols(a["ln_b_2"][0]),
           pairs(a["cmp_pe_k_2"][0]), pairs(a["cmp_pe_v_2"][0])]
    squares, masks, cmask, onehots = shape_constants()
    tabs = np.concatenate([np.concatenate([a["rel_bias_table"], a["rel_bias_2"]], 1),
                           np.full((1, 40), NEG, np.float32)], 0)

    def tiles(v):
        return v.T.reshape(-1, P, SEQ).transpose(1, 0, 2)

    return {
        "W": np.concatenate(parts, 0), "xT": tiles(a["x"][0]), "memT": tiles(a["mem_2"][0]),
        "vecs": np.concatenate(vec, 1), "squares": squares, "masks": masks, "cmask": cmask, "onehots": onehots,
        "tabs": tabs, "sinks": a["a_sinks"], "ln_rows": np.concatenate([a["sgu_ln_g_2"], a["sgu_ln_b_2"]], 1),
        "sgu_wT": a["sgu_w_2"][0].transpose(2, 0, 1), "sgu_b": a["sgu_b_2"].reshape(1, -1),
        "lru_w": np.stack([a["lru_wa_2"][0], a["lru_wx_2"][0]], 0).transpose(2, 0, 1, 3),
        "gl_w": w[:, 7680:7728].reshape(NT, P, 48).transpose(1, 0, 2), "gl_b": a["nsa_gate_b_2"],
        "cmp_w1": np.stack([pairs(a["cmp_w1_k_2"][0].reshape(32, HD, 256)),
                            pairs(a["cmp_w1_v_2"][0].reshape(32, HD, 256))], 0),
        "cmp_w2k": a["cmp_w2_k_2"][0].reshape(2, P, HD).transpose(1, 0, 2),
        "cmp_w2v": a["cmp_w2_v_2"][0].reshape(2, P, HD).transpose(1, 0, 2),
    }


def kernel(**inputs):
    from concourse import bacc
    from concourse.bass_utils import run_bass_kernel_spmd

    nc = bacc.Bacc("TRN2", target_bir_lowering=False, num_devices=1)
    arrays = {k: np.ascontiguousarray(v) for k, v in lay_out(inputs).items()}
    args = [nc.dram_tensor(k, v.shape, mybir.dt.from_np(v.dtype), kind="ExternalInput").ap()
            for k, v in arrays.items()]
    out = nc.dram_tensor("out", (P, NT, SEQ), F32, kind="ExternalOutput").ap()
    two_blocks(nc, *args, out)
    r = run_bass_kernel_spmd(nc, [arrays], core_ids=[0])
    y = r.results[0]["out"]
    return np.ascontiguousarray(y.transpose(1, 0, 2).reshape(DM, SEQ).T)[None]
```

```python
import math
from contextlib import ExitStack
from itertools import islice

import numpy as np
import concourse.bass as bass
from concourse import mybir

F32 = mybir.dt.float32
F32R = mybir.dt.float32r
ACT = mybir.ActivationFunctionType
ALU = mybir.AluOpType
AX = mybir.AxisListType.X

P = 128
SEQ = 256
DM = 2048
NT = DM // P
HD = 64
NF = 44
UK, UN = 2, 512
RING = 4
LEAD = 3
NEG = -1.0e30
TABW = 512
EPS, LN_EPS = 1e-6, 1e-5

STREAM = {}
_at = 0
for _name, _chunks, _per in (("proj", 11, 8), ("mem", 4, 8), ("wout", 4, 8), ("up", 22, 8),
                             ("down", 22, 4), ("p_a", 6, 8), ("p_m", 4, 8), ("m_a", 4, 12), ("p_c", 7, 8),
                             ("m_m", 4, 12), ("p_b", 4, 8), ("m_c", 4, 12), ("m_b", 4, 12), ("out2", 4, 8)):
    STREAM[_name] = _at
    _at += _chunks * _per
UNITS = _at

VEC = {}
_at = 0
for _name, _n in (("attn_norm", 16), ("ffn_norm", 16), ("mix_gain", 16), ("aq", 1), ("ak", 1), ("cq", 1),
                  ("ck", 1), ("conv_w", 3 * 88), ("conv_b", 88), ("conv2_w", 32), ("conv2_b", 8),
                  ("lru_ba", 8), ("lru_bx", 8), ("lru_lam", 8), ("ln_g", 16), ("ln_b", 16),
                  ("cmp_pe_k", 16), ("cmp_pe_v", 16)):
    VEC[_name] = (_at, _n)
    _at += _n
NVEC = _at


class Signal:

    def __init__(self, sem, base):
        self.sem, self.base = sem, base

    def __call__(self, n):
        return self.sem, n + self.base




def two_blocks(nc, W, xT, memT, vecs, squares, masks, cmask, onehots, tabs, sinks, ln_rows, sgu_wT, sgu_b,
               lru_w, gl_w, gl_b, cmp_w1, cmp_w2k, cmp_w2v, out):
    ctx = ExitStack()
    with ctx:
        def sb(name, shape, dt=F32):
            return ctx.enter_context(nc.sbuf_tensor(name, shape, dt))

        def sem(name):
            return ctx.enter_context(nc.semaphore(name))

        raw = sb("raw", [P, RING, UK * UN])
        w_hi = sb("w_hi", [P, RING, UK * UN], F32R)
        w_lo = sb("w_lo", [P, RING, UK * UN], F32R)
        x = sb("x", [P, NT, SEQ])
        h_hi = sb("h_hi", [P, NT, SEQ], F32R)
        h_lo = sb("h_lo", [P, NT, SEQ], F32R)
        o_hi = sb("o_hi", [P, 8, SEQ], F32R)
        o_lo = sb("o_lo", [P, 8, SEQ], F32R)
        kmT = sb("kmT", [P, 8, SEQ])
        vm = sb("vm", [P, 2, 1024])
        vec = sb("vec", [P, NVEC])
        sq_c = sb("sq_c", [P, 5, P])
        ones, blocks, ident, tri, causal = (sq_c[:, n, :] for n in range(5))
        small = sb("small", [P, 160])
        AW = 18950
        arena = sb("arena", [P, AW])
        bank = [ctx.enter_context(nc.psum_tensor(f"bank{n}", [P, 512], F32)) for n in range(8)]

        def at(off, *shape, parts=(0, P)):
            n = int(np.prod(shape))
            assert off + n <= AW, (off, shape)
            v = arena[parts[0]:parts[1], off:off + n]
            if len(shape) == 2:
                v = v.rearrange("p (a b) -> p a b", a=shape[0])
            elif len(shape) == 3:
                v = v.rearrange("p (a b c) -> p a b c", a=shape[0], b=shape[1])
            return v

        def vcol(name, n=0):
            o, cnt = VEC[name]
            assert n < cnt
            return vec[:, o + n:o + n + 1]

        row_dram = nc.dram_tensor("row_dram", (40, TABW), F32, kind="Internal").ap()
        bias_dram = nc.dram_tensor("bias_dram", (40, P, TABW), F32, kind="Internal").ap()

        raw_ready = [sem(f"raw_ready{n}") for n in range(RING)]
        hi_ready, lo_ready, unit_done = sem("hi_ready"), sem("lo_ready"), sem("unit_done")
        stage_done = sem("stage_done")

        def split_hi(act, u, j):
            s = (j + LEAD) % RING
            v = u + LEAD
            act.wait_ge(raw_ready[s], (v - s) * (16 // RING) + 16)
            if not (isinstance(v, int) and v < RING):
                act.wait_ge(unit_done, v - RING + 1)
            nc.scalar.activation(w_hi[:, s, :], raw[:, s, :], ACT.Copy).then_inc(hi_ready, 1)

        def split_lo(dve, u, j):
            s = (j + LEAD) % RING
            v = u + LEAD
            dve.wait_ge(hi_ready, v + 1)
            if not (isinstance(v, int) and v < RING):
                dve.wait_ge(unit_done, v - RING + 1)
            nc.vector.tensor_tensor(w_lo[:, s, :], raw[:, s, :], w_hi[:, s, :].bitcast(F32),
                                    ALU.subtract).then_inc(lo_ready, 1)

        def unit_features(pe, u, j, hi, lo, kt, banks, first, last, tiles=4):
            s = j % RING
            pe.wait_ge(lo_ready, u + 1)
            for k in range(UK):
                for f in range(tiles):
                    o = banks[f // 2][:, (f % 2) * SEQ:(f % 2 + 1) * SEQ]
                    cols = slice(k * UN + f * P, k * UN + (f + 1) * P)
                    for n, (w, m) in enumerate(((w_hi, hi), (w_hi, lo), (w_lo, hi))):
                        mm = nc.tensor.matmul(o, w[:, s, cols], m[:, kt + k, :],
                                              start=first and k == 0 and n == 0 and f % 2 == 0,
                                              stop=last and k == UK - 1 and n == 2, skip_group_check=True)
            return mm

        def unit_tokens(pe, u, j, kt, banks, first, last, c0=0, cols=UN, wait=True):
            s = j % RING
            if wait:
                pe.wait_ge(lo_ready, u + 1)
            for k in range(UK):
                for m in range(2):
                    for n, (w, a) in enumerate(((w_hi, h_hi), (w_lo, h_hi), (w_hi, h_lo))):
                        mm = nc.tensor.matmul(banks[m][:, 0:cols], a[:, kt + k, m * P:(m + 1) * P],
                                              w[:, s, k * UN + c0:k * UN + c0 + cols],
                                              start=first and k == 0 and n == 0,
                                              stop=last and k == UK - 1 and n == 2, skip_group_check=True)
            return mm

        def chunk_steps_pe(pe, ev, u, c, q, kind, first_two, ready=None):
            if not first_two:
                pe.wait_ge(*ev[0](c - 1))
                pe.wait_ge(*ev[1](c - 1))
            banks = bank[2 * q:2 * q + 2]
            for j in range(8):
                if ready:
                    pe.wait_ge(*ready(j + 1))
                if kind == "F":
                    mm = unit_features(pe, u + j, j, h_hi, h_lo, 2 * j, banks, j == 0, j == 7)
                elif kind == "T":
                    mm = unit_tokens(pe, u + j, j, 2 * j, banks, j == 0, j == 7)
                elif kind == "M":
                    unit_features(pe, u + j, j, h_hi, h_lo, 2 * j, banks, j == 0, j == 7, tiles=1)
                    mm = unit_tokens(pe, u + j, j, 2 * j, (banks[1], bank[4]), j == 0, j == 7, P, P, wait=False)
                mm.then_inc(unit_done, 1)
                yield

        def chunk_pe(*args):
            run(chunk_steps_pe(*args))

        def steps_pe(pe, ev, u0, kinds, ready=None, c0=0):
            for c, kind in enumerate(kinds):
                yield from chunk_steps_pe(pe, ev, u0 + 8 * c, c0 + c, (c0 + c) % 2, kind, c0 + c < 2,
                                          ready if c == 0 else None)

        def steps_act(act, ev, u0, kinds, dst, c0=0):
            for c, kind in enumerate(kinds):
                for j in range(8):
                    split_hi(act, u0 + 8 * c + j, j)
                    if j == 7:
                        act.wait_ge(unit_done, u0 + 8 * c + 8)
                        src = bank[2 * ((c0 + c) % 2)][:, 0:SEQ if kind == "M" else UN]
                        nc.scalar.activation(dst(0, c), src.rearrange("p (a b) -> p a b", a=2) if kind == "F" else src,
                                             ACT.Copy).then_inc(ev[0].sem, 1)
                    yield

        def steps_dve(dve, ev, u0, kinds, dst, c0=0):
            for c, kind in enumerate(kinds):
                for j in range(8):
                    split_lo(dve, u0 + 8 * c + j, j)
                    if j == 7:
                        dve.wait_ge(unit_done, u0 + 8 * c + 8)
                        src = bank[2 * ((c0 + c) % 2) + 1][:, 0:P if kind == "M" else UN]
                        if kind == "M":
                            nc.vector.tensor_copy(dst(2, c), bank[4][:, 0:P])
                        nc.vector.tensor_copy(dst(1, c), src.rearrange("p (a b) -> p a b", a=2) if kind == "F" else src)\
                            .then_inc(ev[1].sem, 1)
                    yield

        def to_tiles(dst):
            return lambda half, c: dst[:, 4 * c + 2 * half:4 * c + 2 * half + 2, :]

        def chunk_split(eng, split, u, beside=None):
            for j in range(8):
                split(eng, u + j, j)
                if beside:
                    next(beside, None)

        def F_act(act, ev, u, q, dst):
            act.wait_ge(unit_done, u + 8)
            nc.scalar.activation(dst, bank[2 * q][:, :].rearrange("p (a b) -> p a b", a=2),
                                 ACT.Copy).then_inc(ev[0].sem, 1)

        def F_dve(dve, ev, u, q, dst):
            dve.wait_ge(unit_done, u + 8)
            nc.vector.tensor_copy(dst, bank[2 * q + 1][:, :].rearrange("p (a b) -> p a b", a=2))\
                .then_inc(ev[1].sem, 1)

        def features_pe(pe, ev, u0, chunks, ready=None):
            chunk_pe(pe, ev, u0, 0, 0, "F", True, ready)
            chunk_pe(pe, ev, u0 + 8, 1, 1, "F", True)
            if chunks >= 4:
                with pe.Fori(1, chunks // 2) as i:
                    for q in range(2):
                        chunk_pe(pe, ev, i * 16 + (u0 + 8 * q), i * 2 + q, q, "F", False)
            if chunks % 2:
                chunk_pe(pe, ev, u0 + 8 * (chunks - 1), chunks - 1, 0, "F", False)

        def features_act(act, ev, u0, chunks, dst, t0=0, beside=None):
            for q in range(2):
                chunk_split(act, split_hi, u0 + 8 * q, beside)
                F_act(act, ev, u0 + 8 * q, q, dst[:, t0 + 4 * q:t0 + 4 * q + 2, :])
            if chunks >= 4:
                with act.Fori(1, chunks // 2) as i:
                    for q in range(2):
                        chunk_split(act, split_hi, i * 16 + (u0 + 8 * q))
                        F_act(act, ev, i * 16 + (u0 + 8 * q), q, dst[:, bass.ds(i * 8 + (t0 + 4 * q), 2), :])
            if chunks % 2:
                u, t = u0 + 8 * (chunks - 1), t0 + 4 * (chunks - 1)
                chunk_split(act, split_hi, u)
                F_act(act, ev, u, 0, dst[:, t:t + 2, :])

        def features_dve(dve, ev, u0, chunks, dst, t0=0, beside=None):
            for q in range(2):
                chunk_split(dve, split_lo, u0 + 8 * q, beside)
                F_dve(dve, ev, u0 + 8 * q, q, dst[:, t0 + 4 * q + 2:t0 + 4 * q + 4, :])
            if chunks >= 4:
                with dve.Fori(1, chunks // 2) as i:
                    for q in range(2):
                        chunk_split(dve, split_lo, i * 16 + (u0 + 8 * q))
                        F_dve(dve, ev, i * 16 + (u0 + 8 * q), q, dst[:, bass.ds(i * 8 + (t0 + 4 * q + 2), 2), :])
            if chunks % 2:
                u, t = u0 + 8 * (chunks - 1), t0 + 4 * (chunks - 1) + 2
                chunk_split(dve, split_lo, u)
                F_dve(dve, ev, u, 0, dst[:, t:t + 2, :])

        def tokens_pe(pe, ev, u0, c0, chunks):
            for c in range(chunks):
                chunk_pe(pe, ev, u0 + 8 * c, c0 + c, (c0 + c) % 2, "T", c0 + c < 2)

        def tokens_act(act, ev, u0, c0, chunks, dst):
            for c in range(chunks):
                chunk_split(act, split_hi, u0 + 8 * c)
                act.wait_ge(unit_done, u0 + 8 * c + 8)
                nc.scalar.activation(dst(0, c), bank[2 * ((c0 + c) % 2)][:, :], ACT.Copy).then_inc(ev[0].sem, 1)

        def tokens_dve(dve, ev, u0, c0, chunks, dst):
            for c in range(chunks):
                chunk_split(dve, split_lo, u0 + 8 * c)
                dve.wait_ge(unit_done, u0 + 8 * c + 8)
                nc.vector.tensor_copy(dst(1, c), bank[2 * ((c0 + c) % 2) + 1][:, :]).then_inc(ev[1].sem, 1)

        pool_of_signals = {}

        def sems(stage, names):
            return {n: Signal(sem(f"{stage}_{n}"), 0) for n in names.split()}

        def shared(kind, **totals):
            got = {}
            for n, total in totals.items():
                if (kind, n) not in pool_of_signals:
                    pool_of_signals[kind, n] = [sem(f"{kind}_{n}"), 0]
                s, before = pool_of_signals[kind, n]
                got[n] = Signal(s, before)
                pool_of_signals[kind, n][1] = before + total
            return got

        def halves(chunks):
            S = shared("read", by_act=chunks, by_dve=chunks)
            return S["by_act"], S["by_dve"]

        def rms_pe(pe, S, sq, groups):
            for g, (a, n) in enumerate(groups):
                for t in range(a, a + n):
                    pe.wait_ge(*S["square"](t // 2 + 1))
                    mm = nc.tensor.matmul(bank[4 + g][:, 0:SEQ], ones, sq[:, t, :], start=t == a, stop=t == a + n - 1)
                mm.then_inc(S["sum"].sem, 1)

        def rms_act(act, S, src, sq, sd, groups, arrived=None, between=None):
            def root(g):
                act.wait_ge(*S["sum"](g + 1))
                nc.scalar.activation(sd[:, g, :], bank[4 + g][:, 0:SEQ], ACT.Sqrt, bias=eps_col,
                                     scale=1.0 / (groups[g][1] * P)).then_inc(S["root"].sem, 1)

            for g, (a, n) in enumerate(groups):
                for t in range(a, a + n, 2):
                    if arrived:
                        arrived(act, t)
                    nc.scalar.activation(sq[:, t:t + 2, :], src[:, t:t + 2, :], ACT.Square).then_inc(S["square"].sem, 1)
                if g:
                    root(g - 1)
            if between:
                between(act)
            root(len(groups) - 1)

        def rms_dve(dve, S, src, sd, tmp, gain, groups, put_lo):
            for g, (a, n) in enumerate(groups):
                dve.wait_ge(*S["root"](g + 1))
                nc.vector.reciprocal(sd[:, g, :], sd[:, g, :]).then_inc(S["recip"].sem, 1)
                dve.wait_ge(*S["recip"](g + 1))
                for t in range(a, a + n):
                    nc.vector.scalar_tensor_tensor(tmp[:, t, :], src[:, t, :], vcol(gain, t), sd[:, g, :],
                                                   ALU.mult, ALU.mult).then_inc(S["scaled"].sem, 1)
                    if t % 2:
                        if t > 1:
                            put_lo(t // 2 - 1)
                        yield
            put_lo(NT // 2 - 1)

        def to_moving_act(act, S, tmp, hi, pairs):
            for p in range(pairs):
                act.wait_ge(*S["scaled"](2 * p + 2))
                nc.scalar.activation(hi[:, 2 * p:2 * p + 2, :], tmp[:, 2 * p:2 * p + 2, :], ACT.Copy)\
                    .then_inc(S["hi"].sem, 1)
                yield

        def to_moving_dve(dve, S, tmp, hi, lo):
            def put(p):
                dve.wait_ge(*S["hi"](p + 1))
                nc.vector.tensor_tensor(lo[:, 2 * p:2 * p + 2, :], tmp[:, 2 * p:2 * p + 2, :],
                                        hi[:, 2 * p:2 * p + 2, :].bitcast(F32), ALU.subtract)\
                    .then_inc(S["lo"].sem, 1)
            return put

        eps_col, ln_eps_col = small[:, 150:151], small[:, 151:152]

        def weave(main, n_main, side, n_side, start=0):
            done = 0
            for k, _ in enumerate(main):
                while done < n_side and done * (n_main - start) < (k + 1 - start) * n_side:
                    next(side)
                    done += 1
            for _ in side:
                done += 1
            assert done == n_side, (done, n_side)

        def run(steps):
            for _ in steps:
                pass

        def then(*parts):
            for p in parts:
                yield from p
        stages = []

        S0 = sems("start", "e x0 x1 x2 x3 c v t m r_pe r_act table rows hi lo")
        oh = at(11008, 3, TABW, parts=(0, 33))
        tb = at(12544, 40, parts=(0, 33))
        rows = [at(12608 + 512 * n, TABW, parts=(0, r)) for n, r in enumerate((8, 16, 16))]
        tab_cols = ((0, 8), (8, 24), (24, 40))
        vm_tiles = vm[:, :, :].rearrange("p a b -> p (a b)").rearrange("p (a b) -> p a b", a=8)

        def start_load(pool):
            pool.dma_start(vec[:, :], vecs).then_inc(S0["v"].sem, 16)
            pool.dma_start(oh, onehots[:, 0:3, :]).then_inc(S0["t"].sem, 16)
            pool.dma_start(tb, tabs).then_inc(S0["t"].sem, 16)
            pool.dma_start(kmT[:, :, :], memT[:, 0:8, :]).then_inc(S0["m"].sem, 16)
            pool.dma_start(vm_tiles, memT[:, 8:16, :]).then_inc(S0["m"].sem, 16)
            pool.wait_ge(*S0["r_act"](3))
            for n, (a, b) in enumerate(tab_cols):
                pool.dma_start(row_dram[a:b], rows[n]).then_inc(S0["table"].sem, 16)
            pool.wait_ge(*S0["table"](48))
            for h in range(40):
                pool.dma_start(bias_dram[h], row_dram[h:h + 1].broadcast_to([P, TABW]))\
                    .then_inc(S0["rows"].sem, 16)
            pool.wait_ge(*S0["rows"](16 * 40))

        def start_pe(pe):
            pe.wait_ge(*S0["c"](16))

        def start_act(act):
            act.wait_ge(*S0["e"](2))

        def x_arrived(act, t):
            if t % 4 == 0:
                act.wait_ge(*S0[f"x{t // 4}"](16))

        def first_split_act(act):
            for u in range(LEAD):
                act.wait_ge(raw_ready[u], 16)
                nc.scalar.activation(w_hi[:, u, :], raw[:, u, :], ACT.Copy).then_inc(hi_ready, 1)

        def start_dve(dve):
            nc.vector.memset(eps_col, EPS).then_inc(S0["e"].sem, 1)
            nc.vector.memset(ln_eps_col, LN_EPS).then_inc(S0["e"].sem, 1)
            for u in range(LEAD):
                dve.wait_ge(hi_ready, u + 1)
                nc.vector.tensor_tensor(w_lo[:, u, :], raw[:, u, :], w_hi[:, u, :].bitcast(F32),
                                        ALU.subtract).then_inc(lo_ready, 1)
            dve.wait_ge(*S0["v"](16))

        def rows_pe(pe):
            pe.wait_ge(*S0["t"](32))
            for n, (a, b) in enumerate(tab_cols):
                nc.tensor.matmul(bank[5 + n][0:b - a, :], tb[:, a:b], oh[:, n, :], start=True, stop=True)\
                    .then_inc(S0["r_pe"].sem, 1)

        def rows_act(act):
            for n, (a, b) in enumerate(tab_cols):
                act.wait_ge(*S0["r_pe"](n + 1))
                nc.scalar.activation(rows[n], bank[5 + n][0:b - a, :], ACT.Copy).then_inc(S0["r_act"].sem, 1)

        AHEAD = 4

        def norm_parts(src, gain, groups, tmp, sq, sd, arrived=None, between=None, early=False):
            G = len(groups)
            S = shared("norm", square=NT // 2, sum=G, root=G, recip=G, scaled=NT, hi=NT // 2, lo=NT // 2)

            def four_pe(pe, c, ev):
                for t in range(4 * c, 4 * c + 4):
                    pe.wait_ge(*S["square"](t // 2 + 1))
                    mm = nc.tensor.matmul(bank[4][:, 0:SEQ], ones, sq[:, t, :], start=t == 0, stop=t == NT - 1)
                if c == 3:
                    mm.then_inc(S["sum"].sem, 1)

            def four_act(act, c, ev):
                act.wait_ge(*ev(2 * c + 2))
                for t in (4 * c, 4 * c + 2):
                    nc.scalar.activation(sq[:, t:t + 2, :], src[:, t:t + 2, :], ACT.Square)\
                        .then_inc(S["square"].sem, 1)

            def pe_(pe):
                if not early:
                    rms_pe(pe, S, sq, groups)

            def act_(act):
                if early:
                    act.wait_ge(*S["sum"](1))
                    nc.scalar.activation(sd[:, 0, :], bank[4][:, 0:SEQ], ACT.Sqrt, bias=eps_col, scale=1.0 / DM)\
                        .then_inc(S["root"].sem, 1)
                else:
                    rms_act(act, S, src, sq, sd, groups, arrived, between)
                steps = to_moving_act(act, S, tmp, h_hi, NT // 2)
                run(islice(steps, AHEAD))
                return steps

            def dve_(dve):
                steps = rms_dve(dve, S, src, sd, tmp, gain, groups, to_moving_dve(dve, S, tmp, h_hi, h_lo))
                run(islice(steps, AHEAD))
                return steps

            return pe_, act_, dve_, S["lo"], four_pe, four_act

        norm1 = norm_parts(x, "attn_norm", [(0, NT)], at(0, NT, SEQ), at(4096, NT, SEQ), at(8192, 3, SEQ),
                           x_arrived, first_split_act)

        qk = at(0, 30, SEQ)
        v1 = at(7680, 2, 1664)
        oT = at(11008, NT, SEQ)
        WK = 15104
        CW3 = 3 * P
        rings = at(WK, 4, CW3), at(WK + 4 * CW3, 2, CW3)
        bias_ac = [at(WK + (6 + n) * CW3, CW3) for n in range(2)]
        count = at(WK + 8 * CW3, CW3)
        ev_proj = halves(11)
        UP = STREAM["proj"]

        def proj_dst(half, c):
            if c < 2:
                return to_tiles(qk)(half, 5 + c)
            if c == 2:
                return qk[:, 28, :] if half == 0 else v1[:, half - 1, 0:P]
            return v1[:, half, P + (c - 3) * UN:P + (c - 2) * UN]

        def proj_pe(pe):
            start_pe(pe)
            norm1[0](pe)
            rows_pe(pe)
            features_pe(pe, ev_proj, UP, 5, norm1[3])
            weave(steps_pe(pe, ev_proj, UP + 40, "FFMTTT", None, 5), 48, head_pe(pe), NP + 2)

        def proj_act(act):
            start_act(act)
            steps = norm1[1](act)
            rows_act(act)
            features_act(act, ev_proj, UP, 5, qk, beside=steps)
            weave(steps_act(act, ev_proj, UP + 40, "FFMTTT", proj_dst, 5), 48, head_act(act), NP + 2)

        def proj_dve(dve):
            start_dve(dve)
            features_dve(dve, ev_proj, UP, 5, qk, beside=norm1[2](dve))
            weave(steps_dve(dve, ev_proj, UP + 40, "FFMTTT", proj_dst, 5), 48, head_dve(dve), NP + 2)

        ev_mem = halves(4)
        UM = STREAM["mem"]
        mem = {}
        MEM_UNITS = 22, 10

        def mem_dst(half, c):
            return to_tiles(kmT)(half, c) if c < 2 else vm[:, half, (c - 2) * UN:(c - 1) * UN]

        def mem_pe(pe):
            mem["pe"] = steps_pe(pe, ev_mem, UM, "FFTT", lambda n: S0["lo"]((n + 1) // 2))

        def mem_act(act):
            act.wait_ge(*S0["m"](32))
            for n in range(4):
                src = kmT[:, 4 * n:4 * n + 4, :] if n < 2 else vm_tiles[:, 4 * n - 8:4 * n - 4, :]
                nc.scalar.activation(h_hi[:, 4 * n:4 * n + 4, :], src, ACT.Copy).then_inc(S0["hi"].sem, 1)
            mem["act"] = steps_act(act, ev_mem, UM, "FFTT", mem_dst)

        def mem_dve(dve):
            for n in range(4):
                src = kmT[:, 4 * n:4 * n + 4, :] if n < 2 else vm_tiles[:, 4 * n - 8:4 * n - 4, :]
                dve.wait_ge(*S0["hi"](n + 1))
                nc.vector.tensor_tensor(h_lo[:, 4 * n:4 * n + 4, :], src, h_hi[:, 4 * n:4 * n + 4, :].bitcast(F32),
                                        ALU.subtract).then_inc(S0["lo"].sem, 1)
            mem["dve"] = steps_dve(dve, ev_mem, UM, "FFTT", mem_dst)

        def beside(main, n_main, side, n_side):
            weave(islice(main, n_main), n_main, side, n_side)

        SH = sems("headnorm", "square sum root recip scaled swap sinks")
        pairs = [(0, 2, "aq"), (2, 2, "aq")] + [(t, 2, "cq") for t in range(12, 20, 2)] \
            + [(20, 2, "ck"), (22, 2, "ck"), (28, 1, "ak"), (24, 2, "ck"), (26, 2, "ck")]
        hsq, hsd = at(WK, 2, 2, SEQ), at(WK + 1024, 2, 2, SEQ)
        sink_col = small[:, 0:8]

        def proj_load(pool):
            start_load(pool)
            pool.dma_start(sink_col, sinks.broadcast_to([P, 8])).then_inc(SH["sinks"].sem, 16)
            pool.wait_ge(*SH["scaled"](sum(p[1] for p in pairs[:pairs.index((28, 1, "ak")) + 1])))
            pool.dma_start(qk[HD:P, 29, :], qk[0:HD, 28, :]).then_inc(SH["swap"].sem, 16)
            pool.dma_start(qk[0:HD, 29, :], qk[HD:P, 28, :]).then_inc(SH["swap"].sem, 16)

        NP = len(pairs)

        def head_pe(pe):
            for n in range(NP + 2):
                if n < NP:
                    k = pairs[n][1]
                    pe.wait_ge(*SH["square"](n + 1))
                    if n >= 2:
                        pe.wait_ge(*SH["root"](n - 1))
                    nc.tensor.matmul(bank[6 + n % 2][:, 0:k * SEQ], blocks,
                                     hsq[:, n % 2, 0:k, :].rearrange("p a b -> p (a b)"), start=True, stop=True)\
                        .then_inc(SH["sum"].sem, 1)
                yield

        def head_act(act):
            for n in range(NP + 2):
                if n < NP:
                    t, k, _ = pairs[n]
                    act.wait_ge(*ev_proj[0](t // 4 + 1))
                    act.wait_ge(*ev_proj[1](t // 4 + 1))
                    if n >= 2:
                        act.wait_ge(*SH["sum"](n - 1))
                    nc.scalar.activation(hsq[:, n % 2, 0:k, :], qk[:, t:t + k, :], ACT.Square)\
                        .then_inc(SH["square"].sem, 1)
                if 1 <= n <= NP:
                    k = pairs[n - 1][1]
                    act.wait_ge(*SH["sum"](n))
                    if n >= 3:
                        act.wait_ge(*SH["scaled"](sum(p[1] for p in pairs[:n - 2])))
                    nc.scalar.activation(hsd[:, (n - 1) % 2, 0:k, :],
                                         bank[6 + (n - 1) % 2][:, 0:k * SEQ].rearrange("p (a b) -> p a b", a=k),
                                         ACT.Sqrt, bias=eps_col, scale=1.0 / HD).then_inc(SH["root"].sem, 1)
                yield

        def head_dve(dve):
            for step in range(NP + 2):
                n = step - 2
                if n >= 0:
                    t, k, gain = pairs[n]
                    dve.wait_ge(*SH["root"](n + 1))
                    nc.vector.reciprocal(hsd[:, n % 2, 0:k, :], hsd[:, n % 2, 0:k, :]).then_inc(SH["recip"].sem, 1)
                    dve.wait_ge(*SH["recip"](n + 1))
                    for j in range(k):
                        nc.vector.scalar_tensor_tensor(qk[:, t + j, :], qk[:, t + j, :], vcol(gain),
                                                       hsd[:, n % 2, j, :], ALU.mult, ALU.mult)\
                            .then_inc(SH["scaled"].sem, 1)
                yield

        stages.append(("proj", proj_pe, proj_act, proj_dve, proj_load))

        sinks_signal, tiles_signal = Signal(sem("sinks_negated"), 0), Signal(sem("stage_tiles"), 0)

        def softmax(jobs, scale, evac, rings, bias=None, load_extra=None):
            J = len(jobs)
            lp, pt = rings
            loads = sum(j.get("load") is not None for j in jobs)
            S = shared("softmax", score=J, logit=J, peak=J, neg=J, prob=J,
                       weight=sum(j.get("weights") is not None for j in jobs),
                       sum=sum(bool(j.get("floor")) + (j.get("sink") is not None) for j in jobs),
                       recip=J, norm=J, transposed=J, probT=J, out=J, evac=sum(j["last"] for j in jobs),
                       bias0=32 * ((loads + 1) // 2), bias1=32 * (loads // 2))
            nb = heads = weights = sums = 0
            for n, j in enumerate(jobs):
                nb += j.get("load") is not None
                j["bias_n"] = nb
                j["heads"] = heads
                heads += j["last"]
                j["weight_n"] = weights = weights + (j.get("weights") is not None)
                j["sum_n"] = sums
                sums += bool(j.get("floor")) + (j.get("sink") is not None)
            mx, ng, sm, rc, es, wsm = (small[:, 8 + 8 * k:16 + 8 * k].rearrange("p (a b) -> p a b", a=4)
                                       for k in range(6))
            nsink = small[:, 56:64]

            def load(pool):
                if load_extra:
                    load_extra(pool, tiles_signal)
                for n, j in enumerate(jobs):
                    if j.get("load") is None:
                        continue
                    b = (j["bias_n"] - 1) % 2
                    users = [m for m, o in enumerate(jobs) if o.get("buf") is not None
                             and o["bias_n"] == j["bias_n"] - 2]
                    if users:
                        pool.wait_ge(*S["logit"](users[-1] + 1))
                    g = bias_dram[j["load"]].rearrange("a b -> (a b)")
                    for m in range(2):
                        pool.dma_start(bias[b][:, m * P:P + 2 * m * P], bass.AP(
                            tensor=g.tensor, offset=g.offset + 255 - P * m, ap=[[TABW - 1, P], [1, P + P * m]]))\
                            .then_inc(S[f"bias{b}"].sem, 16)

            def pe_(pe):
                for slot in range(J + 8):
                    n = slot
                    if 0 <= n < J:
                        if n >= 2:
                            pe.wait_ge(*S["logit"](n - 1))
                        for m, (c, w) in enumerate(jobs[n]["segs"]):
                            ops = jobs[n]["scores"](m)
                            for i, (q, k) in enumerate(ops):
                                mm = nc.tensor.matmul(bank[4 + n % 2][:, c:c + w], q, k, start=i == 0,
                                                      stop=i == len(ops) - 1)
                        mm.then_inc(S["score"].sem, 1)
                    n = slot - 6
                    if 0 <= n < J:
                        j = jobs[n]
                        pe.wait_ge(*S["probT"](n + 1))
                        if j["heads"] >= j["out_regions"]:
                            pe.wait_ge(*S["evac"](j["heads"] - j["out_regions"] + 1))
                        for mm in j["pv"](pt[:, n % 2, :]):
                            pass
                        mm.then_inc(S["out"].sem, 1)
                    n = slot - 4
                    if 0 <= n < J:
                        pe.wait_ge(*S["norm"](n + 1))
                        if n >= 1:
                            pe.wait_ge(*S["probT"](n))
                        for t, (c, kw) in enumerate(jobs[n]["parts"]):
                            mm = nc.tensor.transpose(bank[6][0:kw, t * P:(t + 1) * P], lp[:, n % 4, c:c + kw], ident)
                        mm.then_inc(S["transposed"].sem, 1)
                    yield

            def act_(act):
                for slot in range(J + 8):
                    n = slot - 5
                    if 0 <= n < J:
                        j = jobs[n]
                        kw, cnt = j["parts"][0][1], len(j["parts"])
                        act.wait_ge(*S["transposed"](n + 1))
                        if n >= 2:
                            act.wait_ge(*S["out"](n - 1))
                        nc.scalar.activation(pt[0:kw, n % 2, 0:cnt * P], bank[6][0:kw, 0:cnt * P], ACT.Copy)\
                            .then_inc(S["probT"].sem, 1)
                    n = slot - 2
                    if 0 <= n < J:
                        j = jobs[n]
                        act.wait_ge(*S["neg"](n + 1))
                        for m, (c, w) in enumerate(j["segs"]):
                            i = nc.scalar.activation(lp[:, n % 4, c:c + w], lp[:, n % 4, c:c + w], ACT.Exp,
                                                     bias=ng[:, n % 4, m:m + 1], accum_out=sm[:, n % 4, m:m + 1])
                        if j.get("sink") is not None:
                            i = nc.scalar.activation(es[:, n % 4, :], ng[:, n % 4, :], ACT.Exp,
                                                     bias=sink_col[:, j["sink"]:j["sink"] + 1])
                        i.then_inc(S["prob"].sem, 1)
                    yield

            def dve_(dve):
                if jobs[0].get("sink") is not None:
                    nc.vector.tensor_scalar(nsink, sink_col, -1.0, None, ALU.mult).then_inc(sinks_signal.sem, 1)
                    dve.wait_ge(*sinks_signal(1))
                if load_extra:
                    dve.wait_ge(*tiles_signal(16))
                for slot in range(J + 8):
                    n = slot - 7
                    if 0 <= n < J and jobs[n]["last"]:
                        dve.wait_ge(*S["out"](n + 1))
                        evac(jobs[n]["heads"]).then_inc(S["evac"].sem, 1)
                    n = slot - 1
                    if 0 <= n < J:
                        j = jobs[n]
                        segs = j["segs"]
                        w = segs[1][0] + segs[1][1]
                        dve.wait_ge(*S["score"](n + 1))
                        if n >= 4:
                            dve.wait_ge(*S["transposed"](n - 3))
                        lg = lp[:, n % 4, 0:w]
                        if j.get("buf") is not None or j.get("tile") is not None:
                            if j.get("buf") is not None:
                                dve.wait_ge(*S[f"bias{j['buf']}"](32 * ((j["bias_n"] + 1) // 2)))
                            b = bias[j["buf"]] if j.get("buf") is not None else j["tile"]
                            i = nc.vector.scalar_tensor_tensor(lg, bank[4 + n % 2][:, 0:w], scale, b, ALU.mult, ALU.add)
                        else:
                            i = nc.vector.tensor_scalar(lg, bank[4 + n % 2][:, 0:w], scale, None, ALU.mult)
                        i.then_inc(S["logit"].sem, 1)
                        dve.wait_ge(*S["logit"](n + 1))
                        if segs[0][1] == segs[1][1]:
                            i = nc.vector.tensor_reduce(mx[:, n % 4, :], lg.rearrange("p (a b) -> p a b", a=2), AX, ALU.max)
                        else:
                            for m, (c, w) in enumerate(segs):
                                i = nc.vector.tensor_reduce(mx[:, n % 4, m:m + 1], lp[:, n % 4, c:c + w], AX, ALU.max)
                        i.then_inc(S["peak"].sem, 1)
                        dve.wait_ge(*S["peak"](n + 1))
                        if j.get("sink") is not None:
                            i = nc.vector.tensor_scalar(ng[:, n % 4, :], mx[:, n % 4, :], -1.0,
                                                        nsink[:, j["sink"]:j["sink"] + 1], ALU.mult, ALU.min)
                        else:
                            i = nc.vector.tensor_scalar(ng[:, n % 4, :], mx[:, n % 4, :], -1.0, None, ALU.mult)
                        i.then_inc(S["neg"].sem, 1)
                    n = slot - 3
                    if 0 <= n < J:
                        j = jobs[n]
                        dve.wait_ge(*S["prob"](n + 1))
                        s, added = sm[:, n % 4, :], j["sum_n"]
                        if j.get("weights") is not None:
                            for m, (c, w) in enumerate(j["segs"]):
                                i = nc.vector.scalar_tensor_tensor(lp[:, n % 4, c:c + w], lp[:, n % 4, c:c + w], 1.0,
                                                                   j["weights"][:, c:c + w], ALU.mult, ALU.mult,
                                                                   accum_out=wsm[:, n % 4, m:m + 1])
                            i.then_inc(S["weight"].sem, 1)
                            dve.wait_ge(*S["weight"](j["weight_n"]))
                            s = wsm[:, n % 4, :]
                        if j.get("floor"):
                            nc.vector.tensor_scalar(s, s, 1e-30, None, ALU.max).then_inc(S["sum"].sem, 1)
                            added += 1
                            dve.wait_ge(*S["sum"](added))
                        if j.get("sink") is not None:
                            nc.vector.tensor_tensor(s, s, es[:, n % 4, :], ALU.add).then_inc(S["sum"].sem, 1)
                            added += 1
                            dve.wait_ge(*S["sum"](added))
                        nc.vector.reciprocal(rc[:, n % 4, :], s).then_inc(S["recip"].sem, 1)
                        dve.wait_ge(*S["recip"](n + 1))
                        gate = j.get("gate")
                        for m, (c, w) in enumerate(j["segs"]):
                            i = nc.vector.tensor_scalar(lp[:, n % 4, c:c + w], lp[:, n % 4, c:c + w],
                                                        rc[:, n % 4, m:m + 1],
                                                        gate[:, m:m + 1] if gate is not None else None, ALU.mult,
                                                        ALU.mult if gate is not None else ALU.bypass)
                        i.then_inc(S["norm"].sem, 1)
                    yield

            return pe_, act_, dve_, load, J + 8

        CAUSAL = dict(segs=[(0, P), (P, SEQ)], parts=[(0, P), (P, P), (2 * P, P)])

        def causal_pv(dst, val, start, stop):
            def go(pt):
                yield nc.tensor.matmul(dst(0), val(0), pt[:, 0:P], start=start, stop=stop, skip_group_check=True)
                yield nc.tensor.matmul(dst(1), val(0), pt[:, P:2 * P], start=False, stop=False, skip_group_check=True)
                yield nc.tensor.matmul(dst(1), val(1), pt[:, 2 * P:3 * P], start=False, stop=stop,
                                       skip_group_check=True)
            return go

        def head_dst(h):
            return lambda m: bank[7][HD * (h % 2):HD * (h % 2) + HD, m * P:(m + 1) * P]

        def head_evac(dst):
            return lambda h: nc.vector.tensor_copy(dst(h), bank[7][HD * (h % 2):HD * (h % 2) + HD, 0:SEQ])

        def a_job(h):
            p, kv = h % 2, h // 4
            rows_ = slice(HD * p, HD * p + HD)
            return dict(scores=lambda m: [(qk[rows_, h // 2, m * P:(m + 1) * P],
                                           qk[rows_, 28 if kv % 2 == p else 29, 0:P + m * P])],
                        load=h, buf=h % 2, sink=h, last=True, out_regions=2, **CAUSAL,
                        pv=causal_pv(head_dst(h), lambda kt: v1[:, kt, kv * HD:(kv + 1) * HD], True, True))

        SB = sems("att_b", "mask score zs zm small log soft masked arg suffix arg2 w out evac neg")
        m01 = at(WK + 9 * CW3, CW3)

        def count_load(pool, signal):
            pool.dma_start(count, masks[:, CW3:2 * CW3]).then_inc(signal.sem, 16)
            pool.dma_start(m01, masks[:, 0:CW3]).then_inc(SB["mask"].sem, 16)

        def c_job(h):
            rows_ = slice(HD * (h % 2), HD * (h % 2) + HD)
            return dict(scores=lambda m: [(qk[rows_, 12 + h // 2, m * P:(m + 1) * P],
                                           qk[rows_, 20 + h // 2, 0:P + m * P])],
                        load=8 + h, buf=h % 2, weights=count, last=True, out_regions=2, **CAUSAL,
                        pv=causal_pv(head_dst(h), lambda kt: v1[:, kt, 640 + h * HD:640 + (h + 1) * HD], True, True))

        def dst_ac(h):
            return oT[HD * (h % 2):HD * (h % 2) + HD, h // 2 if h < 8 else 4 + h // 2, :]

        att_ac = softmax([a_job(h) for h in range(8)] + [c_job(h) for h in range(16)], HD ** -0.5,
                         head_evac(dst_ac), rings, bias_ac, count_load)
        SLOTS_BEFORE = 3

        def att_ac_pe(pe):
            slots = att_ac[0](pe)
            run(islice(slots, SLOTS_BEFORE))
            mem_pe(pe)
            beside(mem["pe"], MEM_UNITS[0], slots, att_ac[4] - SLOTS_BEFORE)

        def att_ac_act(act):
            slots = att_ac[1](act)
            run(islice(slots, SLOTS_BEFORE))
            mem_act(act)
            beside(mem["act"], MEM_UNITS[0], slots, att_ac[4] - SLOTS_BEFORE)

        def att_ac_dve(dve):
            slots = att_ac[2](dve)
            run(islice(slots, SLOTS_BEFORE))
            mem_dve(dve)
            beside(mem["dve"], MEM_UNITS[0], slots, att_ac[4] - SLOTS_BEFORE)

        stages.append(("att_ac", att_ac_pe, att_ac_act, att_ac_dve, att_ac[3]))

        mneg = at(WK, CW3)
        spr = at(WK + 2 * CW3, 4, CW3)
        zr = at(12 * SEQ, 7, CW3)
        BH = 8

        def b_pe(pe):
            for slot in range(BH + 9):
                h = slot
                if 0 <= h < BH:
                    rows_ = slice(HD * (h % 2), HD * (h % 2) + HD)
                    if h >= 2:
                        pe.wait_ge(*SB["zs"](h - 1))
                    for kt in range(2):
                        mm = nc.tensor.matmul(bank[4 + h % 2][:, kt * SEQ:SEQ + kt * P],
                                              qk[rows_, 8 + h // 2, kt * P:(kt + 1) * P],
                                              qk[rows_, 4 + h // 2, kt * P:SEQ], start=True, stop=True)
                    mm.then_inc(SB["score"].sem, 1)
                h = slot - 7
                if 0 <= h < BH:
                    pe.wait_ge(*SB["w"](h + 1))
                    if h >= 2:
                        pe.wait_ge(*SB["evac"](h - 1))
                    o = bank[7][HD * (h % 2):HD * (h % 2) + HD, :]
                    w = zr[:, h % 7, :]
                    nc.tensor.matmul(o[:, 0:SEQ], v1[:, 0, P + h * HD:P + (h + 1) * HD], w[:, 0:SEQ],
                                     start=True, stop=False, skip_group_check=True)
                    nc.tensor.matmul(o[:, P:SEQ], v1[:, 1, P + h * HD:P + (h + 1) * HD], w[:, SEQ:CW3],
                                     start=False, stop=True, skip_group_check=True).then_inc(SB["out"].sem, 1)
                h = slot - 4
                if 0 <= h < BH:
                    pe.wait_ge(*SB["masked"](h + 1))
                    if h >= 1:
                        pe.wait_ge(*SB["arg2"](h))
                    sp = spr[:, h % 4, :]
                    nc.tensor.matmul(bank[6][:, 0:SEQ], tri, sp[:, 0:SEQ], start=True, stop=False,
                                     skip_group_check=True)
                    nc.tensor.matmul(bank[6][:, P:SEQ], ones, sp[:, SEQ:CW3], start=False, stop=True,
                                     skip_group_check=True)
                    nc.tensor.matmul(bank[6][:, SEQ:CW3], tri, sp[:, SEQ:CW3], start=False, stop=True,
                                     skip_group_check=True).then_inc(SB["suffix"].sem, 1)
                yield

        def b_act(act):
            for slot in range(BH + 9):
                h = slot - 6
                if 0 <= h < BH:
                    act.wait_ge(*SB["arg2"](h + 1))
                    nc.scalar.activation(zr[:, h % 7, :], zr[:, h % 7, :], ACT.Exp).then_inc(SB["w"].sem, 1)
                h = slot - 2
                if 0 <= h < BH:
                    act.wait_ge(*SB["zm"](h + 1))
                    nc.scalar.activation(spr[:, h % 4, :], spr[:, h % 4, :], ACT.Exp).then_inc(SB["small"].sem, 1)
                    act.wait_ge(*SB["small"](h + 1))
                    nc.scalar.activation(spr[:, h % 4, :], spr[:, h % 4, :], ACT.Ln, bias=1.0)\
                        .then_inc(SB["log"].sem, 1)
                yield

        def b_dve(dve):
            dve.wait_ge(*SB["mask"](16))
            nc.vector.tensor_scalar(mneg, m01, -NEG, NEG, ALU.mult, ALU.add).then_inc(SB["neg"].sem, 1)
            dve.wait_ge(*SB["neg"](1))
            for slot in range(BH + 9):
                h = slot - 8
                if 0 <= h < BH:
                    dve.wait_ge(*SB["out"](h + 1))
                    nc.vector.tensor_copy(dst_b(h), bank[7][HD * (h % 2):HD * (h % 2) + HD, 0:SEQ])\
                        .then_inc(SB["evac"].sem, 1)
                h = slot - 1
                if 0 <= h < BH:
                    dve.wait_ge(*SB["score"](h + 1))
                    if h >= 7:
                        dve.wait_ge(*SB["out"](h - 6))
                    if h >= 4:
                        dve.wait_ge(*SB["suffix"](h - 3))
                    z = zr[:, h % 7, :]
                    nc.vector.tensor_scalar(z, bank[4 + h % 2][:, 0:CW3], HD ** -0.5, None, ALU.mult)\
                        .then_inc(SB["zs"].sem, 1)
                    dve.wait_ge(*SB["zs"](h + 1))
                    nc.vector.scalar_tensor_tensor(spr[:, h % 4, :], z, -1.0, z, ALU.mult, ALU.min)\
                        .then_inc(SB["zm"].sem, 1)
                h = slot - 3
                if 0 <= h < BH:
                    z, sp = zr[:, h % 7, :], spr[:, h % 4, :]
                    dve.wait_ge(*SB["log"](h + 1))
                    nc.vector.scalar_tensor_tensor(sp, z, 0.0, sp, ALU.max, ALU.add).then_inc(SB["soft"].sem, 1)
                    dve.wait_ge(*SB["soft"](h + 1))
                    nc.vector.tensor_tensor(sp, sp, m01, ALU.mult).then_inc(SB["masked"].sem, 1)
                    nc.vector.tensor_tensor(z, z, mneg, ALU.add).then_inc(SB["arg"].sem, 1)
                h = slot - 5
                if 0 <= h < BH:
                    dve.wait_ge(*SB["suffix"](h + 1))
                    dve.wait_ge(*SB["arg"](h + 1))
                    nc.vector.tensor_tensor(zr[:, h % 7, :], zr[:, h % 7, :], bank[6][:, 0:CW3], ALU.subtract)\
                        .then_inc(SB["arg2"].sem, 1)
                yield

        def dst_b(h):
            return oT[HD * (h % 2):HD * (h % 2) + HD, 4 + h // 2, :]

        stages.append(("att_b", lambda pe: beside(mem["pe"], MEM_UNITS[1], b_pe(pe), BH + 9),
                       lambda act: beside(mem["act"], MEM_UNITS[1], b_act(act), BH + 9),
                       lambda dve: beside(mem["dve"], MEM_UNITS[1], b_dve(dve), BH + 9), None))

        normmix = norm_parts(oT, "mix_gain", [(0, 4), (4, 4), (8, 8)], at(0, NT, SEQ), at(4096, NT, SEQ),
                             at(8192, 3, SEQ))

        def residual(u0, before, x_ready=None, follow_pe=None, follow_act=None):
            S = shared("residual", ev=8)

            def chunk(pe, u, c, q, first_two):
                if not first_two:
                    pe.wait_ge(*S["ev"](c * 2 - 2))
                for j in range(8):
                    if c == 0:
                        pe.wait_ge(*before[3](j + 1))
                    if c and j == 6 and follow_pe:
                        follow_pe(pe, c - 1, S["ev"])
                    unit_features(pe, u + j, j, h_hi, h_lo, 2 * j, bank[2 * q:2 * q + 2], j == 0, j == 7)\
                        .then_inc(unit_done, 1)

            def pe_(pe):
                before[0](pe)
                chunk(pe, u0, 0, 0, True)
                chunk(pe, u0 + 8, 1, 1, True)
                chunk(pe, u0 + 16, 2, 0, False)
                chunk(pe, u0 + 24, 3, 1, False)
                if follow_pe:
                    follow_pe(pe, 3, S["ev"])

            def act_(act):
                steps = before[1](act)
                for u in range(u0, u0 + 32):
                    if u + LEAD < UNITS:
                        split_hi(act, u, u - u0)
                    if steps and u < u0 + 8:
                        next(steps, None)
                    if follow_act and (u - u0) % 8 == 2 and u - u0 > 8:
                        follow_act(act, (u - u0) // 8 - 1, S["ev"])
                if follow_act:
                    follow_act(act, 3, S["ev"])

            def dve_(dve):
                steps = before[2](dve)
                for c in range(4):
                    for j in range(8):
                        if u0 + 8 * c + j + LEAD < UNITS:
                            split_lo(dve, u0 + 8 * c + j, j)
                        if steps and c == 0:
                            next(steps, None)
                    dve.wait_ge(unit_done, u0 + 8 * c + 8)
                    if c == 0 and x_ready:
                        dve.wait_ge(*x_ready)
                    for b in range(2):
                        t = 4 * c + 2 * b
                        nc.vector.tensor_tensor(x[:, t:t + 2, :], x[:, t:t + 2, :],
                                                bank[2 * (c % 2) + b][:, :].rearrange("p (a b) -> p a b", a=2),
                                                ALU.add).then_inc(S["ev"].sem, 1)

            return pe_, act_, dve_

        norm2 = norm_parts(x, "ffn_norm", [(0, NT)], at(0, NT, SEQ), at(4096, NT, SEQ), at(8192, 3, SEQ), early=True)
        wout = residual(STREAM["wout"], normmix, None, norm2[4], norm2[5])

        gT = at(0, NF, SEQ)
        cv = at(11264, 2, 4, SEQ)
        SU = sems("up", "centre conv1 conv2 silu prod")
        UU = STREAM["up"]
        CW, CB = VEC["conv_w"][0], VEC["conv_b"][0]

        def up_pe(pe):
            wout[0](pe)
            for k in range(2):
                for j in range(8):
                    if k == 0:
                        pe.wait_ge(*norm2[3](j + 1))
                    unit_features(pe, UU + 8 * k + j, j, h_hi, h_lo, 2 * j, bank[2 * k:2 * k + 2],
                                  j == 0, j == 7).then_inc(unit_done, 1)
            with pe.Fori(1, 11) as i:
                for k in range(2):
                    pe.wait_ge(*SU["conv2"](i * 8 + (4 * k - 4)))
                    for j in range(8):
                        unit_features(pe, i * 16 + (UU + 8 * k + j), j, h_hi, h_lo, 2 * j,
                                      bank[2 * k:2 * k + 2], j == 0, j == 7).then_inc(unit_done, 1)

        def up_turn_act(act, i, first, beside=None):
            for k in range(2):
                u = i * 16 + (UU + 8 * k)
                chunk_split(act, split_hi, u, beside)
                act.wait_ge(unit_done, u + 8)
                if not first:
                    act.wait_ge(*SU["prod"](i))
                for f in range(4):
                    c = i * 4 + (44 * k + f)
                    nc.scalar.activation(cv[:, k, f, :], bank[2 * k + f // 2][:, (f % 2) * SEQ:(f % 2 + 1) * SEQ],
                                         ACT.Identity, bias=vec[:, bass.ds(c + CB, 1)],
                                         scale=vec[:, bass.ds(c + (CW + 2 * 88), 1)]).then_inc(SU["centre"].sem, 1)
            act.wait_ge(*SU["conv2"](i * 8 + 4))
            nc.scalar.activation(cv[:, 0, :, :], cv[:, 0, :, :], ACT.Silu).then_inc(SU["silu"].sem, 1)

        def up_act(act):
            wout[1](act)
            up_turn_act(act, 0, True, norm2[1](act))
            with act.Fori(1, 10) as i:
                up_turn_act(act, i, False)
            down_turn_act(act, 0, 0, True)
            down_turn_act(act, 1, 1, True)
            up_turn_act(act, 10, False)

        def up_dve(dve):
            wout[2](dve)
            up_turn_dve(dve, 0, norm2[2](dve))
            with dve.Fori(1, 10) as i:
                up_turn_dve(dve, i)
            down_turn_dve(dve, 0, 0, True)
            down_turn_dve(dve, 1, 1, True)
            up_turn_dve(dve, 10)

        def up_turn_dve(dve, i, beside=None):
            for k in range(2):
                u = i * 16 + (UU + 8 * k)
                chunk_split(dve, split_lo, u, beside)
                for f in range(4):
                    c = i * 4 + (44 * k + f)
                    b = bank[2 * k + f // 2][:, (f % 2) * SEQ:(f % 2 + 1) * SEQ]
                    dve.wait_ge(*SU["centre"](i * 8 + (4 * k + (2 if f < 2 else 4))))
                    nc.vector.scalar_tensor_tensor(cv[:, k, f, 1:SEQ], b[:, 0:SEQ - 1],
                                                   vec[:, bass.ds(c + (CW + 88), 1)], cv[:, k, f, 1:SEQ],
                                                   ALU.mult, ALU.add).then_inc(SU["conv1"].sem, 1)
                for f in range(4):
                    c = i * 4 + (44 * k + f)
                    b = bank[2 * k + f // 2][:, (f % 2) * SEQ:(f % 2 + 1) * SEQ]
                    dve.wait_ge(*SU["conv1"](i * 8 + (4 * k + f + 1)))
                    nc.vector.scalar_tensor_tensor(cv[:, k, f, 2:SEQ], b[:, 0:SEQ - 2],
                                                   vec[:, bass.ds(c + CW, 1)], cv[:, k, f, 2:SEQ],
                                                   ALU.mult, ALU.add).then_inc(SU["conv2"].sem, 1)
                    if f == 3:
                        dve.wait_ge(*SU["conv2"](i * 8 + (4 * k + 4)))
            dve.wait_ge(*SU["silu"](i + 1))
            nc.vector.tensor_tensor(gT[:, bass.ds(i * 4, 4), :], cv[:, 0, :, :], cv[:, 1, :, :], ALU.mult)\
                .then_inc(SU["prod"].sem, 1)

        SD = sems("down", "g_hi g_lo ev_d")
        UD = STREAM["down"]

        def down_turn(pe, i, buf, j0, first, last):
            pe.wait_ge(*SD["g_lo"](i + 1))
            for j in range(4):
                if first and j == 2:
                    pe.wait_ge(*SU["conv2"](88))
                b = 2 * ((j + 2) % 4)
                unit_features(pe, i * 4 + (UD + j), j, o_hi[:, 2 * buf:2 * buf + 2, :], o_lo[:, 2 * buf:2 * buf + 2, :],
                              0, bank[b:b + 2], first, last).then_inc(unit_done, 1)

        def down_pe(pe):
            down_turn(pe, 0, 0, 0, True, False)
            down_turn(pe, 1, 1, 4, False, False)
            with pe.Fori(1, 10) as i:
                for b in range(2):
                    down_turn(pe, i * 2 + b, b, 4 * b, False, False)
            down_turn(pe, 20, 0, 0, False, False)
            down_turn(pe, 21, 1, 4, False, True)

        def down_turn_act(act, i, b, first):
            if not first:
                act.wait_ge(unit_done, i * 4 + (UD - 4))
            nc.scalar.activation(o_hi[:, 2 * b:2 * b + 2, :], gT[:, bass.ds(i * 2, 2), :], ACT.Copy)\
                .then_inc(SD["g_hi"].sem, 1)

        def down_act(act):
            act.wait_ge(*SU["prod"](11))
            down_splits(act, split_hi, down_turn_act)

        def down_splits(eng, split, next_turn):
            def turn(i, b, ahead):
                for j in range(4):
                    split(eng, i * 4 + (UD + j), j)
                    if j == 1 and ahead:
                        next_turn(eng, i + 1, 1 - b, False)

            turn(0, 0, False)
            turn(1, 1, True)
            with eng.Fori(1, 10) as i:
                for b in range(2):
                    turn(i * 2 + b, b, True)
            turn(20, 0, True)
            turn(21, 1, False)

        def down_turn_dve(dve, i, b, first):
            dve.wait_ge(*SD["g_hi"](i + 1))
            if not first:
                dve.wait_ge(unit_done, i * 4 + (UD - 4))
            nc.vector.tensor_tensor(o_lo[:, 2 * b:2 * b + 2, :], gT[:, bass.ds(i * 2, 2), :],
                                    o_hi[:, 2 * b:2 * b + 2, :].bitcast(F32), ALU.subtract).then_inc(SD["g_lo"].sem, 1)

        def down_dve(dve):
            down_splits(dve, split_lo, down_turn_dve)
            dve.wait_ge(unit_done, UD + 88)
            for b in range(10):
                if b < 8:
                    nc.vector.tensor_tensor(x[:, 2 * b:2 * b + 2, :], x[:, 2 * b:2 * b + 2, :],
                                            bank[b][:, :].rearrange("p (a b) -> p a b", a=2), ALU.add)\
                        .then_inc(SD["ev_d"].sem, 1)
                if b >= 2:
                    splitx_lo(dve, b - 2)

        SX = shared("split", hi=8, lo=8)

        def splitx_act(act):
            for p in range(8):
                act.wait_ge(*SD["ev_d"](p + 1))
                nc.scalar.activation(h_hi[:, 2 * p:2 * p + 2, :], x[:, 2 * p:2 * p + 2, :], ACT.Copy)\
                    .then_inc(SX["hi"].sem, 1)

        def splitx_lo(dve, p):
            dve.wait_ge(*SX["hi"](p + 1))
            nc.vector.tensor_tensor(h_lo[:, 2 * p:2 * p + 2, :], x[:, 2 * p:2 * p + 2, :],
                                    h_hi[:, 2 * p:2 * p + 2, :].bitcast(F32), ALU.subtract)\
                .then_inc(SX["lo"].sem, 1)

        merged = at(0, NT, SEQ)
        M0, M1, C0 = 4096, 12288, 10240

        merge_added = [None]

        def merge_stage(name, u0, first, sig, side, o_ready=None, woven=4, late_dve=None):
            S = shared("merge", sig=8, prod=8, add=0 if first else 8)
            n_side = side[3]
            over = 12 * woven if woven > 1 else 8

            def turn_pe(pe, i, first_turn):
                if not first_turn:
                    pe.wait_ge(*S["sig"](i * 2))
                for j in range(8):
                    unit_features(pe, i * 12 + (u0 + j), j, h_hi, h_lo, 2 * j, bank[0:2], j == 0, j == 7)\
                        .then_inc(unit_done, 1)
                    yield
                if not first_turn:
                    pe.wait_ge(*S["prod"](i * 2))
                elif o_ready:
                    pe.wait_ge(*o_ready)
                for j in range(4):
                    unit_features(pe, i * 12 + (u0 + 8 + j), j, o_hi, o_lo, 2 * j, bank[2:4], j == 0, j == 3)\
                        .then_inc(unit_done, 1)
                    yield

            def turn_act(act, i, first_turn):
                for j in range(12):
                    split_hi(act, i * 12 + (u0 + j), j)
                    if j == 7:
                        act.wait_ge(unit_done, i * 12 + (u0 + 8))
                        if not first_turn:
                            act.wait_ge(*S["prod" if first else "add"](i * 2))
                        for b in range(2):
                            nc.scalar.activation(sig[b], bank[b][:, :].rearrange("p (a b) -> p a b", a=2),
                                                 ACT.Sigmoid).then_inc(S["sig"].sem, 1)
                    yield

            def turn_dve(dve, i, first_turn):
                for j in range(12):
                    split_lo(dve, i * 12 + (u0 + j), j)
                    if j < 11:
                        yield
                if late_dve and isinstance(i, int) and i == 3:
                    late_dve(dve)
                dve.wait_ge(unit_done, i * 12 + (u0 + 12))
                dve.wait_ge(*S["sig"](i * 2 + 2))
                for b in range(2):
                    t = i * 4 + 2 * b
                    d = merged[:, t:t + 2, :] if isinstance(i, int) else merged[:, bass.ds(t, 2), :]
                    src = bank[2 + b][:, :].rearrange("p (a b) -> p a b", a=2)
                    nc.vector.tensor_tensor(d if first else sig[b], src, sig[b], ALU.mult).then_inc(S["prod"].sem, 1)
                    if not first:
                        dve.wait_ge(*S["prod"](i * 2 + (b + 1)))
                        nc.vector.tensor_tensor(d, d, sig[b], ALU.add).then_inc(S["add"].sem, 1)
                yield

            def program(turn, steps):
                def go(eng):
                    weave(then(*(turn(eng, i, i == 0) for i in range(woven))), over, steps(eng), n_side)
                    if woven < 4:
                        with eng.Fori(woven, 3) as i:
                            run(turn(eng, i, False))
                        run(turn(eng, 3, False))
                return go

            if not first:
                merge_added[0] = S["add"]
            return program(turn_pe, side[0]), program(turn_act, side[1]), program(turn_dve, side[2])

        def product_steps(src, gate_tiles):
            S = shared("product", silu=1, scaled=8, hi=4, lo=4)

            def pe_(pe):
                yield from range(8)

            def act_(act):
                for step in range(8):
                    if step == 0:
                        nc.scalar.activation(gate_tiles, gate_tiles, ACT.Silu).then_inc(S["silu"].sem, 1)
                    p = step - 2
                    if 0 <= p < 4:
                        act.wait_ge(*S["scaled"](2 * p + 2))
                        nc.scalar.activation(o_hi[:, 2 * p:2 * p + 2, :], src[:, 2 * p:2 * p + 2, :], ACT.Copy)\
                            .then_inc(S["hi"].sem, 1)
                    yield

            def dve_(dve):
                put = to_moving_dve(dve, S, src, o_hi, o_lo)
                for step in range(8):
                    p = step - 1
                    if 0 <= p < 4:
                        if p == 0:
                            dve.wait_ge(*S["silu"](1))
                        nc.vector.tensor_tensor(src[:, 2 * p:2 * p + 2, :], src[:, 2 * p:2 * p + 2, :],
                                                gate_tiles[:, 2 * p:2 * p + 2, :], ALU.mult).then_inc(S["scaled"].sem, 2)
                    if 0 <= step - 3 < 4:
                        put(step - 3)
                    yield

            return pe_, act_, dve_, 8, S["lo"](4)

        def both(one, other):
            return tuple((lambda eng, n=n: then(one[n](eng), other[n](eng))) for n in range(3)) + (one[3] + other[3],)

        def projection(u0, kinds, ev, dst, side):
            n = 8 * len(kinds)
            return (lambda pe: weave(steps_pe(pe, ev, u0, kinds), n, side[0](pe), side[3]),
                    lambda act: weave(steps_act(act, ev, u0, kinds, dst), n, side[1](act), side[3]),
                    lambda dve: weave(steps_dve(dve, ev, u0, kinds, dst), n, side[2](dve), side[3]))

        ua, ga = at(0, 8, SEQ), at(2048, 8, SEQ)
        va = at(M1, 2, 1024)
        sw = at(M1 + 2048, 8, P)
        lnr = at(M1 + 3072, 2, 1024)
        sbr = at(M1 + 5120, 8 * P, parts=(0, 1))
        ev_a = halves(6)
        UA = STREAM["p_a"]
        SA = sems("gmlp", "load gelu st ag sd rc n g b u mask mixed prod")

        def pa_load(pool):
            pool.wait_ge(*SU["prod"](11))
            pool.dma_start(sw, sgu_wT).then_inc(SA["load"].sem, 16)
            pool.dma_start(lnr, ln_rows.broadcast_to([P, 2 * 1024]).rearrange("p (a b) -> p a b", a=2))\
                .then_inc(SA["load"].sem, 16)
            pool.dma_start(sbr, sgu_b).then_inc(SA["load"].sem, 16)

        uag = at(0, 16, SEQ)

        def pa_pe(pe):
            up_pe(pe)
            down_pe(pe)
            features_pe(pe, ev_a, UA, 4, SX["lo"])
            tokens_pe(pe, ev_a, UA + 32, 4, 2)

        def pa_act(act):
            up_act(act)
            down_act(act)
            splitx_act(act)
            features_act(act, ev_a, UA, 4, uag)
            tokens_act(act, ev_a, UA + 32, 4, 2, lambda m, c: va[:, m, c * UN:(c + 1) * UN])

        def pa_dve(dve):
            up_dve(dve)
            down_dve(dve)
            features_dve(dve, ev_a, UA, 4, uag)
            tokens_dve(dve, ev_a, UA + 32, 4, 2, lambda m, c: va[:, m, c * UN:(c + 1) * UN])

        stages.append(("p_a", pa_pe, pa_act, pa_dve, pa_load))

        stat = small[:, 64:88].rearrange("p (a b) -> p a b", a=2)
        mv = small[:, 88:92].rearrange("p (a b) -> p a b", a=2)
        rs = small[:, 92:94]
        GATING = 16

        def gmlp_act(act):
            for step in range(GATING):
                if step < 2:
                    nc.scalar.activation(va[:, step, :], va[:, step, :], ACT.Gelu_apprx_tanh).then_inc(SA["gelu"].sem, 1)
                if step in (4, 5):
                    m = step - 4
                    act.wait_ge(*SA["ag"](m + 1))
                    nc.scalar.activation(rs[:, m:m + 1], mv[:, m, 1:2], ACT.Sqrt, bias=ln_eps_col)\
                        .then_inc(SA["sd"].sem, 1)
                if step == 6:
                    nc.scalar.activation(ua, ua, ACT.Gelu_apprx_tanh).then_inc(SA["u"].sem, 1)
                yield

        def gmlp_dve(dve):
            for step in range(GATING):
                if step == 0:
                    dve.wait_ge(*SA["load"](48))
                    nc.vector.tensor_tensor(sw, sw, causal.unsqueeze(1).broadcast_to([P, 8, P]), ALU.mult)\
                        .then_inc(SA["mask"].sem, 1)
                if step in (2, 3):
                    m = step - 2
                    dve.wait_ge(*SA["gelu"](m + 1))
                    for c in range(2):
                        nc.vector.bn_stats(stat[:, m, 6 * c:6 * c + 6], va[:, m, c * 512:(c + 1) * 512])\
                            .then_inc(SA["st"].sem, 1)
                    dve.wait_ge(*SA["st"](2 * m + 2))
                    nc.vector.bn_aggr(mv[:, m, :], stat[:, m, :]).then_inc(SA["ag"].sem, 1)
                if step in (5, 6):
                    m = step - 5
                    dve.wait_ge(*SA["sd"](m + 1))
                    dve.wait_ge(*SA["ag"](m + 1))
                    nc.vector.reciprocal(rs[:, m:m + 1], rs[:, m:m + 1]).then_inc(SA["rc"].sem, 1)
                    dve.wait_ge(*SA["rc"](m + 1))
                    nc.vector.tensor_scalar(va[:, m, :], va[:, m, :], mv[:, m, 0:1], rs[:, m:m + 1], ALU.subtract,
                                            ALU.mult).then_inc(SA["n"].sem, 1)
                if step in (7, 8):
                    m = step - 7
                    dve.wait_ge(*SA["n"](m + 1))
                    nc.vector.tensor_tensor(va[:, m, :], va[:, m, :], lnr[:, 0, :], ALU.mult).then_inc(SA["g"].sem, 1)
                    dve.wait_ge(*SA["g"](m + 1))
                    nc.vector.tensor_tensor(va[:, m, :], va[:, m, :], lnr[:, 1, :], ALU.add).then_inc(SA["b"].sem, 1)
                if 12 <= step < 16:
                    g = step - 12
                    if g == 0:
                        dve.wait_ge(*SA["u"](1))
                    dve.wait_ge(*SA["mixed"](g + 1))
                    nc.vector.tensor_tensor(ua[:, 2 * g:2 * g + 2, :], ua[:, 2 * g:2 * g + 2, :],
                                            bank[4 + g][:, :].rearrange("p (a b) -> p a b", a=2), ALU.mult)\
                        .then_inc(SA["prod"].sem, 1)
                yield

        def gmlp_pe(pe):
            for step in range(GATING):
                if 10 <= step < 14:
                    if step == 10:
                        pe.wait_ge(*SA["mask"](1))
                        pe.wait_ge(*SA["b"](2))
                    for g in (2 * (step - 10), 2 * (step - 10) + 1):
                        for c in range(2):
                            o = bank[4 + g // 2][:, (g % 2) * SEQ + c * P:(g % 2) * SEQ + (c + 1) * P]
                            nc.tensor.matmul(o, va[:, c, g * P:(g + 1) * P], sw[:, g, :], start=True, stop=False)
                            mm = nc.tensor.matmul(o, ones[0:1, :], sbr[:, g * P:(g + 1) * P], start=False, stop=True)
                    mm.then_inc(SA["mixed"].sem, 1)
                yield

        qgm = at(M0, 16, SEQ)
        qm, gm = at(M0, 8, SEQ), at(M0 + 2048, 8, SEQ)
        om = at(M0 + 4096, 8, SEQ)
        ev_m = halves(4)
        product_a = product_steps(ua, ga)
        stages.append(("p_m", *projection(STREAM["p_m"], "FFFF", ev_m, to_tiles(qgm),
                                          both((gmlp_pe, gmlp_act, gmlp_dve, GATING), product_a)), None))
        m_rings = at(M1, 4, 2 * SEQ), at(M1 + 2048, 2, 2 * SEQ)

        def m_pv(h):
            def go(pt):
                for d in range(2):
                    for kt in range(2):
                        yield nc.tensor.matmul(bank[7][:, d * SEQ:(d + 1) * SEQ],
                                               vm[:, kt, h * SEQ + d * P:h * SEQ + (d + 1) * P],
                                               pt[:, kt * SEQ:(kt + 1) * SEQ], start=kt == 0, stop=kt == 1)
            return go

        def m_job(h):
            return dict(scores=lambda m: [(qm[:, 2 * h + d, m * P:(m + 1) * P], kmT[:, 2 * h + d, :]) for d in range(2)],
                        segs=[(0, SEQ), (SEQ, SEQ)], parts=[(0, P), (SEQ, P), (P, P), (SEQ + P, P)], last=True,
                        out_regions=1, pv=m_pv(h))

        att_m = softmax([m_job(h) for h in range(4)], SEQ ** -0.5, lambda h: nc.vector.tensor_copy(
            om[:, 2 * h:2 * h + 2, :], bank[7][:, :].rearrange("p (a b) -> p a b", a=2)), m_rings)
        sig_a = [at(M0 + 6144 + 512 * b, 2, SEQ) for b in range(2)]
        stages.append(("m_a", *merge_stage("m_a", STREAM["m_a"], True, sig_a, (*att_m[0:3], att_m[4])), None))

        qc = at(C0, 8, SEQ)
        cmpT = at(C0 + 2048, 4, SEQ)
        ksw = at(C0 + 3072, 4, SEQ)
        gc = at(C0 + 4096, 8, SEQ)
        swp = at(C0 + 6144, 4, SEQ)
        vsw = at(C0 + 7168, 2, 512)
        zz = at(M0, 2, 4 * SEQ)
        w1 = at(M0 + 2048, 4096)
        onc = at(M0 + 4096, 8, SEQ)
        qgc = at(C0, 24, SEQ)
        kmF = kmT[:, :, :].rearrange("p a b -> p (a b)")
        glr = kmF[:, 0:768]
        oh2 = kmF[0:33, 768:1280]
        tb2 = kmF[0:33, 1280:1320]
        w2 = vm[:, 0, 0:256].rearrange("p (a b c) -> p a b c", a=2, b=2)
        kcT = vm[:, 0, 256:316]
        vcs = vm[0:15, 0, 320:576]
        hid = vm[:, 0, 576:816].rearrange("p (a b c) -> p a b c", a=2, b=2)
        blk = kmF[:, 0:960].rearrange("p (j h n) -> p j h n", j=16, h=4)
        cmk = vm[:, 0, 820:850]
        glb = vm[:, 0, 850:898]
        gts = vm[:, 0, 900:996].rearrange("p (m g) -> p m g", m=2)
        cb = vm[:, 1, 0:480].rearrange("p (h c) -> p h c", h=16)
        sig_m = [kmF[:, 1320:1832].rearrange("p (a b) -> p a b", a=2),
                 vm[:, 1, 480:992].rearrange("p (a b) -> p a b", a=2)]
        n_rings = kmF[:, 0:4 * CW3].rearrange("p (a b) -> p a b", a=4), at(C0 + 2048, 2, CW3)
        bias_n = [vm[:, 1, 480:480 + CW3], at(C0 + 8192, CW3)]
        ev_c = halves(7)
        UC = STREAM["p_c"]
        SC = sems("nsa", "load swap gate gl bias cbev z w1k w1v hid blk h kc kcv g2")

        def pc_load(pool):
            pool.dma_start(glr.rearrange("p (a b) -> p a b", a=NT), gl_w).then_inc(SC["load"].sem, 16)
            pool.dma_start(glb, gl_b.broadcast_to([P, 48])).then_inc(SC["load"].sem, 16)
            pool.dma_start(oh2, onehots[:, 3, :]).then_inc(SC["load"].sem, 16)
            pool.dma_start(tb2, tabs).then_inc(SC["load"].sem, 16)
            pool.dma_start(cmk, cmask).then_inc(SC["load"].sem, 16)
            pool.dma_start(w2[:, 0, :, :], cmp_w2k).then_inc(SC["load"].sem, 16)
            pool.dma_start(w2[:, 1, :, :], cmp_w2v).then_inc(SC["load"].sem, 16)

        def c_dst(half, c):
            return to_tiles(qgc)(half, c) if c < 6 else vsw[:, half, :]

        product_m = product_steps(om, gm)
        stages.append(("p_c", *projection(UC, "FFFFFFT", ev_c, c_dst, product_m), pc_load))

        def cmp_load(pool):
            for t in range(4):
                pool.dma_start(swp[HD:P, t, :], ksw[0:HD, t, :]).then_inc(SC["swap"].sem, 16)
                pool.dma_start(swp[0:HD, t, :], ksw[HD:P, t, :]).then_inc(SC["swap"].sem, 16)
            for n in range(2):
                for h in range(4):
                    src = cmpT[HD * (h % 2):HD * (h % 2) + HD, 2 * n + h // 2, :]
                    pool.dma_start(zz[0:HD, n, h * SEQ:(h + 1) * SEQ], src).then_inc(SC["z"].sem, 16)
                    pool.dma_start(zz[HD:P, n, h * SEQ:(h + 1) * SEQ - 1], src[:, 1:SEQ]).then_inc(SC["z"].sem, 16)
            pool.dma_start(w1, cmp_w1[0]).then_inc(SC["w1k"].sem, 16)
            pool.wait_ge(*SC["hid"](1))
            pool.dma_start(w1, cmp_w1[1]).then_inc(SC["w1v"].sem, 16)
            pool.wait_ge(*SC["swap"](128))
            pool.wait_ge(*SC["z"](256))

        COMPRESSION = 48

        def cmp_hidden_pe(pe, o, js):
            for j in js:
                mm = nc.tensor.matmul(bank[6 + o][:, 0:60], w1[:, j * 256 + o * P:j * 256 + (o + 1) * P],
                                      blk[:, j, :, :].rearrange("p a b -> p (a b)"), start=j == 0, stop=j == 15)
            return mm

        def cmp_pe(pe):
            for step in range(COMPRESSION):
                if 2 <= step < 10:
                    if step == 2:
                        pe.wait_ge(*SC["load"](112))
                    m = (step - 2) // 4
                    for t in range(4 * ((step - 2) % 4), 4 * ((step - 2) % 4) + 4):
                        mm = nc.tensor.matmul(bank[4][:, 48 * m:48 * m + 48], x[:, t, m * P:(m + 1) * P],
                                              glr[:, 48 * t:48 * t + 48], start=t == 0, stop=t == NT - 1)
                    if step == 9:
                        mm.then_inc(SC["gl"].sem, 1)
                if 10 <= step < 15:
                    for k in range(6 * (step - 10), 6 * (step - 9)):
                        m, n = divmod(k, 15)
                        a = SEQ + P * m - 16 * n - 31
                        mm = nc.tensor.matmul(bank[5][:, k * 16:(k + 1) * 16], oh2[:, a:a + P], tb2[:, 24:40],
                                              start=True, stop=True)
                    if step == 14:
                        mm.then_inc(SC["bias"].sem, 1)
                for n, start in enumerate((18, 30)):
                    if start <= step < start + 8:
                        if step == start:
                            pe.wait_ge(*SC["blk"](4 * n + 4))
                            if n:
                                pe.wait_ge(*SC["h"](2))
                            pe.wait_ge(*SC["w1v" if n else "w1k"](16))
                        o, part = divmod(step - start, 4)
                        mm = cmp_hidden_pe(pe, o, range(4 * part, 4 * part + 4))
                        if step == start + 7:
                            mm.then_inc(SC["hid"].sem, 1)
                if step == 41:
                    pe.wait_ge(*SC["h"](4))
                    pe.wait_ge(*SC["g2"](1))
                    for half in range(2):
                        for o in range(2):
                            nc.tensor.matmul(bank[4][HD * half:HD * half + HD, 0:60], w2[:, 0, o, :],
                                             hid[:, 0, o, :], start=o == 0, stop=o == 1)
                    for h in range(4):
                        for o in range(2):
                            mm = nc.tensor.matmul(bank[6][0:15, h * HD:(h + 1) * HD], hid[:, 1, o, h * 15:(h + 1) * 15],
                                                  w2[:, 1, o, :], start=o == 0, stop=o == 1)
                    mm.then_inc(SC["kc"].sem, 1)
                yield

        def cmp_act(act):
            for step in range(COMPRESSION):
                if step in (27, 39):
                    n = 0 if step == 27 else 1
                    act.wait_ge(*SC["hid"](n + 1))
                    for o in range(2):
                        nc.scalar.activation(hid[:, n, o, :], bank[6 + o][:, 0:60], ACT.Silu).then_inc(SC["h"].sem, 1)
                if step == 12:
                    act.wait_ge(*SC["g2"](1))
                    nc.scalar.activation(gts, gts, ACT.Sigmoid).then_inc(SC["gate"].sem, 1)
                if step == 43:
                    act.wait_ge(*SC["kc"](1))
                    nc.scalar.activation(kcT, bank[4][:, 0:60], ACT.Copy)
                    nc.scalar.activation(vcs, bank[6][0:15, 0:256], ACT.Copy).then_inc(SC["kcv"].sem, 1)
                yield

        def cmp_dve(dve):
            for step in range(COMPRESSION):
                if step == 11:
                    dve.wait_ge(*SC["load"](112))
                    dve.wait_ge(*SC["gl"](1))
                    nc.vector.tensor_tensor(gts, bank[4][:, 0:96].rearrange("p (m g) -> p m g", m=2),
                                            glb.unsqueeze(1).broadcast_to([P, 2, 48]), ALU.add)\
                        .then_inc(SC["g2"].sem, 1)
                if step in (17, 27):
                    n = 0 if step == 17 else 1
                    if n == 0:
                        dve.wait_ge(*SC["z"](256))
                    else:
                        dve.wait_ge(*SC["hid"](1))
                    pv = VEC["cmp_pe_v" if n else "cmp_pe_k"][0]
                    for h in range(4):
                        z = zz[:, n, h * SEQ:(h + 1) * SEQ]
                        z = bass.AP(tensor=z.tensor, offset=z.offset, ap=[z.ap[0], [2, 16], [16, 15]])
                        nc.vector.tensor_tensor(blk[:, :, h, :], z, vec[:, pv:pv + 16].unsqueeze(2)
                                                .broadcast_to([P, 16, 15]), ALU.add).then_inc(SC["blk"].sem, 1)
                if step == 16:
                    dve.wait_ge(*SC["bias"](1))
                    nc.vector.tensor_copy(cb, bank[5][:, 0:480].rearrange("p (c h) -> p h c", h=16))\
                        .then_inc(SC["cbev"].sem, 1)
                yield

        stages.append(("m_m", *merge_stage("m_m", STREAM["m_m"], False, sig_m, (cmp_pe, cmp_act, cmp_dve, COMPRESSION)),
                       cmp_load))

        def n_job(h, br):
            p, kv = h % 2, h // 4
            rows_ = slice(HD * p, HD * p + HD)
            j = dict(last=br == 2, out_regions=2, gate=gts[:, :, 16 * ((br + 1) % 3) + h])
            if br < 2:
                kk, t = ksw if kv % 2 == p else swp, 2 * br + kv // 2
                c = br * SEQ + kv * HD
                j.update(scores=lambda m: [(qc[rows_, h // 2, m * P:(m + 1) * P], kk[rows_, t, 0:P + m * P])],
                         buf=h % 2, **CAUSAL,
                         pv=causal_pv(head_dst(h), lambda kt: vsw[:, kt, c:c + HD], br == 0, False))
                if br == 0:
                    j["load"] = 24 + h
            else:
                j.update(scores=lambda m: [(qc[rows_, h // 2, m * P:(m + 1) * P], kcT[rows_, kv * 15:(kv + 1) * 15])],
                         tile=cb[:, h, :], segs=[(0, 15), (15, 15)], parts=[(0, 15), (15, 15)], weights=cmk, floor=True,
                         pv=lambda pt: [nc.tensor.matmul(bank[7][HD * p:HD * p + HD, 0:SEQ],
                                                         vcs[:, kv * HD:(kv + 1) * HD], pt[0:15, 0:SEQ],
                                                         start=False, stop=True, skip_group_check=True)])
            return j

        def dst_n(h):
            return onc[HD * (h % 2):HD * (h % 2) + HD, h // 2, :]

        att_n = softmax([n_job(h, br) for h in range(16) for br in range(3)], HD ** -0.5, head_evac(dst_n),
                        n_rings, bias_n)
        xb, gb = at(M0, 8, SEQ), at(M0 + 2048, 8, SEQ)
        xc = at(C0, 8, SEQ)
        lw = at(C0 + 2048, 2, 8, P)
        av = at(C0 + 2048, 8, SEQ)
        iv, tv = at(C0 + 6144, 8, SEQ), onc
        rv = xb
        xgb = at(M0, 16, SEQ)
        ev_b = halves(4)
        UB = STREAM["p_b"]
        SL = sems("lru", "load c0 c1 c2 c3 mm i chain spn t a2 f s g1 g2 scan al ex2")

        def lw_load(pool):
            pool.dma_start(lw, lru_w).then_inc(SL["load"].sem, 16)

        stages.append(("p_b", *projection(UB, "FFFF", ev_b, to_tiles(xgb), (*att_n[0:3], att_n[4])), att_n[3]))
        product_c = product_steps(onc, gc)
        C2, C2B = VEC["conv2_w"][0], VEC["conv2_b"][0]
        lam = vec[:, VEC["lru_lam"][0]:VEC["lru_lam"][0] + 8]
        T = [small[:, 94 + 8 * n:102 + 8 * n] for n in range(7)]
        LOG_TERMS = 9

        LRU = 40

        def lru_pe(pe):
            for step in range(LRU):
                t = step - 4
                if 0 <= t < 8:
                    if t == 0:
                        pe.wait_ge(*SL["load"](16))
                    pe.wait_ge(*SL["c3"](t + 1))
                    if t >= 4:
                        pe.wait_ge(*SL["i"](t - 3))
                    for n in range(2):
                        mm = nc.tensor.matmul(bank[4 + t % 4][:, n * SEQ:(n + 1) * SEQ], lw[:, n, t, :], xc[:, t, :],
                                              start=True, stop=True)
                    mm.then_inc(SL["mm"].sem, 1)
                yield

        def lru_act(act):
            for step in range(LRU):
                if step == 1:
                    act.wait_ge(*SL["al"](1))
                    nc.scalar.activation(T[0], T[0], ACT.Exp).then_inc(SL["ex2"].sem, 1)
                t = step - 5
                if 0 <= t < 8:
                    act.wait_ge(*SL["mm"](t + 1))
                    nc.scalar.activation(rv[:, t, :], bank[4 + t % 4][:, 0:SEQ], ACT.Sigmoid, bias=vcol("lru_ba", t))
                    nc.scalar.activation(iv[:, t, :], bank[4 + t % 4][:, SEQ:2 * SEQ], ACT.Sigmoid,
                                         bias=vcol("lru_bx", t)).then_inc(SL["i"].sem, 1)
                p = step - 14
                if 0 <= p < 4:
                    if p == 0:
                        act.wait_ge(*SL["i"](8))
                        act.wait_ge(*SL["spn"](1))
                        act.wait_ge(*product_c[4])
                    for t in (2 * p, 2 * p + 1):
                        nc.scalar.activation(av[:, t, :], rv[:, t, :], ACT.Exp, scale=T[5][:, t:t + 1])
                        nc.scalar.activation(tv[:, t, :], rv[:, t, :], ACT.Tanh, scale=T[6][:, t:t + 1])\
                            .then_inc(SL["t"].sem, 1)
                t = step - 19
                if 0 <= t < 4:
                    act.wait_ge(*SL["f"](t + 1))
                    nc.scalar.activation(tv[:, 2 * t:2 * t + 2, :], tv[:, 2 * t:2 * t + 2, :], ACT.Sqrt)\
                        .then_inc(SL["s"].sem, 1)
                yield

        def lru_dve(dve):
            n = [0]

            def link(i):
                n[0] += 1
                i.then_inc(SL["chain"].sem, 1)
                dve.wait_ge(*SL["chain"](n[0]))
            for step in range(LRU):
                if step == 0:
                    link(nc.vector.tensor_scalar(T[1], lam, -1.0, None, ALU.mult))
                    nc.vector.tensor_tensor(T[0], T[1], lam, ALU.min).then_inc(SL["al"].sem, 1)
                if step == 2:
                    dve.wait_ge(*SL["ex2"](1))
                    link(nc.vector.tensor_scalar(T[2], T[0], 2.0, None, ALU.add))
                    link(nc.vector.reciprocal(T[2], T[2]))
                    link(nc.vector.tensor_tensor(T[2], T[2], T[0], ALU.mult))
                    link(nc.vector.tensor_tensor(T[3], T[2], T[2], ALU.mult))
                    link(nc.vector.memset(T[4], 2.0 / (2 * LOG_TERMS + 1)))
                if 3 <= step < 3 + LOG_TERMS:
                    k = LOG_TERMS - 1 - (step - 3)
                    link(nc.vector.tensor_tensor(T[4], T[4], T[3], ALU.mult))
                    link(nc.vector.tensor_scalar(T[4], T[4], 2.0 / (2 * k + 1), None, ALU.add))
                if step == 3 + LOG_TERMS:
                    link(nc.vector.tensor_tensor(T[4], T[4], T[2], ALU.mult))
                    link(nc.vector.tensor_scalar(T[1], T[1], 0.0, None, ALU.max))
                    link(nc.vector.tensor_tensor(T[4], T[4], T[1], ALU.add))
                    link(nc.vector.tensor_scalar(T[5], T[4], -8.0, None, ALU.mult))
                    nc.vector.tensor_scalar(T[6], T[4], 8.0, None, ALU.mult).then_inc(SL["spn"].sem, 1)
                t = step - 3
                if 0 <= t < 8:
                    for tap in range(4):
                        w = vec[:, C2 + 8 * (3 - tap) + t:C2 + 8 * (3 - tap) + t + 1]
                        if tap == 0:
                            nc.vector.tensor_scalar(xc[:, t, :], xb[:, t, :], w, vec[:, C2B + t:C2B + t + 1], ALU.mult,
                                                    ALU.add).then_inc(SL["c0"].sem, 1)
                        else:
                            dve.wait_ge(*SL[f"c{tap - 1}"](t + 1))
                            nc.vector.scalar_tensor_tensor(xc[:, t, tap:SEQ], xb[:, t, 0:SEQ - tap], w,
                                                           xc[:, t, tap:SEQ], ALU.mult, ALU.add)\
                                .then_inc(SL[f"c{tap}"].sem, 1)
                t = step - 16
                if 0 <= t < 4:
                    dve.wait_ge(*SL["t"](2 * t + 2))
                    two = slice(2 * t, 2 * t + 2)
                    nc.vector.tensor_tensor(rv[:, two, :], av[:, two, :], av[:, two, :], ALU.mult)\
                        .then_inc(SL["a2"].sem, 1)
                    dve.wait_ge(*SL["a2"](t + 1))
                    nc.vector.scalar_tensor_tensor(tv[:, two, :], rv[:, two, :], 1.0, tv[:, two, :], ALU.add, ALU.mult)\
                        .then_inc(SL["f"].sem, 1)
                    nc.vector.tensor_tensor(iv[:, two, :], iv[:, two, :], xc[:, two, :], ALU.mult)\
                        .then_inc(SL["g1"].sem, 1)
                t = step - 22
                if 0 <= t < 4:
                    two = slice(2 * t, 2 * t + 2)
                    dve.wait_ge(*SL["s"](t + 1))
                    dve.wait_ge(*SL["g1"](t + 1))
                    nc.vector.tensor_tensor(iv[:, two, :], iv[:, two, :], tv[:, two, :], ALU.mult)\
                        .then_inc(SL["g2"].sem, 1)
                t = step - 24
                if 0 <= t < 8:
                    dve.wait_ge(*SL["g2"](t // 2 + 1))
                    nc.vector.tensor_tensor_scan(xc[:, t, :], av[:, t, :], iv[:, t, :], 0.0, ALU.mult, ALU.add)\
                        .then_inc(SL["scan"].sem, 1)
                yield

        sig_b = [kmF[:, 512 * b:512 * b + 512].rearrange("p (a b) -> p a b", a=2) for b in range(2)]
        stages.append(("m_c", *merge_stage("m_c", STREAM["m_c"], False, sig_b,
                                           both(product_c, (lru_pe, lru_act, lru_dve, LRU)), product_c[4]), lw_load))
        product_b = product_steps(xc, gb)
        SM = shared("split", hi=4, lo=5)

        def splitm_lo(dve, n):
            dve.wait_ge(*SM["hi"](n + 1))
            nc.vector.tensor_tensor(h_lo[:, 4 * n:4 * n + 4, :], merged[:, 4 * n:4 * n + 4, :],
                                    h_hi[:, 4 * n:4 * n + 4, :].bitcast(F32), ALU.subtract)\
                .then_inc(SM["lo"].sem, 1)

        def late_mb_dve(dve):
            for n in range(3):
                splitm_lo(dve, n)
            nc.vector.tensor_scalar(x[:, :, :], x[:, :, :], 2.0 ** 0.25, None, ALU.mult).then_inc(SM["lo"].sem, 1)

        m_b = merge_stage("m_b", STREAM["m_b"], False, sig_b, product_b, product_b[4], woven=1, late_dve=late_mb_dve)

        def splitm_act(act):
            for n in range(4):
                act.wait_ge(*merge_added[0](6 if n < 3 else 8))
                nc.scalar.activation(h_hi[:, 4 * n:4 * n + 4, :], merged[:, 4 * n:4 * n + 4, :], ACT.Copy)\
                    .then_inc(SM["hi"].sem, 1)

        def splitm_ready(n):
            group = (n + 1) // 2
            return SM["lo"](group if group < 4 else 5)

        SN = sems("ln", "sum mean cent square ssum root recip a b out")
        lsq, lmean, lsd = at(0, 8, SEQ), at(2048, SEQ), at(2304, SEQ)

        def sum_pe(pe, c, ev):
            pe.wait_ge(*ev(2 * c + 2))
            for t in range(4 * c, 4 * c + 4):
                mm = nc.tensor.matmul(bank[4][:, 0:SEQ], ones, x[:, t, :], start=t == 0, stop=t == NT - 1)
            if c == 3:
                mm.then_inc(SN["sum"].sem, 1)

        out2 = residual(STREAM["out2"], (lambda pe: None, splitm_act, lambda dve: splitm_lo(dve, 3), splitm_ready),
                        SM["lo"](4), sum_pe)

        def ln_pe(pe):
            m_b[0](pe)
            out2[0](pe)
            for t in range(NT):
                pe.wait_ge(*SN["square"](t // 2 + 1))
                nc.tensor.matmul(bank[5][:, 0:SEQ], ones, lsq[:, t % 8, :], start=t == 0, stop=t == NT - 1)\
                    .then_inc(SN["ssum"].sem, 1)

        def ln_act(act):
            m_b[1](act)
            out2[1](act)
            act.wait_ge(*SN["sum"](1))
            nc.scalar.activation(lmean, bank[4][:, 0:SEQ], ACT.Copy, scale=1.0 / DM).then_inc(SN["mean"].sem, 1)
            for p in range(NT // 2):
                act.wait_ge(*SN["cent"](p + 1))
                if p >= 4:
                    act.wait_ge(*SN["ssum"](2 * p - 6))
                nc.scalar.activation(lsq[:, 2 * p % 8:2 * p % 8 + 2, :], x[:, 2 * p:2 * p + 2, :], ACT.Square)\
                    .then_inc(SN["square"].sem, 1)
            act.wait_ge(*SN["ssum"](NT))
            nc.scalar.activation(lsd, bank[5][:, 0:SEQ], ACT.Sqrt, bias=ln_eps_col, scale=1.0 / DM)\
                .then_inc(SN["root"].sem, 1)
            for t in range(NT):
                act.wait_ge(*SN["a"](t // 2 + 1))
                nc.scalar.activation(x[:, t, :], x[:, t, :], ACT.Identity, bias=vcol("ln_b", t),
                                     scale=vcol("ln_g", t)).then_inc(SN["b"].sem, 1)

        def ln_dve(dve):
            m_b[2](dve)
            out2[2](dve)
            two = lambda v: v.unsqueeze(1).broadcast_to([P, 2, SEQ])
            dve.wait_ge(*SN["mean"](1))
            for p in range(NT // 2):
                nc.vector.tensor_tensor(x[:, 2 * p:2 * p + 2, :], x[:, 2 * p:2 * p + 2, :], two(lmean), ALU.subtract)\
                    .then_inc(SN["cent"].sem, 1)
            dve.wait_ge(*SN["root"](1))
            nc.vector.reciprocal(lsd, lsd).then_inc(SN["recip"].sem, 1)
            dve.wait_ge(*SN["recip"](1))
            dve.wait_ge(*SN["cent"](NT // 2))
            for p in range(NT // 2):
                dve.wait_ge(*SN["square"](p + 1))
                nc.vector.tensor_tensor(x[:, 2 * p:2 * p + 2, :], x[:, 2 * p:2 * p + 2, :], two(lsd), ALU.mult)\
                    .then_inc(SN["a"].sem, 1)

        def out_sp(sp):
            for n in range(4):
                sp.wait_ge(*SN["b"](4 * n + 4))
                sp.dma_start(out[:, 4 * n:4 * n + 4, :], x[:, 4 * n:4 * n + 4, :]).then_inc(SN["out"].sem, 16)
            sp.wait_ge(*SN["out"](64))

        stages.append(("ln", ln_pe, ln_act, ln_dve, None))

        block = ctx.enter_context(nc.Block())

        def finish_stage(eng, n):
            eng.drain().then_inc(stage_done, 1)
            eng.wait_ge(stage_done, 3 * (n + 1))

        @block.sync
        def _(sp):
            for n in range(4):
                sp.dma_start(x[:, 4 * n:4 * n + 4, :], xT[:, 4 * n:4 * n + 4, :]).then_inc(S0[f"x{n}"].sem, 16)
                if n == 0:
                    sp.dma_start(sq_c[:, :, :], squares).then_inc(S0["c"].sem, 16)
            for s in range(RING):
                sp.dma_start(raw[:, s, :], W[s]).then_inc(raw_ready[s], 16)
            with sp.Fori(1, UNITS // RING) as i:
                for s in range(RING):
                    sp.wait_ge(lo_ready, i * RING + (s - RING + 1))
                    sp.dma_start(raw[:, s, :], W[i * RING + s]).then_inc(raw_ready[s], 16)
            for s in range(RING):
                sp.wait_ge(raw_ready[s], 16 * (UNITS // RING))
            out_sp(sp)

        @block.gpsimd
        def _(pool):
            for n, s in enumerate(stages):
                if s[4]:
                    if n and s[0] != "att_ac":
                        pool.wait_ge(stage_done, 3 * n)
                    s[4](pool)

        @block.scalar
        def _(act):
            for n, s in enumerate(stages):
                s[2](act)
                finish_stage(act, n)

        @block.vector
        def _(dve):
            for n, s in enumerate(stages):
                if s[0] == "att_ac":
                    dve.wait_ge(*S0["rows"](16 * 40))
                    dve.wait_ge(*SH["sinks"](16))
                s[3](dve)
                finish_stage(dve, n)

        @block.tensor
        def _(pe):
            for n, s in enumerate(stages):
                if s[0] == "att_ac":
                    pe.wait_ge(*SH["swap"](32))
                if s[0] == "att_n":
                    pe.wait_ge(*SC["swap"](128))
                s[1](pe)
                finish_stage(pe, n)


def shape_constants():
    f = np.float32
    k, q = np.arange(P)[:, None], np.arange(P)[None, :]
    squares = np.stack([np.ones((P, P)), k // HD == q // HD, k == q, k >= q, q >= k], 1).astype(f)
    key, tok = np.arange(P)[:, None, None] + P * np.arange(2)[None, :, None], np.arange(SEQ)[None, None, :]
    before = key < tok
    dist = np.arange(P)[:, None, None] + P * np.arange(2)[None, :, None] - np.arange(SEQ)[None, None, :]

    def times(d):
        return np.where(d < 0, 0, (d <= P) * 1 + (d % 4 == 0) + (d % 16 == 0))

    def causal_tiles(v, first):
        return np.concatenate([v[:, 0, 0:first], v[:, 1, SEQ - (3 * P - first):]], 1)

    masks = np.concatenate([causal_tiles(before, SEQ), causal_tiles(times(dist), P)], 1).astype(f)
    tok2 = np.arange(P)[:, None, None] + P * np.arange(2)[None, :, None]
    cmask = (tok2 - (16 * np.arange(15)[None, None, :] + 31) >= 0).astype(f).reshape(P, 30)

    def bucket(d, most):
        d = np.maximum(d, 0)
        large = 16 + (np.log(np.maximum(d, 1).astype(f) / f(16)) / f(math.log(most / 16)) * f(16)).astype(np.int32)
        return np.where(d < 16, d, np.minimum(large, 31))

    def onehot(d, ok, most):
        t = np.zeros((33, TABW), f)
        t[np.where(ok, bucket(d, most), 32), np.arange(TABW)] = 1
        return t

    d = 255 - np.arange(TABW)
    up = np.arange(TABW) - SEQ
    onehots = np.stack([onehot(d, (d >= 0) & (d < P), 2048), onehot(d, times(d) > 0, 2048), onehot(d, d >= 0, 1024),
                        onehot(up, up >= 0, 1024)], 1)
    return squares, masks, cmask, onehots


def lay_out(i):
    a = {k: np.asarray(v) for k, v in i.items()}

    def units(w, rows_first=False):
        kk, n = w.shape
        v = w.reshape(kk // (UK * P), UK, P, n // UN, UN)
        return v.transpose((0, 3, 2, 1, 4) if rows_first else (3, 0, 2, 1, 4)).reshape(-1, P, UK * UN)

    w = a["w_in"][0]
    off = np.cumsum([0, 512, 128, 128, 512, 512, 512, 1024, 1024, 1024])
    aq, ak, av, bq, bk, bv, cq, ck, cv = (w[:, off[n]:off[n + 1]] for n in range(9))
    pad = np.zeros((DM, 256), np.float32)
    parts = [units(np.concatenate([aq, bq, bk, cq, ck, ak, av, pad, bv, cv], 1)),
             units(a["w_mem_kv_2"][0]), units(a["w_out"][0])]
    wu = a["w_up"][0]
    for c in range(11):
        parts += [units(wu[:, c * UN:(c + 1) * UN]), units(wu[:, NF * P + c * UN:NF * P + (c + 1) * UN])]
    parts.append(units(np.roll(a["w_down"][0], -DM // 2, 1), True))
    w = a["w_in_2"][0]
    br = a["w_branch_2"][0]

    def merge(n):
        for c in range(4):
            g = 10800 + n * DM + c * UN
            yield units(w[:, g:g + UN])
            yield units(br[n][:, c * UN:(c + 1) * UN])

    parts += [units(np.concatenate([w[:, 0:1024], w[:, 2048:3072], w[:, 1024:2048]], 1))]
    parts += [units(w[:, 8752:10800]), *merge(0)]
    parts += [units(np.concatenate([w[:, 5120:6656], w[:, 6656:6912], w[:, 7168:7424], w[:, 7728:8752],
                                    w[:, 6912:7168], w[:, 7424:7680]], 1)), *merge(3)]
    parts += [units(w[:, 3072:5120]), *merge(2), *merge(1)]
    parts.append(units(a["w_out_2"][0]))

    def cols(v):
        return v.reshape(-1, P).T

    def twice(v):
        return np.concatenate([v, v])[:, None]

    def pairs(v):
        return v.reshape(16, 2, HD, -1).transpose(1, 2, 0, 3).reshape(P, -1)

    vec = [cols(a["attn_norm"][0]), cols(a["ffn_norm"][0]), cols(a["mix_out_gain"][0]), twice(a["a_q_gain"][0]),
           twice(a["a_k_gain"][0]), twice(a["c_q_gain"][0]), twice(a["c_k_gain"][0]), cols(a["conv_w"][0]),
           cols(a["conv_b"][0]), cols(a["conv_w_2"][0]), cols(a["conv_b_2"][0]), cols(a["lru_ba_2"][0]),
           cols(a["lru_bx_2"][0]), cols(a["lru_lambda_2"][0]), cols(a["ln_g_2"][0]), cols(a["ln_b_2"][0]),
           pairs(a["cmp_pe_k_2"][0]), pairs(a["cmp_pe_v_2"][0])]
    squares, masks, cmask, onehots = shape_constants()
    tabs = np.concatenate([np.concatenate([a["rel_bias_table"], a["rel_bias_2"]], 1),
                           np.full((1, 40), NEG, np.float32)], 0)

    def tiles(v):
        return v.T.reshape(-1, P, SEQ).transpose(1, 0, 2)

    return {
        "W": np.concatenate(parts, 0), "xT": tiles(a["x"][0]), "memT": tiles(a["mem_2"][0]),
        "vecs": np.concatenate(vec, 1), "squares": squares, "masks": masks, "cmask": cmask, "onehots": onehots,
        "tabs": tabs, "sinks": a["a_sinks"], "ln_rows": np.concatenate([a["sgu_ln_g_2"], a["sgu_ln_b_2"]], 1),
        "sgu_wT": a["sgu_w_2"][0].transpose(2, 0, 1), "sgu_b": a["sgu_b_2"].reshape(1, -1),
        "lru_w": np.stack([a["lru_wa_2"][0], a["lru_wx_2"][0]], 0).transpose(2, 0, 1, 3),
        "gl_w": w[:, 7680:7728].reshape(NT, P, 48).transpose(1, 0, 2), "gl_b": a["nsa_gate_b_2"],
        "cmp_w1": np.stack([pairs(a["cmp_w1_k_2"][0].reshape(32, HD, 256)),
                            pairs(a["cmp_w1_v_2"][0].reshape(32, HD, 256))], 0),
        "cmp_w2k": a["cmp_w2_k_2"][0].reshape(2, P, HD).transpose(1, 0, 2),
        "cmp_w2v": a["cmp_w2_v_2"][0].reshape(2, P, HD).transpose(1, 0, 2),
    }


def kernel(**inputs):
    from concourse import bacc
    from concourse.bass_utils import run_bass_kernel_spmd

    nc = bacc.Bacc("TRN2", target_bir_lowering=False, num_devices=1)
    arrays = {k: np.ascontiguousarray(v) for k, v in lay_out(inputs).items()}
    args = [nc.dram_tensor(k, v.shape, mybir.dt.from_np(v.dtype), kind="ExternalInput").ap()
            for k, v in arrays.items()]
    out = nc.dram_tensor("out", (P, NT, SEQ), F32, kind="ExternalOutput").ap()
    two_blocks(nc, *args, out)
    r = run_bass_kernel_spmd(nc, [arrays], core_ids=[0])
    y = r.results[0]["out"]
    return np.ascontiguousarray(y.transpose(1, 0, 2).reshape(DM, SEQ).T)[None]
```
